# Optimizing a Trainium2 kernel written in Bass

```python
import jax, jax.numpy as jnp
from jax import lax
import numpy as np

D_MODEL = 1024
BATCH = 1
SEQ = 1024
DEPTH = 1

PLE_DIM = 256
RMS_EPS = 1e-6
MACARON = 0.5
FFN_HIDDEN = 2816
ATT_HEADS = 8
ATT_KV_HEADS = 2
ATT_HEAD_DIM = 64
ATT_WINDOW = 128
ATT_BLOCK = 128
ROPE_THETA = 500000.0
ROPE_DIM = ATT_HEAD_DIM // 4
MLSTM_HEADS = 4
MLSTM_QK_DIM = 128
MLSTM_V_DIM = 256
MLSTM_CHUNK = 64
MLSTM_CONV = 5
ATT_Q_W = ATT_HEADS * ATT_HEAD_DIM
ATT_KV_W = ATT_KV_HEADS * ATT_HEAD_DIM
M_QK_W = MLSTM_HEADS * MLSTM_QK_DIM
M_V_W = MLSTM_HEADS * MLSTM_V_DIM
M_GATE_W = 4 * MLSTM_HEADS
MERGE_W = 2 * D_MODEL
IN_SIZES = (ATT_Q_W, ATT_KV_W, ATT_KV_W, M_QK_W, M_QK_W, M_V_W, M_V_W, M_GATE_W, MERGE_W)
IN_WIDTH = ATT_Q_W + 2 * ATT_KV_W + 2 * M_QK_W + 2 * M_V_W + M_GATE_W + MERGE_W

kernel_name = 'hybrid_swa_mlstm_macaron_encoder'

def rms_norm(x, g):
    xf = x.astype(jnp.float32)
    y = xf * lax.rsqrt(jnp.mean(xf * xf, axis=-1, keepdims=True) + RMS_EPS)
    return (y * g.astype(jnp.float32)).astype(x.dtype)

def swiglu(x, w1, w2):
    z = x @ w1
    return (jax.nn.silu(z[..., :FFN_HIDDEN]) * z[..., FFN_HIDDEN:]) @ w2

def split_cols(z, sizes):
    outs = []
    off = 0
    for s in sizes:
        outs.append(z[..., off:off + s])
        off += s
    return outs

def rope_tables(seq):
    pos = jnp.arange(seq, dtype=jnp.float32)
    inv = ROPE_THETA ** (-jnp.arange(0, ROPE_DIM, 2, dtype=jnp.float32) / ROPE_DIM)
    ang = pos[:, None] * inv[None, :]
    return jnp.cos(ang)[:, None, :], jnp.sin(ang)[:, None, :]

def partial_rope(x, cos, sin):
    half = ROPE_DIM // 2
    xr = x[..., :ROPE_DIM].astype(jnp.float32)
    x1, x2 = xr[..., :half], xr[..., half:]
    rot = jnp.concatenate([x1 * cos - x2 * sin, x2 * cos + x1 * sin], axis=-1)
    return jnp.concatenate([rot.astype(x.dtype), x[..., ROPE_DIM:]], axis=-1)

def windowed_gqa(q, k, v, sink):
    b, s, hq, dh = q.shape
    g = hq // ATT_KV_HEADS
    blk = ATT_BLOCK
    nb = s // blk
    pad = ((0, 0), (blk, blk), (0, 0), (0, 0))
    kb = jnp.pad(k, pad).reshape(b, nb + 2, blk, ATT_KV_HEADS, dh)
    vb = jnp.pad(v, pad).reshape(b, nb + 2, blk, ATT_KV_HEADS, dh)
    kw = jnp.concatenate([kb[:, :-2], kb[:, 1:-1], kb[:, 2:]], axis=2)
    vw = jnp.concatenate([vb[:, :-2], vb[:, 1:-1], vb[:, 2:]], axis=2)
    qb = q.reshape(b, nb, blk, ATT_KV_HEADS, g, dh)
    sc = jnp.einsum('bnqhgd,bnkhd->bnhgqk', qb, kw).astype(jnp.float32) * (dh ** -0.5)
    qi = jnp.arange(blk)[:, None]
    kc = jnp.arange(3 * blk)[None, :]
    rel = kc - blk - qi
    kpos = jnp.arange(nb)[:, None, None] * blk - blk + kc[None]
    mask = (jnp.abs(rel) <= ATT_WINDOW)[None] & (kpos >= 0) & (kpos < s)
    sc = jnp.where(mask[None, :, None, None], sc, -jnp.inf)
    sk = sink.astype(jnp.float32).reshape(1, 1, ATT_KV_HEADS, g, 1, 1)
    mx = jnp.maximum(jnp.max(sc, axis=-1, keepdims=True), sk)
    pr = jnp.exp(sc - mx)
    pr = pr / (jnp.sum(pr, axis=-1, keepdims=True) + jnp.exp(sk - mx))
    o = jnp.einsum('bnhgqk,bnkhd->bnqhgd', pr.astype(v.dtype), vw)
    return o.reshape(b, s, hq * dh)

def centred_depthwise_conv(x, w, bias):
    c = x.shape[-1]
    y = lax.conv_general_dilated(
        x, w[:, None, :].astype(x.dtype), window_strides=(1,),
        padding=((MLSTM_CONV // 2, MLSTM_CONV // 2),),
        dimension_numbers=('NWC', 'WIO', 'NWC'), feature_group_count=c)
    return y + bias

def mlstm_chunkwise(q, k, v, log_i, log_f):
    n, s, h, dk = q.shape
    dv = v.shape[-1]
    L = MLSTM_CHUNK
    nc = s // L

    def to_chunks(t):
        return jnp.moveaxis(t.reshape((n, nc, L, h) + t.shape[3:]), (1, 3), (0, 2))

    xs = (to_chunks(q), to_chunks(k), to_chunks(v), to_chunks(log_i), to_chunks(log_f))
    tril = jnp.tril(jnp.ones((L, L), dtype=bool))

    def step(carry, inp):
        c_mat, n_vec, m_prev = carry
        qc, kc, vc, li, lf = inp
        b = jnp.cumsum(lf, axis=-1)
        d_log = jnp.where(tril, b[..., :, None] - b[..., None, :] + li[..., None, :], -jnp.inf)
        inter = b + m_prev[..., None]
        m_row = jnp.maximum(inter, jnp.max(d_log, axis=-1))
        w_intra = jnp.exp(d_log - m_row[..., None])
        w_inter = jnp.exp(inter - m_row)
        sc = jnp.einsum('nhjd,nhtd->nhjt', qc, kc) * w_intra
        num = jnp.einsum('nhjt,nhtv->nhjv', sc, vc) + w_inter[..., None] * jnp.einsum('nhjd,nhdv->nhjv', qc, c_mat)
        den = jnp.sum(sc, axis=-1) + w_inter * jnp.einsum('nhjd,nhd->nhj', qc, n_vec)
        h_out = num / jnp.maximum(jnp.abs(den), jnp.exp(-m_row))[..., None]
        b_last = b[..., -1]
        k_log = b_last[..., None] - b + li
        m_new = jnp.maximum(b_last + m_prev, jnp.max(k_log, axis=-1))
        w_k = jnp.exp(k_log - m_new[..., None])
        decay = jnp.exp(b_last + m_prev - m_new)
        c_new = decay[..., None, None] * c_mat + jnp.einsum('nht,nhtd,nhtv->nhdv', w_k, kc, vc)
        n_new = decay[..., None] * n_vec + jnp.einsum('nht,nhtd->nhd', w_k, kc)
        return (c_new, n_new, m_new), h_out

    init = (jnp.zeros((n, h, dk, dv), jnp.float32), jnp.zeros((n, h, dk), jnp.float32), jnp.zeros((n, h), jnp.float32))
    _, hs = lax.scan(step, init, xs)
    return jnp.moveaxis(hs, (0, 2), (1, 3)).reshape(n, s, h, dv)

def mlstm_bidirectional(q, k, v, li_fw, lf_fw, li_bw, lf_bw):
    nb = q.shape[0]

    def both(a, c):
        return jnp.concatenate([a, jnp.flip(c, axis=1)], axis=0)

    hs = mlstm_chunkwise(both(q, q), both(k, k), both(v, v), both(li_fw, li_bw), both(lf_fw, lf_bw))
    return hs[:nb] + jnp.flip(hs[nb:], axis=1)

def token_mixer(u, w_in, b_gates, conv_w, conv_b, attn_sink, mlstm_norm, w_branch_attn, w_branch_mlstm, w_out):
    bsz, s, _ = u.shape
    z = u @ w_in
    aq, ak, av, mq, mk, mv, mo, mg, bg = split_cols(z, IN_SIZES)
    cos, sin = rope_tables(s)
    aq = partial_rope(aq.reshape(bsz, s, ATT_HEADS, ATT_HEAD_DIM), cos, sin)
    ak = partial_rope(ak.reshape(bsz, s, ATT_KV_HEADS, ATT_HEAD_DIM), cos, sin)
    av = av.reshape(bsz, s, ATT_KV_HEADS, ATT_HEAD_DIM)
    ya = windowed_gqa(aq, ak, av, attn_sink) @ w_branch_attn
    mqk = jax.nn.silu(centred_depthwise_conv(jnp.concatenate([mq, mk], axis=-1), conv_w, conv_b))
    mq = mqk[..., :M_QK_W].reshape(bsz, s, MLSTM_HEADS, MLSTM_QK_DIM)
    mk = mqk[..., M_QK_W:].reshape(bsz, s, MLSTM_HEADS, MLSTM_QK_DIM) * (MLSTM_QK_DIM ** -0.5)
    mv = mv.reshape(bsz, s, MLSTM_HEADS, MLSTM_V_DIM)
    gates = (mg + b_gates).astype(jnp.float32).reshape(bsz, s, 4, MLSTM_HEADS)
    li_fw = gates[:, :, 0]
    lf_fw = jax.nn.log_sigmoid(gates[:, :, 1])
    li_bw = gates[:, :, 2]
    lf_bw = jax.nn.log_sigmoid(gates[:, :, 3])
    hm = mlstm_bidirectional(mq, mk, mv, li_fw, lf_fw, li_bw, lf_bw)
    hm = hm * lax.rsqrt(jnp.mean(hm * hm, axis=-1, keepdims=True) + RMS_EPS)
    hm = hm * mlstm_norm.astype(jnp.float32).reshape(MLSTM_HEADS, MLSTM_V_DIM)
    hm = (hm.reshape(bsz, s, M_V_W) * jax.nn.sigmoid(mo.astype(jnp.float32))).astype(u.dtype)
    ym = hm @ w_branch_mlstm
    merged = jax.nn.sigmoid(bg[..., :D_MODEL]) * ya + jax.nn.sigmoid(bg[..., D_MODEL:]) * ym
    return merged @ w_out

def setup_inputs(seed: int = 0) -> dict:
    key = jax.random.key(seed)
    ks = jax.random.split(key, 25)
    f32 = jnp.float32

    def w(k, shape, fan_in):
        return jax.random.normal(k, shape, f32) * (fan_in ** -0.5)

    def gain(k, width):
        return 1.0 + 0.05 * jax.random.normal(k, (DEPTH, width), f32)

    f_off = jnp.linspace(3.0, 6.0, MLSTM_HEADS)
    i_off = jnp.zeros((MLSTM_HEADS,), f32)
    gate_off = jnp.stack([i_off, f_off, i_off, f_off])
    b_gates = (0.1 * jax.random.normal(ks[8], (DEPTH, 4, MLSTM_HEADS), f32) + gate_off[None]).reshape(DEPTH, M_GATE_W)
    return {
        'x': jax.random.normal(ks[0], (BATCH, SEQ, D_MODEL), f32),
        'p': jax.random.normal(ks[1], (DEPTH, BATCH, SEQ, PLE_DIM), f32),
        'ffn1_norm_pre': gain(ks[2], D_MODEL),
        'ffn1_w1': w(ks[3], (DEPTH, D_MODEL, 2 * FFN_HIDDEN), D_MODEL),
        'ffn1_w2': w(ks[4], (DEPTH, FFN_HIDDEN, D_MODEL), FFN_HIDDEN),
        'ffn1_norm_post': gain(ks[5], D_MODEL),
        'mix_norm_pre': gain(ks[6], D_MODEL),
        'w_in': w(ks[7], (DEPTH, D_MODEL, IN_WIDTH), D_MODEL),
        'b_gates': b_gates,
        'conv_w': w(ks[9], (DEPTH, MLSTM_CONV, 2 * M_QK_W), MLSTM_CONV),
        'conv_b': 0.02 * jax.random.normal(ks[10], (DEPTH, 2 * M_QK_W), f32),
        'attn_sink': 0.5 * jax.random.normal(ks[11], (DEPTH, ATT_HEADS), f32),
        'mlstm_norm': gain(ks[12], M_V_W),
        'w_branch_attn': w(ks[13], (DEPTH, ATT_Q_W, D_MODEL), ATT_Q_W),
        'w_branch_mlstm': w(ks[14], (DEPTH, M_V_W, D_MODEL), M_V_W),
        'w_out': w(ks[15], (DEPTH, D_MODEL, D_MODEL), D_MODEL),
        'mix_norm_post': gain(ks[16], D_MODEL),
        'ffn2_norm_pre': gain(ks[17], D_MODEL),
        'ffn2_w1': w(ks[18], (DEPTH, D_MODEL, 2 * FFN_HIDDEN), D_MODEL),
        'ffn2_w2': w(ks[19], (DEPTH, FFN_HIDDEN, D_MODEL), FFN_HIDDEN),
        'ffn2_norm_post': gain(ks[20], D_MODEL),
        'ple_norm_pre': gain(ks[21], D_MODEL),
        'w_ple_gate': w(ks[22], (DEPTH, D_MODEL, D_MODEL), D_MODEL),
        'w_ple_proj': w(ks[23], (DEPTH, PLE_DIM, D_MODEL), PLE_DIM),
        'ple_norm_post': gain(ks[24], D_MODEL),
    }

def reference(x, p, ffn1_norm_pre, ffn1_w1, ffn1_w2, ffn1_norm_post, mix_norm_pre, w_in, b_gates, conv_w, conv_b,
              attn_sink, mlstm_norm, w_branch_attn, w_branch_mlstm, w_out, mix_norm_post, ffn2_norm_pre, ffn2_w1,
              ffn2_w2, ffn2_norm_post, ple_norm_pre, w_ple_gate, w_ple_proj, ple_norm_post):
    h = x
    for i in range(DEPTH):
        h = h + MACARON * rms_norm(swiglu(rms_norm(h, ffn1_norm_pre[i]), ffn1_w1[i], ffn1_w2[i]), ffn1_norm_post[i])
        mix = token_mixer(rms_norm(h, mix_norm_pre[i]), w_in[i], b_gates[i], conv_w[i], conv_b[i], attn_sink[i],
                          mlstm_norm[i], w_branch_attn[i], w_branch_mlstm[i], w_out[i])
        h = h + rms_norm(mix, mix_norm_post[i])
        h = h + MACARON * rms_norm(swiglu(rms_norm(h, ffn2_norm_pre[i]), ffn2_w1[i], ffn2_w2[i]), ffn2_norm_post[i])
        gate = jax.nn.sigmoid(rms_norm(h, ple_norm_pre[i]) @ w_ple_gate[i])
        h = h + rms_norm((p[i] @ w_ple_proj[i]) * gate, ple_norm_post[i])
    return h


_drawn_inputs = setup_inputs


def setup_inputs(seed=0):
    import zlib

    import numpy as np

    out = dict(_drawn_inputs(seed))
    spreads = {}
    factors = {'conv_b': 5.88,
     'attn_sink': 8.0,
     'ffn2_norm_pre': 2.912,
     'ffn2_norm_post': 4.3,
     'ple_norm_pre': 18.157,
     'ple_norm_post': 3.173}
    for name, (base, spread) in spreads.items():
        noise = np.random.default_rng([zlib.crc32(name.encode()), seed]).standard_normal(out[name].shape)
        drawn = base * np.exp(spread * noise) if base else spread * noise
        out[name] = __import__('jax').numpy.asarray(drawn.astype(out[name].dtype))
    for name, factor in factors.items():
        out[name] = (out[name] * factor).astype(out[name].dtype)
    return out
```

```python
from contextlib import ExitStack

import concourse.bass as bass
from concourse import mybir
from concourse.alu_op_type import AluOpType as ALU

F32 = mybir.dt.float32
F32R = mybir.dt.float32r
ACT = mybir.ActivationFunctionType

P = 128
D = 1024
S = 1024
KD = D // P
HALF = 512
FFN = 2816
GROUP = 2
GROUPS = FFN // (GROUP * P)
EPS = 1e-6
NB = S // P

AH, AKV, AD = 8, 2, 64
ATT_SCALE = AD ** -0.5
WINDOW = 3 * P
ROPE = AD // 4
THETA = 500000.0
BLOCKED = 1e30

MH, MD, MV = 4, 128, 256
TAPS = 5
PLE = 256
CHAIN_ROWS = 64
K_SCALE = MD ** -0.5

C_AQ = 0
C_AK = C_AQ + AH * AD
C_AV = C_AK + AKV * AD
C_MQK = C_AV + AKV * AD
C_MV = C_MQK + 2 * MH * MD
C_MO = C_MV + MH * MV
C_MG = C_MO + MH * MV
C_BG = C_MG + 4 * MH

TABLE = {}
for _name, _width in (("ident", P), ("perm", P), ("window", WINDOW), ("later", P), ("earlier", P),
                      ("chains", 2 * MH * P), ("cos", S), ("sin", S), ("inside", S)):
    TABLE[_name] = (sum(w for _, w in TABLE.values()), _width)
TABLE_WIDTH = sum(w for _, w in TABLE.values())

N_QKV = 6
T_MQK = N_QKV
T_MV = T_MQK + KD
T_SIG = T_MV + KD
T_MG = T_SIG + 2 * KD
T_GM = T_MG + 1
N_TILES = T_GM + KD
KB = 1024
RING = 2
VEC_ROWS = 120
NORMS = ['ffn1_norm_pre', 'ffn1_norm_post', 'mix_norm_pre', 'mix_norm_post', 'ffn2_norm_pre', 'ffn2_norm_post',
         'ple_norm_pre', 'ple_norm_post']


class Count:

    def __init__(self, base, per=0, turn=None):
        self.base, self.per, self.turn = base, per, turn

    def n(self, k=0):
        return self.base + k if self.turn is None else self.turn * self.per + (self.base + k)

    def slot(self, k=0):
        return (self.base + k) % RING

    def uses(self, k=0):
        first = (self.base + k) // RING + 1
        return first if self.turn is None else self.turn * (self.per // RING) + first


def build(nc, t, out):
    with ExitStack() as ctx:
        base = (nc.sbuf_base + 63) // 64 * 64

        def at(name, kb, shape, dt=F32):
            return nc.alloc_sbuf_tensor_at(name, shape, dt, offset=base + int(kb * KB))

        def sem(name):
            return ctx.enter_context(nc.semaphore(name))

        resid = at("resid", 0, [P, KD, S])
        u_hi = at("u_hi", 32, [P, KD, S], F32R)
        u_lo = at("u_lo", 64, [P, KD, S], F32R)
        w_raw = at("w_raw", 96, [P, RING, 1024])
        w_hi = at("w_hi", 104, [P, RING, 1024], F32R)
        w_lo = at("w_lo", 112, [P, RING, 1024], F32R)
        tmp = at("tmp", 120, [P, 2, S])
        diag = at("diag", 128.25, [P, KD, P])
        ident = at("ident", 132.25, [P, P])
        ones = at("ones", 132.75, [P, P])
        vec_rows = at("vec_rows", 133.75, [VEC_ROWS, P])
        vecs = at("vecs", 134.25, [P, VEC_ROWS])
        gains = vecs[:, 0:8 * KD].rearrange("p (n k) -> p n k", n=8)
        stat = at("stat", 133.25, [P, 3, KD])
        yacc = at("yacc", 142, [P, KD, S])
        hid_hi = at("hid_hi", 174, [P, 2, GROUP, S], F32R)
        hid_lo = at("hid_lo", 190, [P, 2, GROUP, S], F32R)
        sq = at("sq", 174, [P, KD, S])
        x_in = at("x_in", 142, [P, KD, D])
        x_out = at("x_out", 174, [P, KD, D])

        ps = [ctx.enter_context(nc.psum_tensor(f"acc{n}", [P, S], F32)) for n in range(4)]

        x_loaded = sem("x_loaded")
        consts_ready = sem("consts_ready")
        ident_zero = sem("ident_zero")
        vecs_loaded = sem("vecs_loaded")
        vecs_turned = sem("vecs_turned")
        vecs_ready = sem("vecs_ready")
        gains_halved = sem("gains_halved")
        x_turned = sem("x_turned")
        x_kept = sem("x_kept")
        raw_loaded = [sem(f"raw_loaded{n}") for n in range(RING)]
        whi_ready = sem("whi_ready")
        wlo_ready = sem("wlo_ready")
        block_used = sem("block_used")
        gateup_done = sem("gateup_done")
        silu_done = sem("silu_done")
        prod_done = sem("prod_done")
        hhi_ready = sem("hhi_ready")
        hid_ready = sem("hid_ready")
        y_done = sem("y_done")
        y_added = sem("y_added")
        sq_act = sem("sq_act")
        sq_dve = sem("sq_dve")
        stat_done = sem("stat_done")
        mean_ready = sem("mean_ready")
        root_ready = sem("root_ready")
        rinv_ready = sem("rinv_ready")
        diag_ready = sem("diag_ready")
        bc_done = sem("bc_done")
        u_made = sem("u_made")
        uhi_ready = sem("uhi_ready")
        ulo_ready = sem("ulo_ready")
        post_made = sem("post_made")
        resid_ready = sem("resid_ready")
        out_turned = sem("out_turned")
        out_copied = sem("out_copied")
        stored = sem("stored")

        STAT = ps[3][:, 0:KD]
        BC = ps[2]

        def w1_block(name, cols):
            return t[name][0, :, cols].rearrange("(k p) n -> p k n", p=P)

        def w2_block(name, rows, half):
            return t[name][0, rows, half * 512:half * 512 + 512].rearrange("(k p) n -> p k n", p=P)

        def load(sp, c, k, src):
            if c.base + k >= RING:
                sp.wait_ge(wlo_ready, c.n(k - RING + 1))
            s = c.slot(k)
            nk = src.shape[1]
            sp.dma_start(w_raw[:, s, :].rearrange("p (k n) -> p k n", k=nk), src).then_inc(raw_loaded[s], 16)

        def split_hi(act, c, k):
            act.wait_ge(raw_loaded[c.slot(k)], c.uses(k) * 16)
            if c.base + k >= RING:
                act.wait_ge(block_used, c.n(k - RING + 1))
            nc.scalar.activation(w_hi[:, c.slot(k), :], w_raw[:, c.slot(k), :], ACT.Copy).then_inc(whi_ready, 1)

        def split_lo(dve, c, k):
            s = c.slot(k)
            dve.wait_ge(whi_ready, c.n(k + 1))
            nc.vector.tensor_tensor(w_lo[:, s, :], w_raw[:, s, :], w_hi[:, s, :].bitcast(F32),
                                    ALU.subtract).then_inc(wlo_ready, 1)

        def product(acc, terms, first=True, last=True, new_block=False):
            for n, (s, off, a_hi, a_lo) in enumerate(terms):
                hi, lo = w_hi[:, s, off:off + P], w_lo[:, s, off:off + P]
                for h in range(2):
                    cols = slice(h * HALF, (h + 1) * HALF)
                    mm = nc.tensor.matmul(acc[:, cols], hi, a_hi[:, cols], start=(first and n == 0), stop=False)
                    if new_block and n == 0 and h == 0:
                        mm.then_inc(block_used, 1)
                    nc.tensor.matmul(acc[:, cols], hi, a_lo[:, cols], start=False, stop=False)
                    mm = nc.tensor.matmul(acc[:, cols], lo, a_hi[:, cols], start=False,
                                          stop=(last and n == len(terms) - 1))
            return mm

        def norm_act(act, n, src):
            for k in range(0, KD, 2):
                norm_src_wait(act, n, k)
                nc.scalar.activation(sq[:, k, :], src[:, k, :], ACT.Square).then_inc(sq_act, 1)
            act.wait_ge(mean_ready, n + 1)
            nc.scalar.activation(stat[:, 1, :], stat[:, 0, :], ACT.Sqrt).then_inc(root_ready, 1)

        def norm_src_wait(eng, n, k):
            if n == 0:
                eng.wait_ge(x_kept, k + 1)
            elif n % 2 == 0:
                eng.wait_ge(resid_ready, KD * (n // 2 - 1) + k + 1)
            elif n == 3:
                eng.wait_ge(mix_left, N_TILES + k + 1)
            elif n == 7:
                eng.wait_ge(prod_done, 2 * GROUPS * GROUP + (k + 1 if k < 2 else KD))
            elif k < 2:
                eng.wait_ge(y_added, KD * (GROUPS + 1) * {1: 1, 5: 2}[n])

        def norm_dve(dve, n, src):
            for k in range(1, KD, 2):
                norm_src_wait(dve, n, k)
                nc.vector.tensor_tensor(sq[:, k, :], src[:, k, :], src[:, k, :], ALU.mult).then_inc(sq_dve, 1)
            dve.wait_ge(stat_done, n + 1)
            nc.vector.tensor_scalar(stat[:, 0, :], STAT, 1.0 / D, EPS, ALU.mult, ALU.add).then_inc(mean_ready, 1)
            dve.wait_ge(root_ready, n + 1)
            nc.vector.reciprocal(stat[:, 2, :], stat[:, 1, :]).then_inc(rinv_ready, 1)
            dve.wait_ge(rinv_ready, n + 1)
            nc.vector.tensor_tensor(diag[:, :, :], ident[:, :].unsqueeze(1).to_broadcast([P, KD, P]),
                                    stat[:, 2, :].unsqueeze(2).to_broadcast([P, KD, P]),
                                    ALU.mult).then_inc(diag_ready, 1)

        def norm_pe(pe, n, new_block=False):
            for k in range(KD):
                if k % 2 == 0:
                    pe.wait_ge(sq_act, 4 * n + k // 2 + 1)
                else:
                    pe.wait_ge(sq_dve, 4 * n + k // 2 + 1)
                for j in range(KD):
                    mm = nc.tensor.matmul(ps[3][:, j:j + 1], sq[:, k, j * P:(j + 1) * P], ones[:, 0:1],
                                          start=(k == 0 and j == 0), stop=(k == KD - 1), skip_group_check=True)
                    if new_block and k == 0 and j == 0:
                        mm.then_inc(block_used, 1)
            mm.then_inc(stat_done, 1)
            pe.wait_ge(diag_ready, n + 1)
            for h in range(2):
                mm = nc.tensor.matmul(BC[:, h * HALF:(h + 1) * HALF], ones[:, :],
                                      diag[:, 4 * h:4 * h + 4, :].rearrange("p j n -> p (j n)"),
                                      start=True, stop=True)
            mm.then_inc(bc_done, 1)

        def pre_dve(dve, n):
            pre = n // 2
            dve.wait_ge(bc_done, n + 1)
            for k in range(KD):
                if KD * pre + k >= 2:
                    dve.wait_ge(ulo_ready, KD * pre + k - 1)
                nc.vector.scalar_tensor_tensor(out=tmp[:, k % 2, :], in0=resid[:, k, :], scalar=gains[:, n, k:k + 1],
                                               in1=BC[:, :], op0=ALU.mult, op1=ALU.mult).then_inc(u_made, 1)
                if k:
                    pre_lo(dve, pre, k - 1)
            pre_lo(dve, pre, KD - 1)

        def pre_lo(dve, pre, k):
            dve.wait_ge(uhi_ready, KD * pre + k + 1)
            nc.vector.tensor_tensor(u_lo[:, k, :], tmp[:, k % 2, :], u_hi[:, k, :].bitcast(F32),
                                    ALU.subtract).then_inc(ulo_ready, 1)

        def pre_act(act, n):
            pre = n // 2
            for k in range(KD):
                act.wait_ge(u_made, KD * pre + k + 1)
                nc.scalar.activation(u_hi[:, k, :], tmp[:, k % 2, :], ACT.Copy).then_inc(uhi_ready, 1)

        def post_dve(dve, n, y):
            post = n // 2
            dve.wait_ge(bc_done, n + 1)
            for k in range(KD):
                nc.vector.scalar_tensor_tensor(out=y[:, k, :], in0=y[:, k, :], scalar=gains[:, n, k:k + 1],
                                               in1=BC[:, :], op0=ALU.mult, op1=ALU.mult).then_inc(post_made, 1)
                if k:
                    dve.wait_ge(post_made, KD * post + k)
                    nc.vector.tensor_tensor(resid[:, k - 1, :], resid[:, k - 1, :], y[:, k - 1, :],
                                            ALU.add).then_inc(resid_ready, 1)
            dve.wait_ge(post_made, KD * post + KD)
            nc.vector.tensor_tensor(resid[:, KD - 1, :], resid[:, KD - 1, :], y[:, KD - 1, :],
                                    ALU.add).then_inc(resid_ready, 1)

        BLOCKS_FFN = GROUPS * 6

        def ffn_sp(sp, f, b, w1, w2):
            def s1(c, k, col):
                for j in range(GROUP):
                    load(sp, c, k + 2 * j, w1_block(w1, bass.ds(col + j * P, P)))
                    load(sp, c, k + 2 * j + 1, w1_block(w1, bass.ds(col + FFN + j * P, P)))

            def s2(c, k, row):
                for h in range(2):
                    load(sp, c, k + h, w2_block(w2, bass.ds(row, GROUP * P), h))

            W = GROUP * P
            s1(Count(b), 0, 0)
            with sp.Fori(0, GROUPS // 2) as i:
                c = Count(b + 4, 12, i)
                s1(c, 0, i * (2 * W) + W)
                s2(c, 4, i * (2 * W))
                s1(c, 6, i * (2 * W) + 2 * W)
                s2(c, 10, i * (2 * W) + W)
            s2(Count(b + BLOCKS_FFN - 2), 0, (GROUPS - 1) * W)

        def ffn_act(act, f, b):
            def s1(c, g, k, more=True):
                split_hi(act, c, k + 1)
                split_hi(act, c, k + 2)
                for j in range(GROUP):
                    act.wait_ge(gateup_done, g.n() * 4 + 2 * j + 1)
                    if g.base * GROUP + j >= 2:
                        act.wait_ge(hid_ready, g.n() * GROUP + j - 1)
                    nc.scalar.activation(tmp[:, j, :], ps[2 * j][:, :], ACT.Silu).then_inc(silu_done, 1)
                    split_hi(act, c, k + 3 + j)

            def s2(c, k, more=True):
                split_hi(act, c, k + 1)
                if more:
                    split_hi(act, c, k + 2)

            split_hi(act, Count(b), 0)
            s1(Count(b), Count(f * GROUPS), 0)
            with act.Fori(0, GROUPS // 2) as i:
                c = Count(b + 4, 12, i)
                s1(c, Count(f * GROUPS + 1, 2, i), 0)
                s2(c, 4)
                s1(c, Count(f * GROUPS + 2, 2, i), 6)
                s2(c, 10)
            s2(Count(b + BLOCKS_FFN - 2), 0, more=False)

        def ffn_dve(dve, f, b):
            def hidden(g, j):
                dve.wait_ge(silu_done, g.n() * 2 + j + 1)
                dve.wait_ge(gateup_done, g.n() * 4 + 2 * j + 2)
                par = (g.base - f * GROUPS) % 2
                nc.vector.tensor_tensor(tmp[:, j, :], tmp[:, j, :], ps[2 * j + 1][:, :],
                                        ALU.mult).then_inc(prod_done, 1)
                dve.wait_ge(prod_done, g.n() * 2 + j + 1)
                nc.vector.tensor_copy(hid_hi[:, par, j, :], tmp[:, j, :]).then_inc(hhi_ready, 1)
                dve.wait_ge(hhi_ready, g.n() * 2 + j + 1)
                nc.vector.tensor_tensor(hid_lo[:, par, j, :], tmp[:, j, :], hid_hi[:, par, j, :].bitcast(F32),
                                        ALU.subtract).then_inc(hid_ready, 1)

            def add_y(g, m):
                dve.wait_ge(y_done, g.n() * KD + m + 1)
                dve.wait_ge(y_added, g.n() * KD + KD * f + m + 1)
                nc.vector.tensor_tensor(yacc[:, m, :], yacc[:, m, :], ps[m % 4][:, :], ALU.add).then_inc(y_added, 1)

            def s1(c, g, k, y=None):
                split_lo(dve, c, k + 1)
                if y is not None:
                    add_y(y, KD - 1)
                split_lo(dve, c, k + 2)
                split_lo(dve, c, k + 3)
                hidden(g, 0)
                split_lo(dve, c, k + 4)

            def s2(c, g, y, k, more=True):
                split_lo(dve, c, k + 1)
                if g is not None:
                    hidden(g, 1)
                for m in range(3):
                    add_y(y, m)
                if more:
                    split_lo(dve, c, k + 2)
                for m in range(3, KD - 1):
                    add_y(y, m)

            G = f * GROUPS
            split_lo(dve, Count(b), 0)
            s1(Count(b), Count(G), 0)
            hidden(Count(G), 1)
            with dve.Fori(0, GROUPS // 2) as i:
                c = Count(b + 4, 12, i)
                s1(c, Count(G + 1, 2, i), 0)
                s2(c, Count(G + 1, 2, i), Count(G, 2, i), 4)
                s1(c, Count(G + 2, 2, i), 6, y=Count(G, 2, i))
                s2(c, Count(G + 2, 2, i), Count(G + 1, 2, i), 10)
                add_y(Count(G + 1, 2, i), KD - 1)
            s2(Count(b + BLOCKS_FFN - 2), None, Count(G + GROUPS - 1), 0, more=False)
            add_y(Count(G + GROUPS - 1), KD - 1)

        def ffn_pe(pe, f, b, pre):
            def s1(c, g, k, first=False):
                for n in range(4):
                    pe.wait_ge(wlo_ready, c.n(k + n + 1))
                    if not first:
                        pe.wait_ge(y_added, (g.n() - 1) * KD + KD * f + 4 + n + 1)
                    if first and n == 0:
                        for kk in range(KD):
                            pe.wait_ge(ulo_ready, KD * pre + kk + 1)
                            terms = [(c.slot(k), kk * P, u_hi[:, kk, :], u_lo[:, kk, :])]
                            mm = product(ps[0], terms, first=(kk == 0), last=(kk == KD - 1),
                                         new_block=False)
                    else:
                        mm = product(ps[n], [(c.slot(k + n), kk * P, u_hi[:, kk, :], u_lo[:, kk, :])
                                             for kk in range(KD)], new_block=True)
                    mm.then_inc(gateup_done, 1)

            def s2(c, g, k, last_s1):
                par = (g.base - f * GROUPS) % 2
                pe.wait_ge(hid_ready, g.n() * GROUP + GROUP)
                for m in range(KD):
                    h = m // 4
                    if m % 4 == 0:
                        pe.wait_ge(wlo_ready, c.n(k + h + 1))
                    if m < 4:
                        if last_s1 is not None:
                            if m % 2 == 0:
                                pe.wait_ge(silu_done, last_s1.n() * GROUP + m // 2 + 1)
                            else:
                                pe.wait_ge(prod_done, last_s1.n() * GROUP + m // 2 + 1)
                        else:
                            pe.wait_ge(y_added, g.n() * KD + KD * f + 4 + m + 1)
                    else:
                        pe.wait_ge(y_added, g.n() * KD + KD * (f + 1) + m - 4 + 1)
                    mm = product(ps[m % 4], [(c.slot(k + h), j * 512 + (m % 4) * P, hid_hi[:, par, j, :],
                                              hid_lo[:, par, j, :]) for j in range(GROUP)],
                                 new_block=(m % 4 == 0))
                    mm.then_inc(y_done, 1)

            G = f * GROUPS
            s1(Count(b), Count(G), 0, first=True)
            with pe.Fori(0, GROUPS // 2) as i:
                c = Count(b + 4, 12, i)
                s1(c, Count(G + 1, 2, i), 0)
                s2(c, Count(G, 2, i), 4, Count(G + 1, 2, i))
                s1(c, Count(G + 2, 2, i), 6)
                s2(c, Count(G + 1, 2, i), 10, Count(G + 2, 2, i))
            s2(Count(b + BLOCKS_FFN - 2), Count(G + GROUPS - 1), 0, None)

        mqk = at("mqk", 0, [P, 2 * MH, S])
        zpad = at("zpad", 120, [P, 2, S + TAPS - 1])
        rope_t = at("rope_t", 128.25, [P, S])
        att_q = at("att_q", 142, [P, AH // 2, S])
        att_k = at("att_k", 158, [P, S])
        att_v = at("att_v", 162, [P, NB, P])
        cos_sb = at("cos_sb", 166, [P, S])
        sin_sb = at("sin_sb", 170, [P, S])
        m_v = at("m_v", 166, [P, NB, MH, MV + 1])
        q_st = at("q_st", 136, [P, 2, AH // 2, P])
        window = at("window", 140, [P, WINDOW])
        perm = at("perm", 141.5, [P, P])
        prob = at("prob", 199, [P, 2, WINDOW])
        prob_t = at("prob_t", 202, [P, 2, WINDOW])
        o_sb = at("o_sb", 205, [P, AH * AD])
        sinks = at("sinks", 134.75, [P, AH])
        att = at("att", 134.8125, [P, 8, AH])
        A_MAX, A_NEG, A_SUM, A_SINK, A_ESINK, A_DEN, A_REC, neg_sinks = (att[:, n, :] for n in range(8))
        tick = at("tick", 135.8125, [P, 1])
        gate_bias = at("gate_bias", 135.0625, [CHAIN_ROWS, 2])
        m_cols = at("m_cols", 135.125, [P, 3, NB * MH])
        chunk_rows = at("chunk_rows", 135.5, [CHAIN_ROWS, 2, NB])

        r_li = at("r_li", 199, [CHAIN_ROWS, S])
        r_lf = at("r_lf", 162, [CHAIN_ROWS, S])
        r_b = at("r_b", 158, [CHAIN_ROWS, S])
        r_m = at("r_m", 203, [CHAIN_ROWS, S])
        r_in = at("r_in", 136, [CHAIN_ROWS, S])
        r_g, r_wi, r_r, r_em, r_wk = r_li, r_lf, r_b, r_m, r_in

        col = at("col", 32, [P, NB, 3, CHAIN_ROWS])
        h_col = at("h_col", 38, [P, 2, NB, 3])
        h_sel = at("h_sel", 38.5, [CHAIN_ROWS, 2, P])
        state = at("state", 39.5, [P, 2, 2, MV + 1])
        h_k = at("h_k", 43.75, [P, NB, P])
        h_s = at("h_s", 47.75, [P, 2, NB, P])
        h_q = at("h_q", 55.75, [P, 2, NB, P])
        h_arg = at("h_arg", 128.25, [P, NB, P])
        h_kw = at("h_kw", 120, [P, 2, NB, P])
        h_dec = at("h_dec", 38.25, [P, 2, NB])
        h_den = at("h_den", 38.3125, [P, 2, 2])
        hm = at("hm", 64, [P, NB, MH, MV])
        chains = at("chains", 199, [CHAIN_ROWS, 2, MH, P])
        order = at("order", 203, [P, 2, P])

        h_junk = [at(f"h_junk{n}", 136 + n if n < 6 else 198 + n, [P, MV]) for n in range(NB)]
        h_tick = at("h_tick", 135.84375, [P, 1])

        hm_hi = at("hm_hi", 0, [P, KD, S], F32R)
        hm_lo = at("hm_lo", 32, [P, KD, S], F32R)
        o_hi = at("o_hi", 167, [P, AH // 2, S], F32R)
        o_lo = at("o_lo", 183, [P, AH // 2, S], F32R)
        mg_hi = at("mg_hi", 64, [P, KD, S], F32R)
        mg_lo = at("mg_lo", 135, [P, KD, S], F32R)
        p_in = at("p_in", 174, [P, NB, PLE])
        p_hi = at("p_hi", 182, [P, PLE // P, S], F32R)
        p_lo = at("p_lo", 190, [P, PLE // P, S], F32R)
        sig_in = at("sig_in", 199, [P, 2, S])
        mix_y = at("mix_y", 32, [P, KD, S])

        sig_dram = nc.dram_tensor("sig_dram", (3 * KD, P, S), F32, kind="Internal").ap()
        resid_dram = nc.dram_tensor("resid_dram", (KD, P, S), F32, kind="Internal").ap()

        (spilled, tables_loaded, rot_done, rope_cos, rope_sin, rope_done, vt_done, vt_left, mix_done, mix_left,
         pad_zero, conv_step, conv_done, mqk_ready, ones_v, small_loaded) = (sem(x) for x in (
            "spilled", "tables_loaded", "rot_done", "rope_cos", "rope_sin", "rope_done", "vt_done", "vt_left",
            "mix_done", "mix_left", "pad_zero", "conv_step", "conv_done", "mqk_ready", "ones_v",
            "small_loaded"))
        (qst_ready, score_done, max_done, neg_ready, prob_ready, pt_done, pt_left, pv_done, sink_arg, sink_exp,
         den_ready, rec_ready, osb_ready, ot_done, ot_left, qst_zero, sinks_ready) = (sem(x) for x in (
            "qst_ready", "score_done", "max_done", "neg_ready", "prob_ready", "pt_done", "pt_left", "pv_done",
            "sink_arg", "sink_exp", "den_ready", "rec_ready", "osb_ready", "ot_done", "ot_left", "qst_zero", "sinks_ready"))
        raw_q = [sem(f"raw_q{n}") for n in range(RING)]
        sig_stored = [sem(f"sig_stored{n}") for n in range(2)]
        row_act, row_dve, wz = (sem(x) for x in ("row_act", "row_dve", "wz"))

        W_IN = t["w_in"][0]

        def copy(dst, src, scale=1.0):
            return nc.vector.tensor_scalar(dst, src, scale, None, ALU.mult)

        def in_block(first):
            return W_IN[:, bass.ds(first, P)].rearrange("(k p) n -> p k n", p=P)

        def table(name, rows=P):
            first, width = TABLE[name]
            return t["tables"][0:rows, first:first + width]

        def sig_tile(n):
            return sig_dram[bass.ds(n, 1)].rearrange("a p n -> (a p) n")

        def mix_sp(sp, b):
            c = Count(b)
            wq = W_IN[:, C_AQ:C_AQ + AH * AD].rearrange("(k p) (g i d) -> i p k g d", p=P, g=2, d=AD)

            for k in range(AH // 2):
                load_q2(sp, c, k, wq)
                if k == 1:
                    for m in range(KD):
                        sp.wait_ge(resid_ready, m + 1)
                        sp.dma_start(resid_dram[m], resid[:, m, :]).then_inc(spilled, 16)
                    sp.dma_start(cos_sb[:, :], table("cos")).then_inc(tables_loaded, 16)
                    sp.dma_start(sin_sb[:, :], table("sin")).then_inc(tables_loaded, 16)
                    sp.dma_start(perm[:, :], table("perm")).then_inc(tables_loaded, 16)
                    sp.dma_start(window[:, :], table("window")).then_inc(tables_loaded, 16)
            load(sp, c, 4, in_block(C_AK))
            load(sp, c, 5, in_block(C_AV))
            with sp.Fori(0, KD // 2) as i:
                c = Count(b + T_MQK, 2, i)
                for k in range(2):
                    load(sp, c, k, in_block(i * (2 * P) + (C_MQK + k * P)))
            with sp.Fori(0, KD // 2) as i:
                c = Count(b + T_MV, 2, i)
                for k in range(2):
                    load(sp, c, k, in_block(i * (2 * P) + (C_MV + k * P)))

            def store_sig(c, k, tile):
                sp.wait_ge(mix_left, c.n(k + 1))
                s = c.slot(k)
                sp.dma_start(sig_tile(tile), tmp[:, s, :]).then_inc(sig_stored[s], 16)

            c = Count(b + T_SIG)
            load(sp, c, 0, in_block(C_MO))
            load(sp, c, 1, in_block(C_BG))
            ct = Count(T_SIG)
            with sp.Fori(0, KD - 1) as i:
                c, ct = Count(b + T_SIG + 2, 2, i), Count(T_SIG, 2, i)
                load(sp, c, 0, in_block(i * P + (C_MO + P)))
                store_sig(ct, 0, i)
                load(sp, c, 1, in_block(i * P + (C_BG + P)))
                store_sig(ct, 1, i + KD)
            c, ct = Count(b + T_MG), Count(T_SIG + 2 * KD - 2)
            load_gates(sp, c)
            store_sig(ct, 0, KD - 1)
            load(sp, Count(b + T_GM), 0, in_block(C_BG + D))
            store_sig(ct, 1, 2 * KD - 1)
            sp.wait_ge(score_done, AH * NB)
            sp.dma_start(r_in[:, :], table("inside", CHAIN_ROWS)).then_inc(tables_loaded, 16)
            load(sp, Count(b + T_GM), 1, in_block(C_BG + D + P))
            for k in range(KD):
                if k + 2 < KD:
                    load(sp, Count(b + T_GM), k + 2, in_block(C_BG + D + (k + 2) * P))
                store_sig(Count(T_GM), k, 2 * KD + k)

        def load_q2(sp, c, k, wq):
            if c.base + k >= RING:
                sp.wait_ge(wlo_ready, c.n(k - RING + 1))
            s = c.slot(k)
            both = w_raw[:, s, :].rearrange("p (k g d) -> p k g d", k=KD, g=2)
            sp.dma_start(both[:, :, 0, :], wq[k][:, :, 0, :]).then_inc(raw_q[s], 16)
            sp.dma_start(both[:, :, 1, :], wq[k][:, :, 1, :]).then_inc(raw_loaded[s], 16)

        def load_gates(sp, c):
            sp.wait_ge(wlo_ready, c.n(-RING + 1))
            s = c.slot(0)
            sp.dma_start(w_raw[:, s, 0:KD * 4 * MH].rearrange("p (k n) -> p k n", k=KD),
                         W_IN[:, C_MG:C_MG + 4 * MH].rearrange("(k p) n -> p k n", p=P)).then_inc(raw_loaded[s], 16)

        def mix_product(pe, ct, cb, k, pieces=range(KD), u_wait=None):
            acc = ps[ct.slot(k)]
            if pieces[0] == 0:
                pe.wait_ge(wlo_ready, cb.n(k + 1))
                if ct.base + k >= 2:
                    pe.wait_ge(mix_left, ct.n(k - 1))
            for kk in pieces:
                if u_wait is not None:
                    pe.wait_ge(ulo_ready, KD * u_wait + kk + 1)
                mm = product(acc, [(cb.slot(k), kk * P, u_hi[:, kk, :], u_lo[:, kk, :])], first=(kk == 0),
                             last=(kk == KD - 1), new_block=(kk == 0 and u_wait is None))
            if pieces[-1] == KD - 1:
                mm.then_inc(mix_done, 1)

        def rotate(pe, k):
            pe.wait_ge(mix_left, k + 1)
            if k:
                pe.wait_ge(rope_sin, k)
            else:
                pe.wait_ge(tables_loaded, 64)
            for h in range(2):
                cols = slice(h * HALF, (h + 1) * HALF)
                mm = nc.tensor.matmul(ps[2][:, cols], perm[:, :], tmp[:, k % 2, cols], start=True, stop=True)
            mm.then_inc(rot_done, 1)

        def turn_values(pe, ct, cv, k):
            pe.wait_ge(mix_left, ct.n(k + 1))
            if cv.base + k >= 1:
                pe.wait_ge(vt_left, cv.n(k))
            for n in range(NB):
                mm = nc.tensor.transpose(ps[3][:, n * P:(n + 1) * P], tmp[:, ct.slot(k), n * P:(n + 1) * P],
                                         ident[:, :])
            mm.then_inc(vt_done, 1)

        def heads():
            return [(j, j // 2, j % 2, j // 2 + AH // 2 * (j % 2)) for j in range(AH)]

        def att_window(n, edge):
            if edge == 0:
                return 0, 2, P
            if edge == 2:
                return (NB - 2) * P, 2, 0
            return n * P - P, 3, 0

        def score_bank(j):
            return ps[2][:, (j % 2) * HALF:(j % 2) * HALF + WINDOW]

        PT = ps[3][:, 0:WINDOW]
        OT = ps[3][:, 0:HALF]
        OA = ps[3][:, HALF:2 * HALF]

        def att_pe(pe, n, edge, cu, ct, cb):
            key0, blocks, _ = att_window(n, edge)
            width = blocks * P

            def score(j, i, g, head):
                if j == 0:
                    pe.wait_ge(qst_ready, n + 1)
                if cu.base + j >= 2:
                    pe.wait_ge(max_done, cu.n(j - 1))
                nc.tensor.matmul(score_bank(j)[:, 0:width], q_st[:, g, i, :], att_k[:, bass.ds(key0, width)],
                                 start=True, stop=True).then_inc(score_done, 1)

            def turn(j, i, g, head):
                pe.wait_ge(prob_ready, cu.n(j + 1))
                if j or cu.base:
                    pe.wait_ge(pt_left, cu.n(j))
                if j == 0 and cu.base:
                    pe.wait_ge(ot_left, n)
                for w in range(blocks):
                    mm = nc.tensor.transpose(PT[:, w * P:(w + 1) * P], prob[:, j % 2, w * P:(w + 1) * P],
                                             ident[:, :])
                mm.then_inc(pt_done, 1)

            def weigh(j, i, g, head):
                pe.wait_ge(pt_left, cu.n(j + 1))
                if j == 0 and cu.base:
                    pe.wait_ge(osb_ready, n)
                for w in range(blocks):
                    block_n = (key0 // P + w) if edge != 1 else n + (w - 1)
                    mm = nc.tensor.matmul(OA[:, head * AD:(head + 1) * AD], prob_t[:, j % 2, w * P:(w + 1) * P],
                                          att_v[:, bass.ds(block_n, 1), g * AD:(g + 1) * AD].rearrange(
                                              "p a d -> p (a d)"),
                                          start=(w == 0), stop=(w == blocks - 1))
                mm.then_inc(pv_done, 1)

            pieces = [(k, kk) for k in range(2) for kk in range(KD)]
            H = heads()
            for step in range(12):
                for _ in range(2 if step < 4 else 1):
                    k, kk = pieces.pop(0)
                    mix_product(pe, ct, cb, k, [kk])
                if step < AH:
                    score(*H[step])
                if 1 <= step <= AH:
                    turn(*H[step - 1])
                if 2 <= step <= AH + 1:
                    weigh(*H[step - 2])
            pe.wait_ge(osb_ready, n + 1)
            for kt in range(AH // 2):
                mm = nc.tensor.transpose(OT[:, kt * P:(kt + 1) * P], o_sb[:, kt * P:(kt + 1) * P], ident[:, :])
            mm.then_inc(ot_done, 1)

        def mix_pe(pe, b, pre):
            cb, ct = Count(b), Count(0)
            mix_product(pe, ct, cb, 0, u_wait=pre)
            for k in range(1, N_QKV):
                mix_product(pe, ct, cb, k)
                rotate(pe, k - 1)
            turn_values(pe, Count(N_QKV - 1), Count(0), 0)
            with pe.Fori(0, KD // 2) as i:
                cb, ct = Count(b + T_MQK, 2, i), Count(T_MQK, 2, i)
                mix_product(pe, ct, cb, 0)
                mix_product(pe, ct, cb, 1)
            with pe.Fori(0, KD // 4) as i:
                cb, ct, cv = Count(b + T_MV, 4, i), Count(T_MV, 4, i), Count(1, 4, i)
                mix_product(pe, ct, cb, 0)
                for k in range(1, 4):
                    mix_product(pe, ct, cb, k)
                    turn_values(pe, ct, cv, k - 1)
                turn_values(pe, ct, cv, 3)
            att_pe(pe, 0, 0, Count(0), Count(T_SIG), Count(b + T_SIG))
            with pe.Fori(0, NB - 2) as i:
                att_pe(pe, i + 1, 1, Count(AH, AH, i), Count(T_SIG + 2, 2, i), Count(b + T_SIG + 2, 2, i))
            att_pe(pe, NB - 1, 2, Count(AH * (NB - 1)), Count(T_MG - 2), Count(b + T_MG - 2))
            mix_product(pe, Count(T_MG), Count(b + T_MG), 0)
            for k in range(KD):
                mix_product(pe, Count(T_GM), Count(b + T_GM), k)

        def evac(act, ct, k, func, dst, before=()):
            act.wait_ge(mix_done, ct.n(k + 1))
            for s_, v_ in before:
                act.wait_ge(s_, v_)
            nc.scalar.activation(dst, ps[ct.slot(k)][:, :], func).then_inc(mix_left, 1)

        def silu_conv(act, cc, k, m):
            act.wait_ge(conv_done, cc.n(k + 1))
            tile = mqk[:, bass.ds(m, 1), :].rearrange("p a n -> p (a n)")
            nc.scalar.activation(tile, tile, ACT.Silu).then_inc(mqk_ready, 1)

        def conv_act(act, b, i, first):
            cb, ct, cc = Count(b + T_MQK + first, 2, i), Count(T_MQK + first, 2, i), Count(first, 2, i)
            for k in range(2):
                if first + k >= 2:
                    act.wait_ge(conv_done, cc.n(k - 1))
                elif k == 0:
                    act.wait_ge(pad_zero, 1)
                evac(act, ct, k, ACT.Copy, zpad[:, k, TAPS // 2:TAPS // 2 + S])
                split_hi(act, cb, k + 2)
                silu_conv(act, cc, k, i * 2 + (first + k))

        def att_act(act, n, edge, cu, ct, cb, next_hi):
            blocks = att_window(n, edge)[1]
            width = blocks * P

            def expo(j):
                act.wait_ge(neg_ready, cu.n(j + 1))
                nc.scalar.activation(prob[:, j % 2, 0:width], prob[:, j % 2, 0:width], ACT.Exp,
                                     bias=A_NEG[:, j:j + 1], scale=ATT_SCALE,
                                     accum_out=A_SUM[:, j:j + 1]).then_inc(prob_ready, 1)

            def keep(j):
                act.wait_ge(pt_done, cu.n(j + 1))
                if cu.base + j >= 2:
                    act.wait_ge(pv_done, cu.n(j - 1))
                nc.scalar.copy(prob_t[:, j % 2, 0:width], PT[:, 0:width]).then_inc(pt_left, 1)

            def sig(k):
                s = ct.slot(k)
                before = []
                if ct.base + k >= T_SIG + 2:
                    uses = (ct.base + k - T_SIG) // 2
                    before = [(sig_stored[s], 16 * uses if ct.turn is None else ct.turn * 16 + 16 * uses)]
                evac(act, ct, k, ACT.Sigmoid, tmp[:, s, :], before)

            for j in range(AH):
                expo(j)
                if j:
                    keep(j - 1)
                if j == 4:
                    sig(0)
                    next_hi(2)
            keep(AH - 1)
            act.wait_ge(sink_arg, n + 1)
            nc.scalar.activation(A_ESINK[:, :], A_SINK[:, :], ACT.Exp).then_inc(sink_exp, 1)
            sig(1)
            next_hi(3)

        def gates_hi(act, c):
            s = c.slot()
            act.wait_ge(raw_loaded[s], c.uses() * 16)
            act.wait_ge(wz, 2)
            for n in range(4):
                op = nc.scalar.activation(gate_cols(w_hi, s, n), raw_gate_cols(s, n), ACT.Copy)
            op.then_inc(whi_ready, 1)

        def gate_cols(w, s, n):
            first = 64 * (n % 2) + 32 * (n // 2)
            return w[:, s, :].rearrange("p (k n) -> p k n", k=KD)[:, :, first:first + MH]

        def raw_gate_cols(s, n):
            return w_raw[:, s, 0:KD * 4 * MH].rearrange("p (k n) -> p k n", k=KD)[:, :, n * MH:(n + 1) * MH]

        def mix_act(act, b):
            cb, ct = Count(b), Count(0)
            for k in range(N_QKV):
                if k < 2:
                    act.wait_ge(raw_q[cb.slot(k)], 32)
                evac(act, ct, k, ACT.Copy, tmp[:, k % 2, :],
                     [(rope_done, k - 1)] if k >= 2 else [(ulo_ready, 2 * KD)])
                split_hi(act, cb, k + 2)
            with act.Fori(0, MH // 2) as i:
                conv_act(act, b, i, 0)
            with act.Fori(0, MH // 2) as i:
                conv_act(act, b, i, MH)
            act.wait_ge(conv_done, KD)
            with act.Fori(0, KD // 4) as i:
                cb, ct = Count(b + T_MV, 4, i), Count(T_MV, 4, i)
                for k in range(4):
                    evac(act, ct, k, ACT.Copy, tmp[:, ct.slot(k), :], [(vt_done, Count(max(k, 1), 4, i).n())])
                    split_hi(act, cb, k + 2)
            act.wait_ge(vt_done, 1 + KD)
            cb = Count(b + T_SIG)
            att_act(act, 0, 0, Count(0), Count(T_SIG), cb, lambda k: split_hi(act, cb, k))
            with act.Fori(0, NB - 2) as i:
                cbi = Count(b + T_SIG + 2, 2, i)
                att_act(act, i + 1, 1, Count(AH, AH, i), Count(T_SIG + 2, 2, i), cbi,
                        lambda k: split_hi(act, cbi, k))
            last = {2: lambda: gates_hi(act, Count(b + T_MG)), 3: lambda: split_hi(act, Count(b + T_GM), 0)}
            att_act(act, NB - 1, 2, Count(AH * (NB - 1)), Count(T_MG - 2), Count(b + T_MG - 2),
                    lambda k: last[k]())
            act.wait_ge(mix_done, T_MG + 1)
            act.wait_ge(small_loaded, 48)
            act.wait_ge(pv_done, AH * NB)
            acc = ps[T_MG % 2]
            nc.scalar.activation(r_li[:, :], acc[0:CHAIN_ROWS, :], ACT.Identity,
                                 bias=gate_bias[:, 0:1]).then_inc(row_act, 1)
            nc.scalar.activation(r_lf[:, :], acc[CHAIN_ROWS:P, :], ACT.Copy).then_inc(mix_left, 1)
            split_hi(act, Count(b + T_GM), 1)
            act.wait_ge(row_dve, 1)
            nc.scalar.activation(r_b[:, :], r_lf[:, :], ACT.Abs).then_inc(row_act, 1)
            act.wait_ge(row_act, 2)
            nc.scalar.activation(r_b[:, :], r_b[:, :], ACT.Exp, scale=-1.0).then_inc(row_act, 1)
            act.wait_ge(row_act, 3)
            nc.scalar.activation(r_b[:, :], r_b[:, :], ACT.Ln, bias=1.0).then_inc(row_act, 1)

            def gm(ct, cb, k, stored):
                evac(act, ct, k, ACT.Sigmoid, tmp[:, ct.slot(k), :], [(sig_stored[ct.slot(k)], stored)])
                if cb is not None:
                    split_hi(act, cb, k + 2)

            for k in range(2):
                gm(Count(T_GM), Count(b + T_GM), k, 16 * KD)
            act.wait_ge(row_dve, 12)
            nc.scalar.activation(r_wi[:, :], r_wi[:, :], ACT.Exp).then_inc(row_act, 1)
            nc.scalar.activation(r_em[:, :], r_em[:, :], ACT.Exp, scale=-1.0).then_inc(row_act, 1)
            nc.scalar.activation(r_wk[:, :], r_wk[:, :], ACT.Exp).then_inc(row_act, 1)
            with act.Fori(0, 2) as i:
                for k in range(2):
                    gm(Count(T_GM + 2, 2, i), Count(b + T_GM + 2, 2, i), k, i * 16 + 16 * (KD + 1))
            for k in range(6, KD):
                gm(Count(T_GM), None, k, 16 * (KD + k // 2))

        def att_dve(dve, n, edge, cu, cb, next_lo):
            key0, blocks, mask0 = att_window(n, edge)
            width = blocks * P
            if edge:
                dve.wait_ge(score_done, cu.n(0))
            else:
                dve.wait_ge(qst_zero, 1)
                dve.wait_ge(rope_done, AH // 2 + 1)
            for g in range(2):
                rows = slice(64 * g, 64 * g + 64)
                op = copy(q_st[rows, g, :, :], att_q[rows, :, bass.ds(n * P, P)])
            op.then_inc(qst_ready, 1)
            for j in range(AH):
                if cu.base + j >= 2:
                    dve.wait_ge(pt_done, cu.n(j - 1))
                dve.wait_ge(score_done, cu.n(j + 1))
                nc.vector.tensor_copy(tick[:, :], neg_sinks[:, 0:1])
                nc.vector.tensor_tensor_reduce(out=prob[:, j % 2, 0:width], in0=score_bank(j)[:, 0:width],
                                               in1=window[:, mask0:mask0 + width], scale=1.0, scalar=-3e38,
                                               op0=ALU.add, op1=ALU.max, accum_out=A_MAX[:, j:j + 1]
                                               ).then_inc(max_done, 1)
                dve.wait_ge(max_done, cu.n(j + 1))
                if j == 0 and cu.base:
                    dve.wait_ge(den_ready, n)
                nc.vector.tensor_scalar(A_NEG[:, j:j + 1], A_MAX[:, j:j + 1], -ATT_SCALE, neg_sinks[:, j:j + 1],
                                        ALU.mult, ALU.min).then_inc(neg_ready, 1)
                if j == 4:
                    next_lo(2)
            dve.wait_ge(neg_ready, cu.n(AH))
            nc.vector.tensor_tensor(A_SINK[:, :], A_NEG[:, :], neg_sinks[:, :], ALU.subtract).then_inc(sink_arg, 1)
            dve.wait_ge(sink_exp, n + 1)
            dve.wait_ge(prob_ready, cu.n(AH))
            nc.vector.tensor_tensor(A_DEN[:, :], A_SUM[:, :], A_ESINK[:, :], ALU.add).then_inc(den_ready, 1)
            dve.wait_ge(den_ready, n + 1)
            nc.vector.reciprocal(A_REC[:, :], A_DEN[:, :]).then_inc(rec_ready, 1)
            dve.wait_ge(rec_ready, n + 1)
            dve.wait_ge(pv_done, cu.n(AH))
            if cu.base:
                dve.wait_ge(ot_done, n)
            for g in range(2):
                heads_g = slice(g * AH // 2 * AD, (g + 1) * AH // 2 * AD)
                op = nc.vector.tensor_tensor(
                    o_sb[:, heads_g].rearrange("p (i d) -> p i d", d=AD),
                    OA[:, heads_g].rearrange("p (i d) -> p i d", d=AD),
                    A_REC[:, :].rearrange("p (i g) -> p g i", g=2)[:, g, :].unsqueeze(2).to_broadcast(
                        [P, AH // 2, AD]), ALU.mult)
            op.then_inc(osb_ready, 1)
            dve.wait_ge(ot_done, n + 1)
            copy(att_q[:, :, bass.ds(n * P, P)], OT.rearrange("p (k n) -> p k n", n=P)).then_inc(ot_left, 1)
            next_lo(3)

        def rope(dve, k):
            dst = att_q[:, k, :] if k < AH // 2 else att_k[:, :]
            dve.wait_ge(rot_done, k + 1)
            if k:
                dve.wait_ge(rope_done, k)
            nc.vector.tensor_tensor(dst, tmp[:, k % 2, :], cos_sb[:, :], ALU.mult).then_inc(rope_cos, 1)
            nc.vector.tensor_tensor(rope_t[:, :], ps[2][:, :], sin_sb[:, :], ALU.mult).then_inc(rope_sin, 1)
            dve.wait_ge(rope_cos, k + 1)
            dve.wait_ge(rope_sin, k + 1)
            nc.vector.tensor_tensor(dst, dst, rope_t[:, :], ALU.add).then_inc(rope_done, 1)

        def convolve(dve, cc, ct, k, m, slot):
            dve.wait_ge(mix_left, ct.n(k + 1))
            tile = mqk[:, bass.ds(m, 1), :].rearrange("p a n -> p (a n)")
            steps = Count(cc.base * (TAPS - 1), cc.per * (TAPS - 1), cc.turn)

            def vec(first):
                return vecs[:, bass.ds(m + first, 1)]

            nc.vector.tensor_scalar(tile, zpad[:, slot, 0:S], vec(80), vec(72), ALU.mult,
                                    ALU.add).then_inc(conv_step, 1)
            for tap in range(1, TAPS):
                dve.wait_ge(conv_step, steps.n((TAPS - 1) * k + tap))
                nc.vector.scalar_tensor_tensor(out=tile, in0=zpad[:, slot, tap:tap + S], scalar=vec(80 + KD * tap),
                                               in1=tile, op0=ALU.mult, op1=ALU.add
                                               ).then_inc(conv_step if tap < TAPS - 1 else conv_done, 1)

        def conv_dve(dve, b, i, first):
            cb, ct, cc = Count(b + T_MQK + first, 2, i), Count(T_MQK + first, 2, i), Count(first, 2, i)
            for k in range(2):
                split_lo(dve, cb, k + 2)
                convolve(dve, cc, ct, k, i * 2 + (first + k), k)

        def mix_dve(dve, b):
            cb = Count(b)
            dve.wait_ge(tables_loaded, 64)
            for k in range(N_QKV - 1):
                split_lo(dve, cb, k + 2)
                rope(dve, k)
            split_lo(dve, cb, N_QKV + 1)
            dve.wait_ge(vt_done, 1)
            nc.vector.tensor_copy(att_v[:, :, :], ps[3][:, :].rearrange("p (b n) -> p b n", n=P)
                                  ).then_inc(vt_left, 1)
            dve.wait_ge(spilled, 16 * KD)
            with dve.Fori(0, MH // 2) as i:
                conv_dve(dve, b, i, 0)
            with dve.Fori(0, MH // 2) as i:
                conv_dve(dve, b, i, MH)
            dve.wait_ge(ones_v, 1)
            with dve.Fori(0, KD // 4) as i:
                cb, cv = Count(b + T_MV, 4, i), Count(1, 4, i)
                for k in range(4):
                    split_lo(dve, cb, k + 2)
                    dve.wait_ge(vt_done, cv.n(k + 1))
                    copy(m_v[:, :, bass.ds(i * 2 + k // 2, 1), (k % 2) * P:(k % 2 + 1) * P],
                         ps[3][:, :].rearrange("p (b a n) -> p b a n", a=1, n=P)).then_inc(vt_left, 1)
            dve.wait_ge(small_loaded, 48)
            nc.vector.tensor_scalar(neg_sinks.rearrange("p (i g) -> p i g", g=2),
                                    sinks[:, :].rearrange("p (g i) -> p i g", g=2), -1.0, None, ALU.mult).then_inc(sinks_ready, 1)
            dve.wait_ge(sinks_ready, 1)
            cb = Count(b + T_SIG)
            att_dve(dve, 0, 0, Count(0), cb, lambda k: split_lo(dve, cb, k))
            with dve.Fori(0, NB - 2) as i:
                cbi = Count(b + T_SIG + 2, 2, i)
                att_dve(dve, i + 1, 1, Count(AH, AH, i), cbi, lambda k: split_lo(dve, cbi, k))

            def gates_lo(c):
                s = c.slot()
                dve.wait_ge(block_used, c.n(-RING + 1))
                dve.wait_ge(wlo_ready, c.n(-RING + 1))
                for w in (w_hi, w_lo):
                    nc.vector.memset(w[:, s, :].bitcast(F32), 0.0).then_inc(wz, 1)
                dve.wait_ge(whi_ready, c.n(1))
                dve.wait_ge(wz, 2)
                for n in range(4):
                    op = nc.vector.tensor_tensor(gate_cols(w_lo, s, n), raw_gate_cols(s, n),
                                                 gate_cols(w_hi, s, n).bitcast(F32), ALU.subtract)
                op.then_inc(wlo_ready, 1)

            last = {2: lambda: gates_lo(Count(b + T_MG)), 3: lambda: split_lo(dve, Count(b + T_GM), 0)}
            att_dve(dve, NB - 1, 2, Count(AH * (NB - 1)), Count(b + T_MG - 2), lambda k: last[k]())
            split_lo(dve, Count(b + T_GM), 1)
            dve.wait_ge(mix_left, T_MG + 1)
            dve.wait_ge(tables_loaded, 80)

            fw, bw = slice(0, 32), slice(32, CHAIN_ROWS)
            nc.vector.tensor_scalar(r_lf[:, :], r_lf[:, :], gate_bias[:, 1:2], None, ALU.add).then_inc(row_dve, 1)
            dve.wait_ge(row_act, 4)
            nc.vector.scalar_tensor_tensor(out=r_lf[:, :], in0=r_lf[:, :], scalar=0.0, in1=r_b[:, :], op0=ALU.min,
                                           op1=ALU.subtract).then_inc(row_dve, 1)
            dve.wait_ge(row_dve, 2)
            nc.vector.tensor_tensor_scan(r_b[fw, :], r_in[fw, :], r_lf[fw, :], 0.0, ALU.mult,
                                         ALU.add).then_inc(row_dve, 1)
            nc.vector.tensor_tensor_scan(r_b[bw, ::-1], r_in[bw, ::-1], r_lf[bw, ::-1], 0.0, ALU.mult,
                                         ALU.add).then_inc(row_dve, 1)
            nc.vector.tensor_tensor_scan(r_m[fw, :], r_lf[fw, :], r_li[fw, :], 0.0, ALU.add,
                                         ALU.max).then_inc(row_dve, 1)
            nc.vector.tensor_tensor_scan(r_m[bw, ::-1], r_lf[bw, ::-1], r_li[bw, ::-1], 0.0, ALU.add,
                                         ALU.max).then_inc(row_dve, 1)
            dve.wait_ge(row_dve, 6)
            nc.vector.tensor_tensor(r_g[:, :], r_li[:, :], r_b[:, :], ALU.subtract).then_inc(row_dve, 1)
            dve.wait_ge(row_dve, 7)
            nc.vector.tensor_tensor(r_r[:, :], r_m[:, :], r_b[:, :], ALU.subtract).then_inc(row_dve, 1)
            dve.wait_ge(row_dve, 8)
            before, last_r = chunk_rows[:, 0, :], chunk_rows[:, 1, :]
            m_t = r_m[:, :].rearrange("p (b n) -> p b n", n=P)
            r_t = r_r[:, :].rearrange("p (b n) -> p b n", n=P)
            nc.vector.memset(chunk_rows[:, :, :], 0.0).then_inc(row_dve, 1)
            dve.wait_ge(row_dve, 9)
            nc.vector.tensor_copy(before[fw, 1:NB], m_t[fw, 0:NB - 1, P - 1])
            nc.vector.tensor_copy(before[bw, 0:NB - 1], m_t[bw, 1:NB, 0])
            nc.vector.tensor_copy(last_r[fw, :], r_t[fw, :, P - 1])
            nc.vector.tensor_copy(last_r[bw, :], r_t[bw, :, 0]).then_inc(row_dve, 1)
            dve.wait_ge(row_dve, 10)

            def spread(x):
                return x.unsqueeze(2).to_broadcast([CHAIN_ROWS, NB, P])

            nc.vector.tensor_tensor(r_wi[:, :].rearrange("p (b n) -> p b n", n=P), spread(before), r_t,
                                    ALU.subtract).then_inc(row_dve, 1)
            nc.vector.tensor_tensor(r_wk[:, :].rearrange("p (b n) -> p b n", n=P),
                                    r_g[:, :].rearrange("p (b n) -> p b n", n=P), spread(last_r),
                                    ALU.subtract).then_inc(row_dve, 1)
            cb = Count(b + T_GM)
            split_lo(dve, cb, 2)
            split_lo(dve, cb, 3)
            with dve.Fori(0, 2) as i:
                for k in range(2):
                    split_lo(dve, Count(b + T_GM + 2, 2, i), k + 2)
        (cols_turned, cols_left, chains_loaded, hk_ready, hsel_ready, hcol_ready, st_done, kt_done, rb_done, arg_sub,
         arg_ready, exp_ready, s_ready, wb_done, q_ready, dec_ready, kw_ready, out_done, dc_done, c_ready, den_abs, den_max,
         den_inv, hm_left, sq_heads) = (sem(x) for x in (
            "cols_turned", "cols_left", "chains_loaded", "hk_ready", "hsel_ready", "hcol_ready", "st_done",
            "kt_done", "rb_done", "arg_sub", "arg_ready", "exp_ready", "s_ready", "wb_done", "q_ready", "dec_ready",
            "kw_ready", "out_done", "dc_done", "c_ready", "den_abs", "den_max", "den_inv", "hm_left", "sq_heads"))
        ST = ps[0]
        BCAST = ps[1]
        KT = ps[2]
        G_COL, WK_COL, EM_COL = range(3)
        UNITS = 2 * NB

        def chunk_of(way, n):
            return n if way == 0 else NB - 1 - n

        def d_state(way):
            return ps[2][:, way * HALF:way * HALF + MV + 1]

        def d_out(way):
            return ps[3][:, way * HALF:way * HALF + MV + 1]

        def mlstm_pe(pe):
            pe.wait_ge(row_act, 7)
            pe.wait_ge(row_dve, 12)
            for n in range(NB):
                for q, rows in ((G_COL, r_g), (WK_COL, r_wk), (EM_COL, r_em)):
                    at_ = (n * 3 + q) * CHAIN_ROWS
                    mm = nc.tensor.transpose(ps[2 + at_ // S][:, at_ % S:at_ % S + CHAIN_ROWS],
                                             rows[:, n * P:(n + 1) * P], ident[0:CHAIN_ROWS, 0:CHAIN_ROWS])
            mm.then_inc(cols_turned, 1)
            pe.wait_ge(cols_left, 2)
            pe.wait_ge(mix_left, N_TILES)
            with pe.Fori(0, MH) as h:
                head = Count(0, 1, h)
                ways = Count(0, 2, h)
                units = Count(0, UNITS, h)
                q_h = mqk[:, bass.ds(h, 1), :].rearrange("p a n -> p (a n)")
                pe.wait_ge(hk_ready, head.n(1))
                for n in range(NB):
                    mm = nc.tensor.matmul(ST[:, n * P:(n + 1) * P], h_k[:, n, :],
                                          mqk[:, bass.ds(h, 1), n * P:(n + 1) * P].rearrange("p a n -> p (a n)"),
                                          start=True, stop=True)
                mm.then_inc(st_done, 1)
                for n in range(NB):
                    mm = nc.tensor.transpose(KT[:, n * P:(n + 1) * P], h_k[:, n, :], ident[:, :])
                mm.then_inc(kt_done, 1)
                pe.wait_ge(hsel_ready, ways.n(2))
                for way in range(2):
                    if way:
                        pe.wait_ge(dec_ready, ways.n(way))
                    for f in range(2):
                        mm = nc.tensor.matmul(BCAST[:, f * HALF:(f + 1) * HALF], h_sel[:, way, :],
                                              r_r[:, f * HALF:(f + 1) * HALF], start=True, stop=True)
                    mm.then_inc(rb_done, 1)
                    pe.wait_ge(arg_sub, ways.n(way + 1))
                    for f in range(2):
                        mm = nc.tensor.matmul(BCAST[:, f * HALF:(f + 1) * HALF], h_sel[:, way, :],
                                              r_wi[:, f * HALF:(f + 1) * HALF], start=True, stop=True)
                    mm.then_inc(wb_done, 1)
                pe.wait_ge(kw_ready, ways.n(2))
                for n in range(NB):
                    for way in range(2):
                        c = chunk_of(way, n)
                        u = n * 2 + way
                        v = m_v[:, c, bass.ds(h, 1), :].rearrange("p a n -> p (a n)")
                        if n == 0:
                            pe.wait_ge(s_ready, ways.n(way + 1))
                        if u >= 2:
                            pe.wait_ge(hm_left, units.n(u - 1))
                        mm = nc.tensor.matmul(d_out(way), h_s[:, way, c, :], v, start=True, stop=(n == 0))
                        if n:
                            if n == 1:
                                pe.wait_ge(q_ready, ways.n(way + 1))
                            pe.wait_ge(c_ready, Count(0, UNITS - 2, h).n(u - 1))
                            mm = nc.tensor.matmul(d_out(way), h_q[:, way, c, :], state[:, way, n % 2, :],
                                                  start=False, stop=True)
                        mm.then_inc(out_done, 1)
                        if n < NB - 1:
                            nc.tensor.matmul(d_state(way), h_kw[:, way, c, :], v, start=True,
                                             stop=True).then_inc(dc_done, 1)

        def mlstm_act(act):
            nc.scalar.copy(h_tick[:, :], ones[:, 0:1]).then_inc(sq_heads, 1)
            with act.Fori(0, MH) as h:
                ways = Count(0, 2, h)
                units = Count(0, UNITS, h)
                for way in range(2):
                    act.wait_ge(arg_ready, ways.n(way + 1))
                    nc.scalar.activation(h_s[:, way, :, :], h_arg[:, :, :], ACT.Exp,
                                         scale=-1.0).then_inc(exp_ready, 1)
                act.wait_ge(hm_left, units.n(UNITS))
                act.wait_ge(sq_heads, Count(1, NB, h).n())
                nc.scalar.copy(h_tick[:, :], ones[:, 0:1])
                for c in range(NB):
                    nc.scalar.activation(h_junk[c][:, :], hm[:, c, bass.ds(h, 1), :].rearrange("p a n -> p (a n)"),
                                         ACT.Square, accum_out=m_cols[:, 0, bass.ds(h * NB + c, 1)]
                                         ).then_inc(sq_heads, 1)

        def mlstm_dve(dve):
            dve.wait_ge(cols_turned, 1)
            dve.wait_ge(mix_done, N_TILES)
            flat = col[:, :, :, :].rearrange("p b q n -> p (b q n)")
            nc.vector.tensor_copy(flat[:, 0:S], ps[2][:, :]).then_inc(cols_left, 1)
            nc.vector.tensor_copy(flat[:, S:3 * NB * CHAIN_ROWS], ps[3][:, 0:3 * NB * CHAIN_ROWS - S]
                                  ).then_inc(cols_left, 1)
            dve.wait_ge(cols_left, 2)
            dve.wait_ge(chains_loaded, 48)
            for s in range(2):
                dve.wait_ge(sig_stored[s], 16 * 12)
            with dve.Fori(0, MH) as h:
                head = Count(0, 1, h)
                ways = Count(0, 2, h)
                units = Count(0, UNITS, h)
                turns = Count(0, UNITS - 2, h)
                copy(h_k[:, :, :].rearrange("p n k -> p (n k)"),
                     mqk[:, bass.ds(h + MH, 1), :].rearrange("p a n -> p (a n)"), K_SCALE).then_inc(hk_ready, 1)
                for way in range(2):
                    copy(h_sel[:, way, :], chains[:, way, bass.ds(h, 1), :].rearrange("p a n -> p (a n)")
                         ).then_inc(hsel_ready, 1)
                    copy(h_col[:, way, :, :],
                         col[:, :, :, bass.ds(h + 32 * way, 1)].rearrange("p b q a -> p b (q a)")
                         ).then_inc(hcol_ready, 1)
                for way in range(2):
                    def spread(q):
                        return h_col[:, way, :, q].unsqueeze(2).to_broadcast([P, NB, P])

                    dve.wait_ge(rb_done, ways.n(way + 1))
                    dve.wait_ge(hcol_ready, ways.n(2))
                    if way:
                        dve.wait_ge(exp_ready, ways.n(way))
                    nc.vector.tensor_tensor(h_arg[:, :, :], BCAST[:, :].rearrange("p (b n) -> p b n", n=P),
                                            spread(G_COL), ALU.subtract).then_inc(arg_sub, 1)
                    dve.wait_ge(arg_sub, ways.n(way + 1))
                    nc.vector.tensor_tensor(h_arg[:, :, :], h_arg[:, :, :],
                                            order[:, way, :].unsqueeze(1).to_broadcast([P, NB, P]),
                                            ALU.max).then_inc(arg_ready, 1)
                    if way == 0:
                        dve.wait_ge(kt_done, head.n(1))
                        for w2 in range(2):
                            nc.vector.tensor_tensor(h_kw[:, w2, :, :], KT[:, :].rearrange("p (b n) -> p b n", n=P),
                                                    h_col[:, w2, :, WK_COL].unsqueeze(2).to_broadcast([P, NB, P]),
                                                    ALU.mult).then_inc(kw_ready, 1)
                    dve.wait_ge(wb_done, ways.n(way + 1))
                    nc.vector.tensor_tensor(h_q[:, way, :, :].rearrange("p b n -> p (b n)"),
                                            mqk[:, bass.ds(h, 1), :].rearrange("p a n -> p (a n)"), BCAST[:, :],
                                            ALU.mult).then_inc(q_ready, 1)
                    last = 0 if way else P - 1
                    nc.vector.tensor_copy(h_dec[:, way, :],
                                          BCAST[:, :].rearrange("p (b n) -> p b n", n=P)[:, :, last]
                                          ).then_inc(dec_ready, 1)
                    dve.wait_ge(exp_ready, ways.n(way + 1))
                    dve.wait_ge(st_done, head.n(1))
                    nc.vector.tensor_tensor(h_s[:, way, :, :], ST[:, :].rearrange("p (b n) -> p b n", n=P),
                                            h_s[:, way, :, :], ALU.mult).then_inc(s_ready, 1)
                dve.wait_ge(dec_ready, ways.n(2))
                for n in range(NB):
                    for way in range(2):
                        c = chunk_of(way, n)
                        u = n * 2 + way
                        if n < NB - 1:
                            dve.wait_ge(dc_done, turns.n(u + 1))
                            if n == 0:
                                nc.vector.tensor_copy(state[:, way, 1, :], d_state(way)).then_inc(c_ready, 1)
                            else:
                                dve.wait_ge(c_ready, turns.n(u - 1))
                                nc.vector.scalar_tensor_tensor(
                                    out=state[:, way, (n + 1) % 2, :], in0=state[:, way, n % 2, :],
                                    scalar=h_dec[:, way, c:c + 1], in1=d_state(way), op0=ALU.mult,
                                    op1=ALU.add).then_inc(c_ready, 1)
                        dve.wait_ge(out_done, units.n(u + 1))
                        acc = d_out(way)
                        nc.vector.tensor_scalar(h_den[:, way, 0:1], acc[:, MV:MV + 1], -1.0,
                                                h_col[:, way, c, EM_COL:EM_COL + 1], ALU.mult, ALU.max
                                                ).then_inc(den_abs, 1)
                        dve.wait_ge(den_abs, units.n(u + 1))
                        nc.vector.tensor_tensor(h_den[:, way, 0:1], h_den[:, way, 0:1], acc[:, MV:MV + 1],
                                                ALU.max).then_inc(den_max, 1)
                        dve.wait_ge(den_max, units.n(u + 1))
                        nc.vector.reciprocal(h_den[:, way, 1:2], h_den[:, way, 0:1]).then_inc(den_inv, 1)
                        dve.wait_ge(den_inv, units.n(u + 1))
                        out_h = hm[:, c, bass.ds(h, 1), :].rearrange("p a n -> p (a n)")
                        if n < NB // 2:
                            nc.vector.tensor_scalar(out_h, acc[:, 0:MV], h_den[:, way, 1:2], None,
                                                    ALU.mult).then_inc(hm_left, 1)
                        else:
                            nc.vector.scalar_tensor_tensor(out=out_h, in0=acc[:, 0:MV], scalar=h_den[:, way, 1:2],
                                                           in1=out_h, op0=ALU.mult, op1=ALU.add
                                                           ).then_inc(hm_left, 1)

        def mlstm_sp(sp):
            sp.wait_ge(cols_turned, 1)
            sp.dma_start(chains[:, :, :, :].rearrange("p w h n -> p (w h n)"),
                         table("chains", CHAIN_ROWS)).then_inc(chains_loaded, 16)
            sp.dma_start(order[:, 0, :], table("later")).then_inc(chains_loaded, 16)
            sp.dma_start(order[:, 1, :], table("earlier")).then_inc(chains_loaded, 16)


        (heads_mean, heads_root, heads_inv, hm_scaled, hm_turned, hmhi_ready, mlo_ready, ohi_ready, olo_ready,
         br_attn, br_mlstm, br_sum, mghi_ready, resid_back) = (sem(x) for x in (
            "heads_mean", "heads_root", "heads_inv", "hm_scaled", "hm_turned", "hmhi_ready", "mlo_ready",
            "ohi_ready", "olo_ready", "br_attn", "br_mlstm", "br_sum", "mghi_ready", "resid_back"))
        sig_loaded = [sem(f"sig_loaded{n}") for n in range(2)]
        sig_free = [sem(f"sig_free{n}") for n in range(2)]
        T_BR = N_TILES
        T_WO = T_BR + 2 * KD
        T_END = T_WO + KD
        GATED = KD // 2

        def k_tiles(w, first):
            return w[:, bass.ds(first, P)].rearrange("(k p) n -> p k n", p=P)

        def load_part(sp, c, k, src):
            sp.wait_ge(wlo_ready, c.n(k - RING + 1))
            s = c.slot(k)
            nk = src.shape[1]
            sp.dma_start(w_raw[:, s, 0:nk * P].rearrange("p (k n) -> p k n", k=nk), src).then_inc(raw_loaded[s], 16)

        def branch_sp(sp, b):
            W_A, W_M, W_O = t["w_branch_attn"][0], t["w_branch_mlstm"][0], t["w_out"][0]
            load_part(sp, Count(b + T_BR), 0, k_tiles(W_A, 0))
            load(sp, Count(b + T_BR), 1, k_tiles(W_M, 0))
            mlstm_sp(sp)
            sp.wait_ge(hsel_ready, 2 * MH)
            sp.wait_ge(arg_ready, 2 * MH)
            for m in range(KD):
                if m == 1:
                    sp.wait_ge(sq_heads, 1 + MH * NB)
                if m >= 2:
                    sp.wait_ge(sig_free[m % 2], m // 2)
                sp.dma_start(sig_in[:, m % 2, :], sig_dram[m]).then_inc(sig_loaded[m % 2], 16)

            def merge_gates(m, k, i):
                for j in range(2):
                    sp.wait_ge(sig_free[j], Count(GATED + k, 2, i).n())
                    sp.dma_start(sig_in[:, j, :], sig_tile(m + KD * (1 + j))).then_inc(sig_loaded[j], 16)

            with sp.Fori(0, KD // 2 - 1) as i:
                c = Count(b + T_BR + 2, 4, i)
                for k in range(2):
                    merge_gates(i * 2 + k, k, i)
                    load_part(sp, c, 2 * k, k_tiles(W_A, i * (2 * P) + (k + 1) * P))
                    load(sp, c, 2 * k + 1, k_tiles(W_M, i * (2 * P) + (k + 1) * P))
            merge_gates(KD - 2, KD - 2, None)
            c = Count(b + T_WO - 2)
            load_part(sp, c, 0, k_tiles(W_A, (KD - 1) * P))
            load(sp, c, 1, k_tiles(W_M, (KD - 1) * P))
            merge_gates(KD - 1, KD - 1, None)
            for m in range(KD):
                load(sp, Count(b + T_WO), m, k_tiles(W_O, m * P))
                if m == 1:
                    sp.wait_ge(block_used, b + T_WO)
                    for k in range(KD):
                        sp.dma_start(resid[:, k, :], resid_dram[k]).then_inc(resid_back, 16)

        def branch_pe(pe, b):
            for m in range(KD):
                pe.wait_ge(hm_scaled, m // 2 + 1)
                if m >= 4:
                    pe.wait_ge(sig_free[m % 2], (m - 4) // 2 + 1)
                for c in range(NB):
                    mm = nc.tensor.transpose(ps[m % 4][:, c * P:(c + 1) * P],
                                             hm[:, c, m // 2, (m % 2) * P:(m % 2 + 1) * P], ident[:, :])
                mm.then_inc(hm_turned, 1)
            pe.wait_ge(olo_ready, AH // 2)
            pe.wait_ge(mlo_ready, KD)
            with pe.Fori(0, KD // 2) as i:
                c = Count(b + T_BR, 4, i)
                for j in range(2):
                    pe.wait_ge(wlo_ready, c.n(2 * j + 1))
                    pe.wait_ge(sig_free[0], Count(GATED + j - 1, 2, i).n())
                    product(ps[2 * j], [(c.slot(2 * j), k * P, o_hi[:, k, :], o_lo[:, k, :])
                                        for k in range(AH // 2)], new_block=True).then_inc(br_attn, 1)
                    pe.wait_ge(wlo_ready, c.n(2 * j + 2))
                    pe.wait_ge(sig_free[1], Count(GATED + j - 1, 2, i).n())
                    product(ps[2 * j + 1], [(c.slot(2 * j + 1), k * P, hm_hi[:, k, :], hm_lo[:, k, :])
                                            for k in range(KD)], new_block=True).then_inc(br_mlstm, 1)
            for j in range(2):
                pe.wait_ge(sig_free[j], GATED + KD)
            pe.wait_ge(mlo_ready, 2 * KD)
            with pe.Fori(0, KD // 4) as i:
                c, ct = Count(b + T_WO, 4, i), Count(N_TILES, 4, i)
                for m in range(4):
                    pe.wait_ge(wlo_ready, c.n(m + 1))
                    pe.wait_ge(mix_left, ct.n(m - 3))
                    product(ps[m], [(c.slot(m), k * P, mg_hi[:, k, :], mg_lo[:, k, :]) for k in range(KD)],
                            new_block=True).then_inc(mix_done, 1)

        def branch_act(act, b):
            act.wait_ge(heads_mean, 1)
            nc.scalar.activation(m_cols[:, 1, :], m_cols[:, 1, :], ACT.Sqrt).then_inc(heads_root, 1)
            act.wait_ge(out_done, MH * UNITS)
            for k in range(AH // 2):
                nc.scalar.activation(o_hi[:, k, :], att_q[:, k, :], ACT.Copy).then_inc(ohi_ready, 1)
            for m in range(KD):
                act.wait_ge(sig_free[m % 2], m // 2 + 1)
                nc.scalar.activation(hm_hi[:, m, :], tmp[:, m % 2, :], ACT.Copy).then_inc(hmhi_ready, 1)
            split_hi(act, Count(b + T_BR), 0)
            with act.Fori(0, KD // 2) as i:
                for k in range(4):
                    split_hi(act, Count(b + T_BR, 4, i), k + 1)
            for m in range(KD):
                if m + 1 < KD:
                    split_hi(act, Count(b + T_WO), m + 1)
                act.wait_ge(mix_done, N_TILES + m + 1)
                nc.scalar.activation(mix_y[:, m, :], ps[m % 4][:, :], ACT.Copy).then_inc(mix_left, 1)

        def branch_dve(dve, b):
            dve.wait_ge(sq_heads, 1 + MH * NB)
            nc.vector.tensor_scalar(m_cols[:, 1, :], m_cols[:, 0, :], 1.0 / MV, EPS, ALU.mult,
                                    ALU.add).then_inc(heads_mean, 1)
            dve.wait_ge(heads_root, 1)
            nc.vector.reciprocal(m_cols[:, 2, :], m_cols[:, 1, :]).then_inc(heads_inv, 1)
            dve.wait_ge(heads_inv, 1)
            for h in range(MH):
                nc.vector.tensor_tensor(hm[:, :, h, :], hm[:, :, h, :],
                                        m_cols[:, 2, h * NB:(h + 1) * NB].unsqueeze(2).to_broadcast([P, NB, MV]),
                                        ALU.mult).then_inc(hm_scaled, 1)

            def gated(m):
                dve.wait_ge(hm_turned, m + 1)
                dve.wait_ge(sig_loaded[m % 2], 16 * (m // 2 + 1))
                if m >= 2:
                    dve.wait_ge(mlo_ready, m - 1)
                nc.vector.scalar_tensor_tensor(out=tmp[:, m % 2, :], in0=ps[m % 4][:, :], scalar=vecs[:, 64 + m:65 + m],
                                               in1=sig_in[:, m % 2, :], op0=ALU.mult, op1=ALU.mult
                                               ).then_inc(sig_free[m % 2], 1)

            def gated_lo(m):
                dve.wait_ge(hmhi_ready, m + 1)
                nc.vector.tensor_tensor(hm_lo[:, m, :], tmp[:, m % 2, :], hm_hi[:, m, :].bitcast(F32),
                                        ALU.subtract).then_inc(mlo_ready, 1)

            gated(0)
            for m in range(1, KD):
                gated(m)
                gated_lo(m - 1)
            gated_lo(KD - 1)
            for k in range(AH // 2):
                dve.wait_ge(ohi_ready, k + 1)
                nc.vector.tensor_tensor(o_lo[:, k, :], att_q[:, k, :], o_hi[:, k, :].bitcast(F32),
                                        ALU.subtract).then_inc(olo_ready, 1)
            dve.wait_ge(olo_ready, AH // 2)
            dve.wait_ge(hm_turned, KD)
            split_lo(dve, Count(b + T_BR), 0)
            with dve.Fori(0, KD // 2) as i:
                c = Count(b + T_BR, 4, i)
                for j in range(2):
                    n = Count(j, 2, i)
                    split_lo(dve, c, 2 * j + 1)
                    split_lo(dve, c, 2 * j + 2)
                    dve.wait_ge(br_attn, n.n(1))
                    dve.wait_ge(sig_loaded[0], Count(16 * (GATED + j + 1), 32, i).n())
                    dve.wait_ge(mlo_ready, n.n(KD))
                    nc.vector.tensor_tensor(tmp[:, 0, :], ps[2 * j][:, :], sig_in[:, 0, :],
                                            ALU.mult).then_inc(sig_free[0], 1)
                    dve.wait_ge(br_mlstm, n.n(1))
                    dve.wait_ge(sig_loaded[1], Count(16 * (GATED + j + 1), 32, i).n())
                    nc.vector.tensor_tensor(tmp[:, 1, :], ps[2 * j + 1][:, :], sig_in[:, 1, :],
                                            ALU.mult).then_inc(sig_free[1], 1)
                    dve.wait_ge(sig_free[0], Count(GATED + j + 1, 2, i).n())
                    dve.wait_ge(sig_free[1], Count(GATED + j + 1, 2, i).n())
                    nc.vector.tensor_tensor(tmp[:, 0, :], tmp[:, 0, :], tmp[:, 1, :], ALU.add).then_inc(br_sum, 1)
                    dve.wait_ge(br_sum, n.n(1))
                    hi = mg_hi[:, bass.ds(i * 2 + j, 1), :].rearrange("p a n -> p (a n)")
                    lo = mg_lo[:, bass.ds(i * 2 + j, 1), :].rearrange("p a n -> p (a n)")
                    copy(hi, tmp[:, 0, :]).then_inc(mghi_ready, 1)
                    dve.wait_ge(mghi_ready, n.n(1))
                    nc.vector.tensor_tensor(lo, tmp[:, 0, :], hi.bitcast(F32), ALU.subtract).then_inc(mlo_ready, 1)
            for m in range(1, KD):
                split_lo(dve, Count(b + T_WO), m)

        p_loaded, p_turned, phi_ready, plo_ready = (sem(x) for x in ("p_loaded", "p_turned", "phi_ready",
                                                                     "plo_ready"))
        PAIRS = 2 * GROUPS * GROUP

        def ple_sp(sp, b):
            W_G, W_P = t["w_ple_gate"][0], t["w_ple_proj"][0]
            load(sp, Count(b), 0, k_tiles(W_G, 0))
            load_part(sp, Count(b), 1, k_tiles(W_P, 0))
            sp.wait_ge(stat_done, 7)
            sp.dma_start(p_in[:, :, :], t["p"][0, 0].rearrange("(n q) c -> q n c", q=P)).then_inc(p_loaded, 16)
            with sp.Fori(0, KD // 2 - 1) as i:
                c = Count(b + 2, 4, i)
                for k in range(2):
                    load(sp, c, 2 * k, k_tiles(W_G, i * (2 * P) + (k + 1) * P))
                    load_part(sp, c, 2 * k + 1, k_tiles(W_P, i * (2 * P) + (k + 1) * P))
            load(sp, Count(b + 2 * KD - 2), 0, k_tiles(W_G, (KD - 1) * P))
            load_part(sp, Count(b + 2 * KD - 2), 1, k_tiles(W_P, (KD - 1) * P))

        def ple_pe(pe, b):
            pe.wait_ge(p_loaded, 16)
            pe.wait_ge(mean_ready, 7)
            for k in range(PLE // P):
                for n in range(NB):
                    mm = nc.tensor.transpose(ps[2 * k + 1][:, n * P:(n + 1) * P], p_in[:, n, k * P:(k + 1) * P],
                                             ident[:, :])
                mm.then_inc(p_turned, 1)
            pe.wait_ge(ulo_ready, 4 * KD)
            pe.wait_ge(plo_ready, PLE // P)
            with pe.Fori(0, KD // 2) as i:
                c = Count(b, 4, i)
                for j in range(2):
                    pe.wait_ge(wlo_ready, c.n(2 * j + 1))
                    pe.wait_ge(silu_done, Count(PAIRS + j - 1, 2, i).n())
                    product(ps[2 * j], [(c.slot(2 * j), k * P, u_hi[:, k, :], u_lo[:, k, :]) for k in range(KD)],
                            new_block=True).then_inc(gateup_done, 1)
                    pe.wait_ge(wlo_ready, c.n(2 * j + 2))
                    pe.wait_ge(prod_done, Count(PAIRS + j - 1, 2, i).n())
                    product(ps[2 * j + 1], [(c.slot(2 * j + 1), k * P, p_hi[:, k, :], p_lo[:, k, :])
                                            for k in range(PLE // P)], new_block=True).then_inc(gateup_done, 1)

        def ple_act(act, b):
            for k in range(PLE // P):
                act.wait_ge(p_turned, k + 1)
                nc.scalar.activation(p_hi[:, k, :], ps[2 * k + 1][:, :], ACT.Copy).then_inc(phi_ready, 1)
            split_hi(act, Count(b), 0)

            def turn(c, g, last):
                for j in range(2):
                    split_hi(act, c, 2 * j + 1)
                    act.wait_ge(gateup_done, 2 * g.n(j) + 1)
                    act.wait_ge(prod_done, g.n(j - 1))
                    nc.scalar.activation(tmp[:, j, :], ps[2 * j][:, :], ACT.Sigmoid).then_inc(silu_done, 1)
                    if not (last and j):
                        split_hi(act, c, 2 * j + 2)

            with act.Fori(0, KD // 2 - 1) as i:
                turn(Count(b, 4, i), Count(PAIRS, 2, i), False)
            turn(Count(b + 2 * KD - 4), Count(PAIRS + KD - 2), True)

        def ple_dve(dve, b):
            for k in range(PLE // P):
                dve.wait_ge(phi_ready, k + 1)
                nc.vector.tensor_tensor(p_lo[:, k, :], ps[2 * k + 1][:, :], p_hi[:, k, :].bitcast(F32),
                                        ALU.subtract).then_inc(plo_ready, 1)
            split_lo(dve, Count(b), 0)

            def turn(c, g, m, last):
                for j in range(2):
                    split_lo(dve, c, 2 * j + 1)
                    if not (last and j):
                        split_lo(dve, c, 2 * j + 2)
                    dve.wait_ge(silu_done, g.n(j + 1))
                    dve.wait_ge(gateup_done, 2 * g.n(j) + 2)
                    nc.vector.tensor_tensor(yacc[:, bass.ds(m + j, 1), :].rearrange("p a n -> p (a n)"),
                                            tmp[:, j, :], ps[2 * j + 1][:, :], ALU.mult).then_inc(prod_done, 1)

            with dve.Fori(0, KD // 2 - 1) as i:
                turn(Count(b, 4, i), Count(PAIRS, 2, i), i * 2, False)
            turn(Count(b + 2 * KD - 4), Count(PAIRS + KD - 2), KD - 2, True)

        vecs_copied = sem("vecs_copied")
        bias_zero = sem("bias_zero")
        B_MIX = BLOCKS_FFN
        B_FFN2 = B_MIX + T_END
        B_PLE = B_FFN2 + BLOCKS_FFN

        block = ctx.enter_context(nc.Block())

        @block.gpsimd
        def _(pool):
            nc.gpsimd.memset(ident[:, :], 0.0).then_inc(ident_zero, 1)
            pool.wait_ge(ident_zero, 1)
            nc.gpsimd.affine_select(out=ident[:, :], in_=ident[:, :], compare_op=ALU.not_equal, fill=1.0, base=0,
                                    pattern=[[-1, P]], channel_multiplier=1).then_inc(consts_ready, 1)
            nc.gpsimd.memset(ones[:, :], 1.0).then_inc(consts_ready, 1)
            nc.gpsimd.memset(gate_bias[:, :], 0.0).then_inc(bias_zero, 1)
            nc.gpsimd.memset(q_st[:, :, :, :], 0.0).then_inc(qst_zero, 1)
            pool.wait_ge(x_kept, KD)
            for m in range(KD):
                nc.gpsimd.memset(yacc[:, m, :], 0.0).then_inc(y_added, 1)
            pool.wait_ge(rope_done, AH // 2 + 1)
            nc.gpsimd.memset(m_v[:, :, :, MV:MV + 1], 1.0).then_inc(ones_v, 1)
            pool.wait_ge(vt_done, 1)
            for side in (slice(0, TAPS // 2), slice(TAPS // 2 + S, S + TAPS - 1)):
                op = nc.gpsimd.memset(zpad[:, :, side], 0.0)
            op.then_inc(pad_zero, 1)
            pool.wait_ge(mix_left, N_TILES + KD)
            for m in range(KD):
                nc.gpsimd.memset(yacc[:, m, :], 0.0).then_inc(y_added, 1)

        @block.sync
        def _(sp):
            for j in range(KD):
                sp.dma_start(x_in[:, j, :], t["x"][0, j * P:(j + 1) * P, :]).then_inc(x_loaded, 16)
            rows = 0
            for src in [t[name] for name in NORMS] + [t["mlstm_norm"], t["conv_b"], t["conv_w"]]:
                src = src.rearrange("a (k p) -> (a k) p", p=P) if len(src.shape) == 2 else \
                    src.rearrange("a c (k p) -> (a c k) p", p=P)
                sp.dma_start(vec_rows[rows:rows + src.shape[0], :], src).then_inc(vecs_loaded, 16)
                rows += src.shape[0]
            sp.dma_start(sinks[:, :], t["attn_sink"].to_broadcast([P, AH])).then_inc(small_loaded, 16)
            sp.wait_ge(bias_zero, 1)
            by_head = t["b_gates"].rearrange("a (w g h) -> w (a h) g", w=2, g=2)
            for way in range(2):
                sp.dma_start(gate_bias[32 * way:32 * way + MH, :], by_head[way],
                             allow_slow_non_contiguous=True).then_inc(small_loaded, 16)
            ffn_sp(sp, 0, 0, "ffn1_w1", "ffn1_w2")
            mix_sp(sp, B_MIX)
            branch_sp(sp, B_MIX)
            ffn_sp(sp, 1, B_FFN2, "ffn2_w1", "ffn2_w2")
            ple_sp(sp, B_PLE)
            for j in range(KD):
                sp.wait_ge(out_copied, j + 1)
                sp.dma_start(out[0, j * P:(j + 1) * P, :], x_out[:, j, :]).then_inc(stored, 16)
            sp.wait_ge(stored, 16 * KD)

        @block.scalar
        def _(act):
            for k in range(0, KD, 2):
                act.wait_ge(x_turned, k + 1)
                if k:
                    act.wait_ge(x_kept, k)
                nc.scalar.copy(resid[:, k, :], ps[k % 4][:, :]).then_inc(x_kept, 1)
            norm_act(act, 0, resid)
            pre_act(act, 0)
            ffn_act(act, 0, 0)
            act.wait_ge(raw_q[0], 16)
            split_hi(act, Count(B_MIX), 0)
            norm_act(act, 1, yacc)
            act.wait_ge(raw_q[1], 16)
            split_hi(act, Count(B_MIX), 1)
            norm_act(act, 2, resid)
            pre_act(act, 2)
            mix_act(act, B_MIX)
            mlstm_act(act)
            branch_act(act, B_MIX)
            norm_act(act, 3, mix_y)
            norm_act(act, 4, resid)
            pre_act(act, 4)
            ffn_act(act, 1, B_FFN2)
            norm_act(act, 5, yacc)
            norm_act(act, 6, resid)
            pre_act(act, 6)
            ple_act(act, B_PLE)
            norm_act(act, 7, yacc)

        @block.vector
        def _(dve):
            for k in range(1, KD, 2):
                dve.wait_ge(x_turned, k + 1)
                dve.wait_ge(x_kept, k)
                nc.vector.tensor_copy(resid[:, k, :], ps[k % 4][:, :]).then_inc(x_kept, 1)
            dve.wait_ge(consts_ready, 2)
            dve.wait_ge(vecs_turned, 1)
            nc.vector.tensor_copy(vecs[:, :], ps[0][:, 0:VEC_ROWS]).then_inc(vecs_ready, 1)
            dve.wait_ge(vecs_ready, 1)
            for n in (1, 5):
                nc.vector.tensor_scalar(gains[:, n, :], gains[:, n, :], 0.5, None, ALU.mult).then_inc(gains_halved, 1)
            norm_dve(dve, 0, resid)
            pre_dve(dve, 0)
            ffn_dve(dve, 0, 0)
            split_lo(dve, Count(B_MIX), 0)
            norm_dve(dve, 1, yacc)
            split_lo(dve, Count(B_MIX), 1)
            dve.wait_ge(gains_halved, 2)
            post_dve(dve, 1, yacc)
            norm_dve(dve, 2, resid)
            pre_dve(dve, 2)
            mix_dve(dve, B_MIX)
            mlstm_dve(dve)
            branch_dve(dve, B_MIX)
            norm_dve(dve, 3, mix_y)
            dve.wait_ge(resid_back, 16 * KD)
            post_dve(dve, 3, mix_y)
            norm_dve(dve, 4, resid)
            pre_dve(dve, 4)
            ffn_dve(dve, 1, B_FFN2)
            norm_dve(dve, 5, yacc)
            post_dve(dve, 5, yacc)
            norm_dve(dve, 6, resid)
            pre_dve(dve, 6)
            ple_dve(dve, B_PLE)
            norm_dve(dve, 7, yacc)
            post_dve(dve, 7, yacc)
            for j in range(KD):
                dve.wait_ge(out_turned, j + 1)
                nc.vector.tensor_copy(x_out[:, j, :], ps[j % 4][:, :]).then_inc(out_copied, 1)

        @block.tensor
        def _(pe):
            pe.wait_ge(consts_ready, 2)
            pe.wait_ge(x_loaded, 16 * KD)
            for k in range(KD):
                if k >= 4:
                    pe.wait_ge(x_kept, k - 3)
                for j in range(KD):
                    mm = nc.tensor.transpose(ps[k % 4][:, j * P:(j + 1) * P], x_in[:, j, k * P:(k + 1) * P],
                                             ident[:, :])
                mm.then_inc(x_turned, 1)
            pe.wait_ge(vecs_loaded, 16 * 11)
            pe.wait_ge(x_kept, 5)
            nc.tensor.transpose(ps[0][:, 0:VEC_ROWS], vec_rows[:, :], ident[0:VEC_ROWS, 0:VEC_ROWS]).then_inc(vecs_turned, 1)
            pe.wait_ge(x_kept, KD)
            norm_pe(pe, 0)
            ffn_pe(pe, 0, 0, 0)
            norm_pe(pe, 1, new_block=True)
            norm_pe(pe, 2)
            mix_pe(pe, B_MIX, 1)
            mlstm_pe(pe)
            branch_pe(pe, B_MIX)
            pe.wait_ge(mix_left, N_TILES + KD)
            norm_pe(pe, 3, new_block=True)
            norm_pe(pe, 4)
            ffn_pe(pe, 1, B_FFN2, 2)
            norm_pe(pe, 5)
            norm_pe(pe, 6)
            ple_pe(pe, B_PLE)
            pe.wait_ge(prod_done, PAIRS + KD)
            norm_pe(pe, 7)
            pe.wait_ge(resid_ready, 4 * KD)
            for j in range(KD):
                if j >= 4:
                    pe.wait_ge(out_copied, j - 3)
                for k in range(KD):
                    mm = nc.tensor.transpose(ps[j % 4][:, k * P:(k + 1) * P], resid[:, k, j * P:(j + 1) * P],
                                             ident[:, :])
                mm.then_inc(out_turned, 1)


def tables():
    import numpy as np

    f = np.float32
    p, c = np.arange(P)[:, None], np.arange(P)[None, :]
    made = {"ident": p == c}
    d = np.arange(P) % AD
    partner = np.where(d < ROPE // 2, np.arange(P) + ROPE // 2, np.arange(P) - ROPE // 2)
    partner = np.where(d < ROPE, partner, np.arange(P))
    made["perm"] = p == partner[None, :]
    key = np.arange(WINDOW)[None, :] - P
    made["window"] = np.where(np.abs(key - p) <= P, 0, -BLOCKED)
    made["later"] = np.where(p <= c, 0, BLOCKED)
    made["earlier"] = np.where(p >= c, 0, BLOCKED)
    chains = np.zeros((P, 2, MH, P))
    for way in range(2):
        for h in range(MH):
            chains[32 * way + h, way, h] = 1
    made["chains"] = chains.reshape(P, -1)
    inv = f(THETA) ** (-np.arange(0, ROPE, 2, dtype=f) / f(ROPE))
    angle = (np.arange(S, dtype=f)[:, None] * inv[None, :]).astype(f)
    cos, sin = np.ones((P, S)), np.zeros((P, S))
    for n in range(P):
        if n % AD < ROPE:
            cos[n] = np.cos(angle[:, n % AD % (ROPE // 2)])
            sin[n] = np.sin(angle[:, n % AD % (ROPE // 2)]) * (-1 if n % AD < ROPE // 2 else 1)
    made["cos"], made["sin"] = cos, sin
    token = np.arange(S)[None, :] % P
    made["inside"] = np.where(p < 32, token != 0, token != P - 1)
    return {"tables": np.concatenate([np.broadcast_to(made[n], (P, w)).astype(f) for n, (_, w) in TABLE.items()], 1)}


_INS = ['x', 'p', 'ffn1_norm_pre', 'ffn1_w1', 'ffn1_w2', 'ffn1_norm_post', 'mix_norm_pre', 'w_in', 'b_gates',
        'conv_w', 'conv_b', 'attn_sink', 'mlstm_norm', 'w_branch_attn', 'w_branch_mlstm', 'w_out', 'mix_norm_post',
        'ffn2_norm_pre', 'ffn2_w1', 'ffn2_w2', 'ffn2_norm_post', 'ple_norm_pre', 'w_ple_gate', 'w_ple_proj',
        'ple_norm_post']


def kernel(**inputs):
    import numpy as np
    import concourse.bacc as bacc
    from concourse.bass_utils import run_bass_kernel_spmd

    nc = bacc.Bacc("TRN2", target_bir_lowering=False, num_devices=1)
    arrays, args = {}, {}
    for name in _INS:
        arrays[name] = np.ascontiguousarray(inputs[name])
        args[name] = nc.dram_tensor(name, arrays[name].shape, F32, kind="ExternalInput").ap()
    for name, array in tables().items():
        arrays[name] = array
        args[name] = nc.dram_tensor(name, array.shape, F32, kind="ExternalInput").ap()
    out = nc.dram_tensor("out", (1, S, D), F32, kind="ExternalOutput").ap()
    build(nc, args, out)
    r = run_bass_kernel_spmd(nc, [arrays], core_ids=[0])
    return r.results[0]["out"]
```

```python
from contextlib import ExitStack

import concourse.bass as bass
from concourse import mybir
from concourse.alu_op_type import AluOpType as ALU

F32 = mybir.dt.float32
F32R = mybir.dt.float32r
ACT = mybir.ActivationFunctionType

P = 128
D = 1024
S = 1024
KD = D // P
HALF = 512
FFN = 2816
GROUP = 2
GROUPS = FFN // (GROUP * P)
EPS = 1e-6
NB = S // P

AH, AKV, AD = 8, 2, 64
ATT_SCALE = AD ** -0.5
WINDOW = 3 * P
ROPE = AD // 4
THETA = 500000.0
BLOCKED = 1e30

MH, MD, MV = 4, 128, 256
TAPS = 5
PLE = 256
CHAIN_ROWS = 64
K_SCALE = MD ** -0.5

C_AQ = 0
C_AK = C_AQ + AH * AD
C_AV = C_AK + AKV * AD
C_MQK = C_AV + AKV * AD
C_MV = C_MQK + 2 * MH * MD
C_MO = C_MV + MH * MV
C_MG = C_MO + MH * MV
C_BG = C_MG + 4 * MH

TABLE = {}
for _name, _width in (("ident", P), ("perm", P), ("window", WINDOW), ("later", P), ("earlier", P),
                      ("chains", 2 * MH * P), ("cos", S), ("sin", S), ("inside", S)):
    TABLE[_name] = (sum(w for _, w in TABLE.values()), _width)
TABLE_WIDTH = sum(w for _, w in TABLE.values())

N_QKV = 6
T_MQK = N_QKV
T_MV = T_MQK + KD
T_SIG = T_MV + KD
T_MG = T_SIG + 2 * KD
T_GM = T_MG + 1
N_TILES = T_GM + KD
KB = 1024
RING = 2
VEC_ROWS = 120
NORMS = ['ffn1_norm_pre', 'ffn1_norm_post', 'mix_norm_pre', 'mix_norm_post', 'ffn2_norm_pre', 'ffn2_norm_post',
         'ple_norm_pre', 'ple_norm_post']


class Count:

    def __init__(self, base, per=0, turn=None):
        self.base, self.per, self.turn = base, per, turn

    def n(self, k=0):
        return self.base + k if self.turn is None else self.turn * self.per + (self.base + k)

    def slot(self, k=0):
        return (self.base + k) % RING

    def uses(self, k=0):
        first = (self.base + k) // RING + 1
        return first if self.turn is None else self.turn * (self.per // RING) + first


def build(nc, t, out):
    with ExitStack() as ctx:
        base = (nc.sbuf_base + 63) // 64 * 64

        def at(name, kb, shape, dt=F32):
            return nc.alloc_sbuf_tensor_at(name, shape, dt, offset=base + int(kb * KB))

        def sem(name):
            return ctx.enter_context(nc.semaphore(name))

        resid = at("resid", 0, [P, KD, S])
        u_hi = at("u_hi", 32, [P, KD, S], F32R)
        u_lo = at("u_lo", 64, [P, KD, S], F32R)
        w_raw = at("w_raw", 96, [P, RING, 1024])
        w_hi = at("w_hi", 104, [P, RING, 1024], F32R)
        w_lo = at("w_lo", 112, [P, RING, 1024], F32R)
        tmp = at("tmp", 120, [P, 2, S])
        ident = at("ident", 132.25, [P, P])
        band = at("band", 132.75, [P, 2 * NB - 1])
        eps = at("eps", 132.875, [P, 1])
        vec_rows = at("vec_rows", 133.75, [VEC_ROWS, P])
        vecs = at("vecs", 134.25, [P, VEC_ROWS])
        gains = vecs[:, 0:8 * KD].rearrange("p (n k) -> p n k", n=8)
        rinv = at("rinv", 133.25, [NB, P])
        yacc = at("yacc", 142, [P, KD, S])
        hid_hi = at("hid_hi", 174, [P, 2, GROUP, S], F32R)
        hid_lo = at("hid_lo", 190, [P, 2, GROUP, S], F32R)
        sq = at("sq", 174, [P, KD, S])
        x_in = at("x_in", 142, [P, KD, D])
        x_out = at("x_out", 174, [P, KD, D])

        ps = [ctx.enter_context(nc.psum_tensor(f"acc{n}", [P, S], F32)) for n in range(4)]

        x_loaded = sem("x_loaded")
        consts_ready = sem("consts_ready")
        ident_zero = sem("ident_zero")
        vecs_loaded = sem("vecs_loaded")
        vecs_turned = sem("vecs_turned")
        vecs_ready = sem("vecs_ready")
        gains_halved = sem("gains_halved")
        x_turned = sem("x_turned")
        x_kept = sem("x_kept")
        raw_loaded = [sem(f"raw_loaded{n}") for n in range(RING)]
        whi_ready = sem("whi_ready")
        wlo_ready = sem("wlo_ready")
        block_used = sem("block_used")
        gateup_done = sem("gateup_done")
        silu_done = sem("silu_done")
        prod_done = sem("prod_done")
        hhi_ready = sem("hhi_ready")
        hid_ready = sem("hid_ready")
        y_done = sem("y_done")
        y_added = sem("y_added")
        sq_ready = sem("sq_ready")
        sq_pair = sem("sq_pair")
        sum_done = sem("sum_done")
        root_ready = sem("root_ready")
        rinv_ready = sem("rinv_ready")
        spread_done = sem("spread_done")
        u_made = sem("u_made")
        uhi_ready = sem("uhi_ready")
        ulo_ready = sem("ulo_ready")
        post_made = sem("post_made")
        resid_dve = sem("resid_dve")
        resid_pool = sem("resid_pool")
        out_turned = sem("out_turned")
        out_copied = sem("out_copied")
        stored = sem("stored")

        def w1_block(name, cols):
            return t[name][0, :, cols].rearrange("(k p) n -> p k n", p=P)

        def w2_block(name, rows, half):
            return t[name][0, rows, half * 512:half * 512 + 512].rearrange("(k p) n -> p k n", p=P)

        def load(sp, c, k, src):
            if c.base + k >= RING:
                sp.wait_ge(wlo_ready, c.n(k - RING + 1))
            s = c.slot(k)
            nk = src.shape[1]
            sp.dma_start(w_raw[:, s, :].rearrange("p (k n) -> p k n", k=nk), src).then_inc(raw_loaded[s], 16)

        def split_hi(act, c, k, width=1024):
            act.wait_ge(raw_loaded[c.slot(k)], c.uses(k) * 16)
            if c.base + k >= RING:
                act.wait_ge(block_used, c.n(k - RING + 1))
            nc.scalar.activation(w_hi[:, c.slot(k), 0:width], w_raw[:, c.slot(k), 0:width], ACT.Copy).then_inc(whi_ready, 1)

        def split_lo(dve, c, k, width=1024):
            s = c.slot(k)
            dve.wait_ge(whi_ready, c.n(k + 1))
            nc.vector.tensor_tensor(w_lo[:, s, 0:width], w_raw[:, s, 0:width], w_hi[:, s, 0:width].bitcast(F32),
                                    ALU.subtract).then_inc(wlo_ready, 1)

        def product(acc, terms, first=True, last=True, new_block=False):
            for n, (s, off, a_hi, a_lo) in enumerate(terms):
                hi, lo = w_hi[:, s, off:off + P], w_lo[:, s, off:off + P]
                for h in range(2):
                    cols = slice(h * HALF, (h + 1) * HALF)
                    mm = nc.tensor.matmul(acc[:, cols], hi, a_hi[:, cols], start=(first and n == 0), stop=False)
                    if new_block and n == 0 and h == 0:
                        mm.then_inc(block_used, 1)
                    nc.tensor.matmul(acc[:, cols], hi, a_lo[:, cols], start=False, stop=False)
                    mm = nc.tensor.matmul(acc[:, cols], lo, a_hi[:, cols], start=False,
                                          stop=(last and n == len(terms) - 1))
            return mm

        def first_pair(pe, c, pre, done):
            for k in range(KD):
                pe.wait_ge(ulo_ready, KD * pre + k + 1)
                for j in range(2):
                    if k == 0:
                        pe.wait_ge(wlo_ready, c.n(j + 1))
                    mm = product(ps[j], [(c.slot(j), k * P, u_hi[:, k, :], u_lo[:, k, :])], first=(k == 0),
                                 last=(k == KD - 1), new_block=(j == 1 and k == KD - 1))
                    if k == KD - 1:
                        mm.then_inc(done, 1)

        PAIRED = 3

        def resid_wait(eng, post, k):
            eng.wait_ge(resid_dve if k % 2 else resid_pool, KD // 2 * post + k // 2 + 1)

        def norm_src_wait(eng, n, k):
            if n == 0:
                eng.wait_ge(x_kept, k + 1)
            elif n % 2 == 0:
                resid_wait(eng, n // 2 - 1, k)
            elif n == 3:
                eng.wait_ge(mix_left, N_TILES + k + 1)
            elif n == 7:
                eng.wait_ge(prod_done, 2 * GROUPS * GROUP + min(k + 1 + k // 6, KD))
            else:
                eng.wait_ge(y_added, KD * (GROUPS + 1) * (n // 4 + 1) - KD + min(k + 1 + k // 6, KD))

        def sums(n):
            return (ps[0] if n == 7 else ps[2])[0:NB, 0:P]

        RINV = ps[3]

        def place(n, k):
            return [2, 3, 6, 7, 3, 7, 0, 1][k] if n % 2 else k

        def square_act(act, n, src):
            for k in range(KD):
                norm_src_wait(act, n, k)
                if n % 2 and k in (4, 5):
                    act.wait_ge(sq_pair, PAIRED * (n // 2) + k - 3)
                nc.scalar.activation(sq[:, place(n, k), :], src[:, k, :], ACT.Square).then_inc(sq_ready, 1)

        def pair_pool(pool, n):
            for i in range(PAIRED):
                pool.wait_ge(sq_ready, KD * n + 2 * i + 2)
                a, b = place(n, 2 * i), place(n, 2 * i + 1)
                nc.gpsimd.tensor_tensor(sq[:, a, :], sq[:, a, :], sq[:, b, :], ALU.add).then_inc(sq_pair, 1)

        def norm_pe(pe, n, new_block=False):
            tiles = [0, 2, 4, 6, 7] if n % 2 else range(KD)
            for k in tiles:
                if n % 2 and k < 2 * PAIRED:
                    pe.wait_ge(sq_pair, PAIRED * (n // 2) + k // 2 + 1)
                else:
                    pe.wait_ge(sq_ready, KD * n + k + 1)
                for j in range(NB):
                    mm = nc.tensor.matmul(sums(n), band[:, NB - 1 - j:2 * NB - 1 - j],
                                          sq[:, place(n, k), j * P:(j + 1) * P], start=(k == 0 and j == 0),
                                          stop=(k == KD - 1 and j == NB - 1))
                    if new_block and k == 0 and j == 0:
                        mm.then_inc(block_used, 1)
            mm.then_inc(sum_done, 1)
            pe.wait_ge(rinv_ready, n + 1)
            for j in range(NB):
                mm = nc.tensor.matmul(RINV[:, j * P:(j + 1) * P], ident[0:NB, j:j + 1].to_broadcast([NB, P]),
                                      rinv[:, :], start=True, stop=True)
            mm.then_inc(spread_done, 1)

        def root_act(act, n):
            act.wait_ge(sum_done, n + 1)
            nc.scalar.activation(rinv[:, :], sums(n), ACT.Sqrt, bias=eps[0:NB, :], scale=1.0 / D
                                 ).then_inc(root_ready, 1)

        def inverse_dve(dve, n):
            dve.wait_ge(root_ready, n + 1)
            nc.vector.reciprocal(rinv[:, :], rinv[:, :]).then_inc(rinv_ready, 1)
            dve.wait_ge(spread_done, n + 1)

        def pre_dve(dve, n):
            pre = n // 2
            inverse_dve(dve, n)
            for k in range(KD):
                if KD * pre + k >= 2:
                    dve.wait_ge(ulo_ready, KD * pre + k - 1)
                nc.vector.scalar_tensor_tensor(out=tmp[:, k % 2, :], in0=resid[:, k, :], scalar=gains[:, n, k:k + 1],
                                               in1=RINV[:, :], op0=ALU.mult, op1=ALU.mult).then_inc(u_made, 1)
                if k:
                    pre_lo(dve, pre, k - 1)
            pre_lo(dve, pre, KD - 1)

        def pre_lo(dve, pre, k):
            dve.wait_ge(uhi_ready, KD * pre + k + 1)
            nc.vector.tensor_tensor(u_lo[:, k, :], tmp[:, k % 2, :], u_hi[:, k, :].bitcast(F32),
                                    ALU.subtract).then_inc(ulo_ready, 1)

        def pre_act(act, n):
            pre = n // 2
            for k in range(KD):
                act.wait_ge(u_made, KD * pre + k + 1)
                nc.scalar.activation(u_hi[:, k, :], tmp[:, k % 2, :], ACT.Copy).then_inc(uhi_ready, 1)

        def post_dve(dve, n, y):
            post = n // 2
            inverse_dve(dve, n)
            for k in range(KD):
                nc.vector.scalar_tensor_tensor(out=y[:, k, :], in0=y[:, k, :], scalar=gains[:, n, k:k + 1],
                                               in1=RINV[:, :], op0=ALU.mult, op1=ALU.mult).then_inc(post_made, 1)
                if k and k % 2 == 0:
                    post_add(dve, nc.vector, post, k - 1, y, resid_dve)
            post_add(dve, nc.vector, post, KD - 1, y, resid_dve)

        def post_pool(pool, n, y):
            for k in range(0, KD, 2):
                post_add(pool, nc.gpsimd, n // 2, k, y, resid_pool)

        def post_add(eng, engine, post, k, y, done):
            eng.wait_ge(post_made, KD * post + k + 1)
            engine.tensor_tensor(resid[:, k, :], resid[:, k, :], y[:, k, :], ALU.add).then_inc(done, 1)

        BLOCKS_FFN = GROUPS * 6

        def ffn_sp(sp, f, b, w1, w2):
            def s1(c, k, col):
                for j in range(GROUP):
                    load(sp, c, k + 2 * j, w1_block(w1, bass.ds(col + j * P, P)))
                    load(sp, c, k + 2 * j + 1, w1_block(w1, bass.ds(col + FFN + j * P, P)))

            def s2(c, k, row):
                for h in range(2):
                    load(sp, c, k + h, w2_block(w2, bass.ds(row, GROUP * P), h))

            W = GROUP * P
            s1(Count(b), 0, 0)
            with sp.Fori(0, GROUPS // 2) as i:
                c = Count(b + 4, 12, i)
                s1(c, 0, i * (2 * W) + W)
                s2(c, 4, i * (2 * W))
                s1(c, 6, i * (2 * W) + 2 * W)
                s2(c, 10, i * (2 * W) + W)
            s2(Count(b + BLOCKS_FFN - 2), 0, (GROUPS - 1) * W)

        def ffn_act(act, f, b):
            def s1(c, g, k, first=False):
                if not first:
                    split_hi(act, c, k + 1)
                split_hi(act, c, k + 2)
                for j in range(GROUP):
                    act.wait_ge(gateup_done, g.n() * 4 + 2 * j + 1)
                    if g.base * GROUP + j >= 2:
                        act.wait_ge(hid_ready, g.n() * GROUP + j - 1)
                    nc.scalar.activation(tmp[:, j, :], ps[2 * j][:, :], ACT.Silu).then_inc(silu_done, 1)
                    split_hi(act, c, k + 3 + j)

            def s2(c, k, more=True):
                split_hi(act, c, k + 1)
                if more:
                    split_hi(act, c, k + 2)

            s1(Count(b), Count(f * GROUPS), 0, first=True)
            with act.Fori(0, GROUPS // 2) as i:
                c = Count(b + 4, 12, i)
                s1(c, Count(f * GROUPS + 1, 2, i), 0)
                s2(c, 4)
                s1(c, Count(f * GROUPS + 2, 2, i), 6)
                s2(c, 10)
            s2(Count(b + BLOCKS_FFN - 2), 0, more=False)

        def ffn_dve(dve, f, b):
            def hidden(g, j):
                dve.wait_ge(silu_done, g.n() * 2 + j + 1)
                dve.wait_ge(gateup_done, g.n() * 4 + 2 * j + 2)
                par = (g.base - f * GROUPS) % 2
                nc.vector.tensor_tensor(tmp[:, j, :], tmp[:, j, :], ps[2 * j + 1][:, :],
                                        ALU.mult).then_inc(prod_done, 1)
                dve.wait_ge(prod_done, g.n() * 2 + j + 1)
                nc.vector.tensor_copy(hid_hi[:, par, j, :], tmp[:, j, :]).then_inc(hhi_ready, 1)
                dve.wait_ge(hhi_ready, g.n() * 2 + j + 1)
                nc.vector.tensor_tensor(hid_lo[:, par, j, :], tmp[:, j, :], hid_hi[:, par, j, :].bitcast(F32),
                                        ALU.subtract).then_inc(hid_ready, 1)

            def add_y(g, m):
                dve.wait_ge(y_done, g.n() * KD + m + 1)
                dve.wait_ge(y_added, g.n() * KD + KD * f + m + 1)
                nc.vector.tensor_tensor(yacc[:, m, :], yacc[:, m, :], ps[m % 4][:, :], ALU.add).then_inc(y_added, 1)

            def s1(c, g, k, y=None, first=False):
                if not first:
                    split_lo(dve, c, k + 1)
                if y is not None:
                    add_y(y, KD - 1)
                split_lo(dve, c, k + 2)
                split_lo(dve, c, k + 3)
                hidden(g, 0)
                split_lo(dve, c, k + 4)

            def s2(c, g, y, k, more=True):
                split_lo(dve, c, k + 1)
                if g is not None:
                    hidden(g, 1)
                for m in range(3):
                    add_y(y, m)
                if more:
                    split_lo(dve, c, k + 2)
                for m in range(3, KD - 1):
                    add_y(y, m)

            G = f * GROUPS
            s1(Count(b), Count(G), 0, first=True)
            hidden(Count(G), 1)
            with dve.Fori(0, GROUPS // 2) as i:
                c = Count(b + 4, 12, i)
                s1(c, Count(G + 1, 2, i), 0)
                s2(c, Count(G + 1, 2, i), Count(G, 2, i), 4)
                s1(c, Count(G + 2, 2, i), 6, y=Count(G, 2, i))
                s2(c, Count(G + 2, 2, i), Count(G + 1, 2, i), 10)
                add_y(Count(G + 1, 2, i), KD - 1)
            s2(Count(b + BLOCKS_FFN - 2), None, Count(G + GROUPS - 1), 0, more=False)
            add_y(Count(G + GROUPS - 1), KD - 1)

        def ffn_pe(pe, f, b, pre):
            def s1(c, g, k, first=False):
                if first:
                    first_pair(pe, c, pre, gateup_done)
                for n in range(2 if first else 0, 4):
                    pe.wait_ge(wlo_ready, c.n(k + n + 1))
                    if not first:
                        pe.wait_ge(y_added, (g.n() - 1) * KD + KD * f + 4 + n + 1)
                    product(ps[n], [(c.slot(k + n), kk * P, u_hi[:, kk, :], u_lo[:, kk, :])
                                    for kk in range(KD)], new_block=True).then_inc(gateup_done, 1)

            def s2(c, g, k, last_s1):
                par = (g.base - f * GROUPS) % 2
                pe.wait_ge(hid_ready, g.n() * GROUP + GROUP)
                for m in range(KD):
                    h = m // 4
                    if m % 4 == 0:
                        pe.wait_ge(wlo_ready, c.n(k + h + 1))
                    if m < 4:
                        if last_s1 is not None:
                            if m % 2 == 0:
                                pe.wait_ge(silu_done, last_s1.n() * GROUP + m // 2 + 1)
                            else:
                                pe.wait_ge(prod_done, last_s1.n() * GROUP + m // 2 + 1)
                        else:
                            pe.wait_ge(y_added, g.n() * KD + KD * f + 4 + m + 1)
                    else:
                        pe.wait_ge(y_added, g.n() * KD + KD * (f + 1) + m - 4 + 1)
                    mm = product(ps[m % 4], [(c.slot(k + h), j * 512 + (m % 4) * P, hid_hi[:, par, j, :],
                                              hid_lo[:, par, j, :]) for j in range(GROUP)],
                                 new_block=(m % 4 == 0))
                    mm.then_inc(y_done, 1)

            G = f * GROUPS
            s1(Count(b), Count(G), 0, first=True)
            with pe.Fori(0, GROUPS // 2) as i:
                c = Count(b + 4, 12, i)
                s1(c, Count(G + 1, 2, i), 0)
                s2(c, Count(G, 2, i), 4, Count(G + 1, 2, i))
                s1(c, Count(G + 2, 2, i), 6)
                s2(c, Count(G + 1, 2, i), 10, Count(G + 2, 2, i))
            s2(Count(b + BLOCKS_FFN - 2), Count(G + GROUPS - 1), 0, None)

        mqk = at("mqk", 0, [P, 2 * MH, S])
        zpad = at("zpad", 120, [P, 2, S + TAPS - 1])
        rope_t = at("rope_t", 128.25, [P, S])
        att_q = at("att_q", 142, [P, AH // 2, S])
        att_k = at("att_k", 158, [P, S])
        att_v = at("att_v", 162, [P, NB, P])
        cos_sb = at("cos_sb", 166, [P, S])
        sin_sb = at("sin_sb", 170, [P, S])
        m_v = at("m_v", 166, [P, NB, MH, MV + 1])
        q_st = at("q_st", 136, [P, 2, AH // 2, P])
        window = at("window", 140, [P, WINDOW])
        perm = at("perm", 141.5, [P, P])
        prob = at("prob", 199, [P, 2, WINDOW])
        prob_t = at("prob_t", 202, [P, 2, WINDOW])
        o_sb = at("o_sb", 205, [P, AH * AD])
        sinks = at("sinks", 134.75, [P, AH])
        att = at("att", 134.8125, [P, 8, AH])
        A_MAX, A_NEG, A_SUM, A_SINK, A_ESINK, A_DEN, A_REC, neg_sinks = (att[:, n, :] for n in range(8))
        tick = at("tick", 135.8125, [P, 1])
        gate_bias = at("gate_bias", 135.0625, [CHAIN_ROWS, 2])
        m_cols = at("m_cols", 135.125, [P, 3, NB * MH])
        chunk_rows = at("chunk_rows", 135.5, [CHAIN_ROWS, 2, NB])

        r_li = at("r_li", 199, [CHAIN_ROWS, S])
        r_lf = at("r_lf", 162, [CHAIN_ROWS, S])
        r_b = at("r_b", 158, [CHAIN_ROWS, S])
        r_m = at("r_m", 203, [CHAIN_ROWS, S])
        r_in = at("r_in", 136, [CHAIN_ROWS, S])
        r_g, r_wi, r_r, r_em, r_wk = r_li, r_lf, r_b, r_m, r_in

        col = at("col", 32, [P, NB, 3, CHAIN_ROWS])
        state = at("state", 39.5, [P, 2, 2, MV + 1])
        h_s = [at("h_s0", 47.75, [P, 2, NB, P]), at("h_s1", 96, [P, 2, NB, P])]
        h_q = [at("h_q0", 55.75, [P, 2, NB, P]), at("h_q1", 104, [P, 2, NB, P])]
        h_kw = [at("h_kw0", 120, [P, 2, NB, P]), at("h_kw1", 112, [P, 2, NB, P])]
        h_dec = at("h_dec", 38.25, [P, 2, 2, NB])
        h_den = at("h_den", 38.4375, [P, 2, 2])
        h_arg = at("h_arg", 128.25, [P, NB, P])
        h_junk = at("h_junk", 136, [P, 4, MV])
        hm = at("hm", 64, [P, NB, MH, MV])
        chains = at("chains", 199, [CHAIN_ROWS, 2, MH, P])
        order = at("order", 203, [P, 2, P])

        hm_hi = at("hm_hi", 0, [P, KD, S], F32R)
        hm_lo = at("hm_lo", 32, [P, KD, S], F32R)
        o_hi = at("o_hi", 167, [P, AH // 2, S], F32R)
        o_lo = at("o_lo", 183, [P, AH // 2, S], F32R)
        mg_hi = at("mg_hi", 64, [P, KD, S], F32R)
        mg_lo = at("mg_lo", 135, [P, KD, S], F32R)
        p_in = at("p_in", 182, [P, NB, PLE])
        p_hi = at("p_hi", 174, [P, PLE // P, S], F32R)
        p_lo = at("p_lo", 190, [P, PLE // P, S], F32R)
        sig_in = at("sig_in", 199, [P, 2, S])
        mix_y = at("mix_y", 32, [P, KD, S])

        sig_dram = nc.dram_tensor("sig_dram", (3 * KD, P, S), F32, kind="Internal").ap()
        resid_dram = nc.dram_tensor("resid_dram", (KD, P, S), F32, kind="Internal").ap()

        (spilled, tables_loaded, rot_done, rope_cos, rope_sin, rope_done, vt_done, vt_left, mix_done, mix_left,
         pad_zero, conv_step, conv_done, mqk_ready, ones_v, small_loaded) = (sem(x) for x in (
            "spilled", "tables_loaded", "rot_done", "rope_cos", "rope_sin", "rope_done", "vt_done", "vt_left",
            "mix_done", "mix_left", "pad_zero", "conv_step", "conv_done", "mqk_ready", "ones_v",
            "small_loaded"))
        (qst_ready, score_done, max_done, neg_ready, prob_ready, pt_done, pt_left, pv_done, sink_arg, sink_exp,
         den_ready, rec_ready, osb_ready, ot_done, ot_left, qst_zero, sinks_ready) = (sem(x) for x in (
            "qst_ready", "score_done", "max_done", "neg_ready", "prob_ready", "pt_done", "pt_left", "pv_done",
            "sink_arg", "sink_exp", "den_ready", "rec_ready", "osb_ready", "ot_done", "ot_left", "qst_zero", "sinks_ready"))
        raw_q = [sem(f"raw_q{n}") for n in range(RING)]
        sig_stored = [sem(f"sig_stored{n}") for n in range(2)]
        row_act, row_dve, wz = (sem(x) for x in ("row_act", "row_dve", "wz"))

        W_IN = t["w_in"][0]

        def copy(dst, src, scale=1.0):
            return nc.vector.tensor_scalar(dst, src, scale, None, ALU.mult)

        def in_block(first):
            return W_IN[:, bass.ds(first, P)].rearrange("(k p) n -> p k n", p=P)

        def table(name, rows=P):
            first, width = TABLE[name]
            return t["tables"][0:rows, first:first + width]

        def sig_tile(n):
            return sig_dram[bass.ds(n, 1)].rearrange("a p n -> (a p) n")

        def mix_sp(sp, b):
            c = Count(b)
            wq = W_IN[:, C_AQ:C_AQ + AH * AD].rearrange("(k p) (g i d) -> i p k g d", p=P, g=2, d=AD)

            for k in range(AH // 2):
                load_q2(sp, c, k, wq)
                if k == 1:
                    for m in range(KD):
                        resid_wait(sp, 0, m)
                        sp.dma_start(resid_dram[m], resid[:, m, :]).then_inc(spilled, 16)
                    sp.dma_start(cos_sb[:, :], table("cos")).then_inc(tables_loaded, 16)
                    sp.dma_start(sin_sb[:, :], table("sin")).then_inc(tables_loaded, 16)
                    sp.dma_start(perm[:, :], table("perm")).then_inc(tables_loaded, 16)
                    sp.dma_start(window[:, :], table("window")).then_inc(tables_loaded, 16)
            load(sp, c, 4, in_block(C_AK))
            load(sp, c, 5, in_block(C_AV))
            with sp.Fori(0, KD // 2) as i:
                c = Count(b + T_MQK, 2, i)
                for k in range(2):
                    load(sp, c, k, in_block(i * (2 * P) + (C_MQK + k * P)))
            with sp.Fori(0, KD // 2) as i:
                c = Count(b + T_MV, 2, i)
                for k in range(2):
                    load(sp, c, k, in_block(i * (2 * P) + (C_MV + k * P)))

            def store_sig(c, k, tile):
                sp.wait_ge(mix_left, c.n(k + 1))
                s = c.slot(k)
                sp.dma_start(sig_tile(tile), tmp[:, s, :]).then_inc(sig_stored[s], 16)

            c = Count(b + T_SIG)
            load(sp, c, 0, in_block(C_MO))
            load(sp, c, 1, in_block(C_BG))
            ct = Count(T_SIG)
            with sp.Fori(0, KD - 1) as i:
                c, ct = Count(b + T_SIG + 2, 2, i), Count(T_SIG, 2, i)
                load(sp, c, 0, in_block(i * P + (C_MO + P)))
                store_sig(ct, 0, i)
                load(sp, c, 1, in_block(i * P + (C_BG + P)))
                store_sig(ct, 1, i + KD)
            c, ct = Count(b + T_MG), Count(T_SIG + 2 * KD - 2)
            load_gates(sp, c)
            store_sig(ct, 0, KD - 1)
            load(sp, Count(b + T_GM), 0, in_block(C_BG + D))
            store_sig(ct, 1, 2 * KD - 1)
            sp.wait_ge(score_done, AH * NB)
            sp.dma_start(r_in[:, :], table("inside", CHAIN_ROWS)).then_inc(tables_loaded, 16)
            load(sp, Count(b + T_GM), 1, in_block(C_BG + D + P))
            for k in range(KD):
                if k + 2 < KD:
                    load(sp, Count(b + T_GM), k + 2, in_block(C_BG + D + (k + 2) * P))
                store_sig(Count(T_GM), k, 2 * KD + k)

        def load_q2(sp, c, k, wq):
            if c.base + k >= RING:
                sp.wait_ge(wlo_ready, c.n(k - RING + 1))
            s = c.slot(k)
            both = w_raw[:, s, :].rearrange("p (k g d) -> p k g d", k=KD, g=2)
            sp.dma_start(both[:, :, 0, :], wq[k][:, :, 0, :]).then_inc(raw_q[s], 16)
            sp.dma_start(both[:, :, 1, :], wq[k][:, :, 1, :]).then_inc(raw_loaded[s], 16)

        def load_gates(sp, c):
            sp.wait_ge(wlo_ready, c.n(-RING + 1))
            s = c.slot(0)
            sp.dma_start(w_raw[:, s, 0:KD * 4 * MH].rearrange("p (k n) -> p k n", k=KD),
                         W_IN[:, C_MG:C_MG + 4 * MH].rearrange("(k p) n -> p k n", p=P)).then_inc(raw_loaded[s], 16)

        def mix_product(pe, ct, cb, k, pieces=range(KD)):
            acc = ps[ct.slot(k)]
            if pieces[0] == 0:
                pe.wait_ge(wlo_ready, cb.n(k + 1))
                if ct.base + k >= 2:
                    pe.wait_ge(mix_left, ct.n(k - 1))
            for kk in pieces:
                mm = product(acc, [(cb.slot(k), kk * P, u_hi[:, kk, :], u_lo[:, kk, :])], first=(kk == 0),
                             last=(kk == KD - 1), new_block=(kk == 0))
            if pieces[-1] == KD - 1:
                mm.then_inc(mix_done, 1)

        def rotate(pe, k):
            pe.wait_ge(mix_left, k + 1)
            if k:
                pe.wait_ge(rope_sin, k)
            else:
                pe.wait_ge(tables_loaded, 64)
            for h in range(2):
                cols = slice(h * HALF, (h + 1) * HALF)
                mm = nc.tensor.matmul(ps[2][:, cols], perm[:, :], tmp[:, k % 2, cols], start=True, stop=True)
            mm.then_inc(rot_done, 1)

        def turn_values(pe, ct, cv, k):
            pe.wait_ge(mix_left, ct.n(k + 1))
            if cv.base + k >= 1:
                pe.wait_ge(vt_left, cv.n(k))
            for n in range(NB):
                mm = nc.tensor.transpose(ps[3][:, n * P:(n + 1) * P], tmp[:, ct.slot(k), n * P:(n + 1) * P],
                                         ident[:, :])
            mm.then_inc(vt_done, 1)

        def heads():
            return [(j, j // 2, j % 2, j // 2 + AH // 2 * (j % 2)) for j in range(AH)]

        def att_window(n, edge):
            if edge == 0:
                return 0, 2, P
            if edge == 2:
                return (NB - 2) * P, 2, 0
            return n * P - P, 3, 0

        def score_bank(j):
            return ps[2][:, (j % 2) * HALF:(j % 2) * HALF + WINDOW]

        PT = ps[3][:, 0:WINDOW]
        OT = ps[3][:, 0:HALF]
        OA = ps[3][:, HALF:2 * HALF]

        def att_pe(pe, n, edge, cu, ct, cb):
            key0, blocks, _ = att_window(n, edge)
            width = blocks * P

            def score(j, i, g, head):
                if j == 0:
                    pe.wait_ge(qst_ready, n + 1)
                if cu.base + j >= 2:
                    pe.wait_ge(max_done, cu.n(j - 1))
                nc.tensor.matmul(score_bank(j)[:, 0:width], q_st[:, g, i, :], att_k[:, bass.ds(key0, width)],
                                 start=True, stop=True).then_inc(score_done, 1)

            def turn(j, i, g, head):
                pe.wait_ge(prob_ready, cu.n(j + 1))
                if j or cu.base:
                    pe.wait_ge(pt_left, cu.n(j))
                if j == 0 and cu.base:
                    pe.wait_ge(ot_left, n)
                for w in range(blocks):
                    mm = nc.tensor.transpose(PT[:, w * P:(w + 1) * P], prob[:, j % 2, w * P:(w + 1) * P],
                                             ident[:, :])
                mm.then_inc(pt_done, 1)

            def weigh(j, i, g, head):
                pe.wait_ge(pt_left, cu.n(j + 1))
                if j == 0 and cu.base:
                    pe.wait_ge(osb_ready, n)
                for w in range(blocks):
                    block_n = (key0 // P + w) if edge != 1 else n + (w - 1)
                    mm = nc.tensor.matmul(OA[:, head * AD:(head + 1) * AD], prob_t[:, j % 2, w * P:(w + 1) * P],
                                          att_v[:, bass.ds(block_n, 1), g * AD:(g + 1) * AD].rearrange(
                                              "p a d -> p (a d)"),
                                          start=(w == 0), stop=(w == blocks - 1))
                mm.then_inc(pv_done, 1)

            pieces = [(k, kk) for k in range(2) for kk in range(KD)]
            H = heads()
            for step in range(12):
                for _ in range(2 if step < 4 else 1):
                    k, kk = pieces.pop(0)
                    mix_product(pe, ct, cb, k, [kk])
                if step < AH:
                    score(*H[step])
                if 1 <= step <= AH:
                    turn(*H[step - 1])
                if 2 <= step <= AH + 1:
                    weigh(*H[step - 2])
            pe.wait_ge(osb_ready, n + 1)
            for kt in range(AH // 2):
                mm = nc.tensor.transpose(OT[:, kt * P:(kt + 1) * P], o_sb[:, kt * P:(kt + 1) * P], ident[:, :])
            mm.then_inc(ot_done, 1)

        def mix_pe(pe, b, pre):
            cb, ct = Count(b), Count(0)
            first_pair(pe, cb, pre, mix_done)
            rotate(pe, 0)
            for k in range(2, N_QKV):
                mix_product(pe, ct, cb, k)
                rotate(pe, k - 1)
            turn_values(pe, Count(N_QKV - 1), Count(0), 0)
            with pe.Fori(0, KD // 2) as i:
                cb, ct = Count(b + T_MQK, 2, i), Count(T_MQK, 2, i)
                mix_product(pe, ct, cb, 0)
                mix_product(pe, ct, cb, 1)
            with pe.Fori(0, KD // 4) as i:
                cb, ct, cv = Count(b + T_MV, 4, i), Count(T_MV, 4, i), Count(1, 4, i)
                mix_product(pe, ct, cb, 0)
                for k in range(1, 4):
                    mix_product(pe, ct, cb, k)
                    turn_values(pe, ct, cv, k - 1)
                turn_values(pe, ct, cv, 3)
            att_pe(pe, 0, 0, Count(0), Count(T_SIG), Count(b + T_SIG))
            with pe.Fori(0, NB - 2) as i:
                att_pe(pe, i + 1, 1, Count(AH, AH, i), Count(T_SIG + 2, 2, i), Count(b + T_SIG + 2, 2, i))
            att_pe(pe, NB - 1, 2, Count(AH * (NB - 1)), Count(T_MG - 2), Count(b + T_MG - 2))
            mix_product(pe, Count(T_MG), Count(b + T_MG), 0)
            for k in range(KD):
                mix_product(pe, Count(T_GM), Count(b + T_GM), k)

        def evac(act, ct, k, func, dst, before=()):
            act.wait_ge(mix_done, ct.n(k + 1))
            for s_, v_ in before:
                act.wait_ge(s_, v_)
            nc.scalar.activation(dst, ps[ct.slot(k)][:, :], func).then_inc(mix_left, 1)

        def silu_conv(act, cc, k, m):
            act.wait_ge(conv_done, cc.n(k + 1))
            tile = mqk[:, bass.ds(m, 1), :].rearrange("p a n -> p (a n)")
            nc.scalar.activation(tile, tile, ACT.Silu).then_inc(mqk_ready, 1)

        def conv_act(act, b, i, first):
            cb, ct, cc = Count(b + T_MQK + first, 2, i), Count(T_MQK + first, 2, i), Count(first, 2, i)
            for k in range(2):
                if first + k >= 2:
                    act.wait_ge(conv_done, cc.n(k - 1))
                elif k == 0:
                    act.wait_ge(pad_zero, 1)
                evac(act, ct, k, ACT.Copy, zpad[:, k, TAPS // 2:TAPS // 2 + S])
                split_hi(act, cb, k + 2)
                silu_conv(act, cc, k, i * 2 + (first + k))

        def att_act(act, n, edge, cu, ct, cb, next_hi):
            blocks = att_window(n, edge)[1]
            width = blocks * P

            def expo(j):
                act.wait_ge(neg_ready, cu.n(j + 1))
                nc.scalar.activation(prob[:, j % 2, 0:width], prob[:, j % 2, 0:width], ACT.Exp,
                                     bias=A_NEG[:, j:j + 1], scale=ATT_SCALE,
                                     accum_out=A_SUM[:, j:j + 1]).then_inc(prob_ready, 1)

            def keep(j):
                act.wait_ge(pt_done, cu.n(j + 1))
                if cu.base + j >= 2:
                    act.wait_ge(pv_done, cu.n(j - 1))
                nc.scalar.copy(prob_t[:, j % 2, 0:width], PT[:, 0:width]).then_inc(pt_left, 1)

            def sig(k):
                s = ct.slot(k)
                before = []
                if ct.base + k >= T_SIG + 2:
                    uses = (ct.base + k - T_SIG) // 2
                    before = [(sig_stored[s], 16 * uses if ct.turn is None else ct.turn * 16 + 16 * uses)]
                evac(act, ct, k, ACT.Copy, tmp[:, s, :], before)

            for j in range(AH):
                expo(j)
                if j:
                    keep(j - 1)
                if j == 4:
                    sig(0)
                    next_hi(2)
            keep(AH - 1)
            act.wait_ge(sink_arg, n + 1)
            nc.scalar.activation(A_ESINK[:, :], A_SINK[:, :], ACT.Exp).then_inc(sink_exp, 1)
            sig(1)
            next_hi(3)

        def gates_hi(act, c):
            s = c.slot()
            act.wait_ge(raw_loaded[s], c.uses() * 16)
            act.wait_ge(wz, 2)
            for n in range(4):
                op = nc.scalar.activation(gate_cols(w_hi, s, n), raw_gate_cols(s, n), ACT.Copy)
            op.then_inc(whi_ready, 1)

        def gate_cols(w, s, n):
            first = 64 * (n % 2) + 32 * (n // 2)
            return w[:, s, :].rearrange("p (k n) -> p k n", k=KD)[:, :, first:first + MH]

        def raw_gate_cols(s, n):
            return w_raw[:, s, 0:KD * 4 * MH].rearrange("p (k n) -> p k n", k=KD)[:, :, n * MH:(n + 1) * MH]

        def mix_act(act, b):
            cb, ct = Count(b), Count(0)
            for k in range(N_QKV):
                if k < 2:
                    act.wait_ge(raw_q[cb.slot(k)], 32)
                evac(act, ct, k, ACT.Copy, tmp[:, k % 2, :],
                     [(rope_done, k - 1)] if k >= 2 else [(ulo_ready, 2 * KD)])
                split_hi(act, cb, k + 2)
            with act.Fori(0, MH // 2) as i:
                conv_act(act, b, i, 0)
            with act.Fori(0, MH // 2) as i:
                conv_act(act, b, i, MH)
            act.wait_ge(conv_done, KD)
            with act.Fori(0, KD // 4) as i:
                cb, ct = Count(b + T_MV, 4, i), Count(T_MV, 4, i)
                for k in range(4):
                    evac(act, ct, k, ACT.Copy, tmp[:, ct.slot(k), :], [(vt_done, Count(max(k, 1), 4, i).n())])
                    split_hi(act, cb, k + 2)
            act.wait_ge(vt_done, 1 + KD)
            cb = Count(b + T_SIG)
            att_act(act, 0, 0, Count(0), Count(T_SIG), cb, lambda k: split_hi(act, cb, k))
            with act.Fori(0, NB - 2) as i:
                cbi = Count(b + T_SIG + 2, 2, i)
                att_act(act, i + 1, 1, Count(AH, AH, i), Count(T_SIG + 2, 2, i), cbi,
                        lambda k: split_hi(act, cbi, k))
            last = {2: lambda: gates_hi(act, Count(b + T_MG)), 3: lambda: split_hi(act, Count(b + T_GM), 0)}
            att_act(act, NB - 1, 2, Count(AH * (NB - 1)), Count(T_MG - 2), Count(b + T_MG - 2),
                    lambda k: last[k]())
            act.wait_ge(mix_done, T_MG + 1)
            act.wait_ge(small_loaded, 48)
            act.wait_ge(pv_done, AH * NB)
            acc = ps[T_MG % 2]
            nc.scalar.activation(r_li[:, :], acc[0:CHAIN_ROWS, :], ACT.Identity,
                                 bias=gate_bias[:, 0:1]).then_inc(row_act, 1)
            nc.scalar.activation(r_lf[:, :], acc[CHAIN_ROWS:P, :], ACT.Copy).then_inc(mix_left, 1)
            split_hi(act, Count(b + T_GM), 1)
            act.wait_ge(row_dve, 1)
            nc.scalar.activation(r_b[:, :], r_lf[:, :], ACT.Abs).then_inc(row_act, 1)
            act.wait_ge(row_act, 2)
            nc.scalar.activation(r_b[:, :], r_b[:, :], ACT.Exp, scale=-1.0).then_inc(row_act, 1)
            act.wait_ge(row_act, 3)
            nc.scalar.activation(r_b[:, :], r_b[:, :], ACT.Ln, bias=1.0).then_inc(row_act, 1)

            def gm(ct, cb, k, stored):
                evac(act, ct, k, ACT.Copy, tmp[:, ct.slot(k), :], [(sig_stored[ct.slot(k)], stored)])
                if cb is not None:
                    split_hi(act, cb, k + 2)

            for k in range(2):
                gm(Count(T_GM), Count(b + T_GM), k, 16 * KD)
            act.wait_ge(row_dve, 12)
            nc.scalar.activation(r_wi[:, :], r_wi[:, :], ACT.Exp).then_inc(row_act, 1)
            nc.scalar.activation(r_em[:, :], r_em[:, :], ACT.Exp, scale=-1.0).then_inc(row_act, 1)
            nc.scalar.activation(r_wk[:, :], r_wk[:, :], ACT.Exp).then_inc(row_act, 1)
            with act.Fori(0, 2) as i:
                for k in range(2):
                    gm(Count(T_GM + 2, 2, i), Count(b + T_GM + 2, 2, i), k, i * 16 + 16 * (KD + 1))
            for k in range(6, KD):
                gm(Count(T_GM), None, k, 16 * (KD + k // 2))

        def att_dve(dve, n, edge, cu, cb, next_lo):
            key0, blocks, mask0 = att_window(n, edge)
            width = blocks * P
            if edge:
                dve.wait_ge(score_done, cu.n(0))
            else:
                dve.wait_ge(qst_zero, 1)
                dve.wait_ge(rope_done, AH // 2 + 1)
            for g in range(2):
                rows = slice(64 * g, 64 * g + 64)
                op = copy(q_st[rows, g, :, :], att_q[rows, :, bass.ds(n * P, P)])
            op.then_inc(qst_ready, 1)
            for j in range(AH):
                if cu.base + j >= 2:
                    dve.wait_ge(pt_done, cu.n(j - 1))
                dve.wait_ge(score_done, cu.n(j + 1))
                nc.vector.tensor_copy(tick[:, :], neg_sinks[:, 0:1])
                nc.vector.tensor_tensor_reduce(out=prob[:, j % 2, 0:width], in0=score_bank(j)[:, 0:width],
                                               in1=window[:, mask0:mask0 + width], scale=1.0, scalar=-3e38,
                                               op0=ALU.add, op1=ALU.max, accum_out=A_MAX[:, j:j + 1]
                                               ).then_inc(max_done, 1)
                dve.wait_ge(max_done, cu.n(j + 1))
                if j == 0 and cu.base:
                    dve.wait_ge(den_ready, n)
                nc.vector.tensor_scalar(A_NEG[:, j:j + 1], A_MAX[:, j:j + 1], -ATT_SCALE, neg_sinks[:, j:j + 1],
                                        ALU.mult, ALU.min).then_inc(neg_ready, 1)
                if j == 4:
                    next_lo(2)
            dve.wait_ge(neg_ready, cu.n(AH))
            nc.vector.tensor_tensor(A_SINK[:, :], A_NEG[:, :], neg_sinks[:, :], ALU.subtract).then_inc(sink_arg, 1)
            dve.wait_ge(sink_exp, n + 1)
            dve.wait_ge(prob_ready, cu.n(AH))
            nc.vector.tensor_tensor(A_DEN[:, :], A_SUM[:, :], A_ESINK[:, :], ALU.add).then_inc(den_ready, 1)
            dve.wait_ge(den_ready, n + 1)
            nc.vector.reciprocal(A_REC[:, :], A_DEN[:, :]).then_inc(rec_ready, 1)
            dve.wait_ge(rec_ready, n + 1)
            dve.wait_ge(pv_done, cu.n(AH))
            if cu.base:
                dve.wait_ge(ot_done, n)
            for g in range(2):
                heads_g = slice(g * AH // 2 * AD, (g + 1) * AH // 2 * AD)
                op = nc.vector.tensor_tensor(
                    o_sb[:, heads_g].rearrange("p (i d) -> p i d", d=AD),
                    OA[:, heads_g].rearrange("p (i d) -> p i d", d=AD),
                    A_REC[:, :].rearrange("p (i g) -> p g i", g=2)[:, g, :].unsqueeze(2).to_broadcast(
                        [P, AH // 2, AD]), ALU.mult)
            op.then_inc(osb_ready, 1)
            dve.wait_ge(ot_done, n + 1)
            copy(att_q[:, :, bass.ds(n * P, P)], OT.rearrange("p (k n) -> p k n", n=P)).then_inc(ot_left, 1)
            next_lo(3)

        def rope(dve, k):
            dst = att_q[:, k, :] if k < AH // 2 else att_k[:, :]
            dve.wait_ge(rot_done, k + 1)
            if k:
                dve.wait_ge(rope_done, k)
            nc.vector.tensor_tensor(dst, tmp[:, k % 2, :], cos_sb[:, :], ALU.mult).then_inc(rope_cos, 1)
            nc.vector.tensor_tensor(rope_t[:, :], ps[2][:, :], sin_sb[:, :], ALU.mult).then_inc(rope_sin, 1)
            dve.wait_ge(rope_cos, k + 1)
            dve.wait_ge(rope_sin, k + 1)
            nc.vector.tensor_tensor(dst, dst, rope_t[:, :], ALU.add).then_inc(rope_done, 1)

        def convolve(dve, cc, ct, k, m, slot):
            dve.wait_ge(mix_left, ct.n(k + 1))
            tile = mqk[:, bass.ds(m, 1), :].rearrange("p a n -> p (a n)")
            steps = Count(cc.base * (TAPS - 1), cc.per * (TAPS - 1), cc.turn)

            def vec(first):
                return vecs[:, bass.ds(m + first, 1)]

            nc.vector.tensor_scalar(tile, zpad[:, slot, 0:S], vec(80), vec(72), ALU.mult,
                                    ALU.add).then_inc(conv_step, 1)
            for tap in range(1, TAPS):
                dve.wait_ge(conv_step, steps.n((TAPS - 1) * k + tap))
                nc.vector.scalar_tensor_tensor(out=tile, in0=zpad[:, slot, tap:tap + S], scalar=vec(80 + KD * tap),
                                               in1=tile, op0=ALU.mult, op1=ALU.add
                                               ).then_inc(conv_step if tap < TAPS - 1 else conv_done, 1)

        def conv_dve(dve, b, i, first):
            cb, ct, cc = Count(b + T_MQK + first, 2, i), Count(T_MQK + first, 2, i), Count(first, 2, i)
            for k in range(2):
                split_lo(dve, cb, k + 2)
                convolve(dve, cc, ct, k, i * 2 + (first + k), k)

        def mix_dve(dve, b):
            cb = Count(b)
            dve.wait_ge(tables_loaded, 64)
            for k in range(N_QKV - 1):
                split_lo(dve, cb, k + 2)
                rope(dve, k)
            split_lo(dve, cb, N_QKV + 1)
            dve.wait_ge(vt_done, 1)
            nc.vector.tensor_copy(att_v[:, :, :], ps[3][:, :].rearrange("p (b n) -> p b n", n=P)
                                  ).then_inc(vt_left, 1)
            dve.wait_ge(spilled, 16 * KD)
            with dve.Fori(0, MH // 2) as i:
                conv_dve(dve, b, i, 0)
            with dve.Fori(0, MH // 2) as i:
                conv_dve(dve, b, i, MH)
            dve.wait_ge(ones_v, 1)
            with dve.Fori(0, KD // 4) as i:
                cb, cv = Count(b + T_MV, 4, i), Count(1, 4, i)
                for k in range(4):
                    split_lo(dve, cb, k + 2)
                    dve.wait_ge(vt_done, cv.n(k + 1))
                    copy(m_v[:, :, bass.ds(i * 2 + k // 2, 1), (k % 2) * P:(k % 2 + 1) * P],
                         ps[3][:, :].rearrange("p (b a n) -> p b a n", a=1, n=P)).then_inc(vt_left, 1)
            dve.wait_ge(small_loaded, 48)
            nc.vector.tensor_scalar(neg_sinks.rearrange("p (i g) -> p i g", g=2),
                                    sinks[:, :].rearrange("p (g i) -> p i g", g=2), -1.0, None, ALU.mult).then_inc(sinks_ready, 1)
            dve.wait_ge(sinks_ready, 1)
            cb = Count(b + T_SIG)
            att_dve(dve, 0, 0, Count(0), cb, lambda k: split_lo(dve, cb, k))
            with dve.Fori(0, NB - 2) as i:
                cbi = Count(b + T_SIG + 2, 2, i)
                att_dve(dve, i + 1, 1, Count(AH, AH, i), cbi, lambda k: split_lo(dve, cbi, k))

            def gates_lo(c):
                s = c.slot()
                dve.wait_ge(block_used, c.n(-RING + 1))
                dve.wait_ge(wlo_ready, c.n(-RING + 1))
                for w in (w_hi, w_lo):
                    nc.vector.memset(w[:, s, :].bitcast(F32), 0.0).then_inc(wz, 1)
                dve.wait_ge(whi_ready, c.n(1))
                dve.wait_ge(wz, 2)
                for n in range(4):
                    op = nc.vector.tensor_tensor(gate_cols(w_lo, s, n), raw_gate_cols(s, n),
                                                 gate_cols(w_hi, s, n).bitcast(F32), ALU.subtract)
                op.then_inc(wlo_ready, 1)

            last = {2: lambda: gates_lo(Count(b + T_MG)), 3: lambda: split_lo(dve, Count(b + T_GM), 0)}
            att_dve(dve, NB - 1, 2, Count(AH * (NB - 1)), Count(b + T_MG - 2), lambda k: last[k]())
            split_lo(dve, Count(b + T_GM), 1)
            dve.wait_ge(mix_left, T_MG + 1)
            dve.wait_ge(tables_loaded, 80)

            fw, bw = slice(0, 32), slice(32, CHAIN_ROWS)
            nc.vector.tensor_scalar(r_lf[:, :], r_lf[:, :], gate_bias[:, 1:2], None, ALU.add).then_inc(row_dve, 1)
            dve.wait_ge(row_act, 4)
            nc.vector.scalar_tensor_tensor(out=r_lf[:, :], in0=r_lf[:, :], scalar=0.0, in1=r_b[:, :], op0=ALU.min,
                                           op1=ALU.subtract).then_inc(row_dve, 1)
            dve.wait_ge(row_dve, 2)
            nc.vector.tensor_tensor_scan(r_b[fw, :], r_in[fw, :], r_lf[fw, :], 0.0, ALU.mult,
                                         ALU.add).then_inc(row_dve, 1)
            nc.vector.tensor_tensor_scan(r_b[bw, ::-1], r_in[bw, ::-1], r_lf[bw, ::-1], 0.0, ALU.mult,
                                         ALU.add).then_inc(row_dve, 1)
            nc.vector.tensor_tensor_scan(r_m[fw, :], r_lf[fw, :], r_li[fw, :], 0.0, ALU.add,
                                         ALU.max).then_inc(row_dve, 1)
            nc.vector.tensor_tensor_scan(r_m[bw, ::-1], r_lf[bw, ::-1], r_li[bw, ::-1], 0.0, ALU.add,
                                         ALU.max).then_inc(row_dve, 1)
            dve.wait_ge(row_dve, 6)
            nc.vector.tensor_tensor(r_g[:, :], r_li[:, :], r_b[:, :], ALU.subtract).then_inc(row_dve, 1)
            dve.wait_ge(row_dve, 7)
            nc.vector.tensor_tensor(r_r[:, :], r_m[:, :], r_b[:, :], ALU.subtract).then_inc(row_dve, 1)
            dve.wait_ge(row_dve, 8)
            before, last_r = chunk_rows[:, 0, :], chunk_rows[:, 1, :]
            m_t = r_m[:, :].rearrange("p (b n) -> p b n", n=P)
            r_t = r_r[:, :].rearrange("p (b n) -> p b n", n=P)
            nc.vector.memset(chunk_rows[:, :, :], 0.0).then_inc(row_dve, 1)
            dve.wait_ge(row_dve, 9)
            nc.vector.tensor_copy(before[fw, 1:NB], m_t[fw, 0:NB - 1, P - 1])
            nc.vector.tensor_copy(before[bw, 0:NB - 1], m_t[bw, 1:NB, 0])
            nc.vector.tensor_copy(last_r[fw, :], r_t[fw, :, P - 1])
            nc.vector.tensor_copy(last_r[bw, :], r_t[bw, :, 0]).then_inc(row_dve, 1)
            dve.wait_ge(row_dve, 10)

            def spread(x):
                return x.unsqueeze(2).to_broadcast([CHAIN_ROWS, NB, P])

            nc.vector.tensor_tensor(r_wi[:, :].rearrange("p (b n) -> p b n", n=P), spread(before), r_t,
                                    ALU.subtract).then_inc(row_dve, 1)
            nc.vector.tensor_tensor(r_wk[:, :].rearrange("p (b n) -> p b n", n=P),
                                    r_g[:, :].rearrange("p (b n) -> p b n", n=P), spread(last_r),
                                    ALU.subtract).then_inc(row_dve, 1)
            cb = Count(b + T_GM)
            split_lo(dve, cb, 2)
            split_lo(dve, cb, 3)
            with dve.Fori(0, 2) as i:
                for k in range(2):
                    split_lo(dve, Count(b + T_GM + 2, 2, i), k + 2)
        (cols_turned, cols_left, chains_loaded, st_done, kt_done, rb_done, arg_sub, arg_ready, exp_ready, s_ready,
         wb_done, q_ready, kw_ready, out_done, dc_done, c_ready, den_bound, den_max, den_inv, hm_left,
         sq_heads) = (sem(x) for x in (
            "cols_turned", "cols_left", "chains_loaded", "st_done", "kt_done", "rb_done", "arg_sub", "arg_ready",
            "exp_ready", "s_ready", "wb_done", "q_ready", "kw_ready", "out_done", "dc_done", "c_ready",
            "den_bound", "den_max", "den_inv", "hm_left", "sq_heads"))
        ST = ps[0]
        BCAST = KT = ps[1]
        G_COL, WK_COL, EM_COL = range(3)

        def chunk_of(way, n):
            return n if way == 0 else NB - 1 - n

        def column(way, h, q):
            return col[:, :, q, 32 * way + h]

        def over_rows(x):
            return x.unsqueeze(2).to_broadcast([P, NB, P])

        def blocks(x):
            return x[:, :].rearrange("p (b n) -> p b n", n=P)

        def d_state(way):
            return ps[2][:, way * HALF:way * HALF + MV + 1]

        def d_out(way):
            return ps[3][:, way * HALF:way * HALF + MV + 1]

        def both_dens():
            return ps[3][:, :].rearrange("p (w n) -> p w n", w=2)[:, :, MV]

        def mlstm_pe(pe):
            pe.wait_ge(row_act, 7)
            pe.wait_ge(row_dve, 12)
            for n in range(NB):
                for q, rows in ((G_COL, r_g), (WK_COL, r_wk), (EM_COL, r_em)):
                    at_ = (n * 3 + q) * CHAIN_ROWS
                    mm = nc.tensor.transpose(ps[2 + at_ // S][:, at_ % S:at_ % S + CHAIN_ROWS],
                                             rows[:, n * P:(n + 1) * P], ident[0:CHAIN_ROWS, 0:CHAIN_ROWS])
            mm.then_inc(cols_turned, 1)
            pe.wait_ge(cols_left, 2)
            pe.wait_ge(mix_left, N_TILES)
            pe.wait_ge(chains_loaded, 48)

            def scores(h):
                if h:
                    pe.wait_ge(s_ready, 2 * h)
                    pe.wait_ge(q_ready, 2 * h)
                for n in range(NB):
                    cols = slice(n * P, (n + 1) * P)
                    mm = nc.tensor.matmul(ST[:, cols], mqk[:, MH + h, cols], mqk[:, h, cols], start=True, stop=True)
                mm.then_inc(st_done, 1)
                for n in range(NB):
                    cols = slice(n * P, (n + 1) * P)
                    mm = nc.tensor.transpose(KT[:, cols], mqk[:, MH + h, cols], ident[:, :])
                mm.then_inc(kt_done, 1)

            def row_on_all(h, way, rows, done, free):
                pe.wait_ge(*free)
                for f in range(2):
                    mm = nc.tensor.matmul(BCAST[:, f * HALF:(f + 1) * HALF], chains[:, way, h, :],
                                          rows[:, f * HALF:(f + 1) * HALF], start=True, stop=True)
                mm.then_inc(done, 1)

            def prepare(h, step):
                if step == 0:
                    scores(h)
                elif step == 2:
                    row_on_all(h, 0, r_r, rb_done, (kw_ready, 2 * h + 2))
                elif step == 3:
                    row_on_all(h, 0, r_wi, wb_done, (arg_sub, 2 * h + 1))
                elif step == 4:
                    row_on_all(h, 1, r_r, rb_done, (q_ready, 2 * h + 1))
                elif step == 5:
                    row_on_all(h, 1, r_wi, wb_done, (arg_sub, 2 * h + 2))

            for step in range(6):
                prepare(0, step)
            for h in range(MH):
                for n in range(NB):
                    first, done = h * NB, h * NB + n
                    if n == 0:
                        pe.wait_ge(s_ready, 2 * h + 2)
                        pe.wait_ge(kw_ready, 2 * h + 2)
                    if done:
                        pe.wait_ge(hm_left, done)
                    for way in range(2):
                        c = chunk_of(way, n)
                        mm = nc.tensor.matmul(d_out(way), h_s[h % 2][:, way, c, :], m_v[:, c, h, :], start=True,
                                              stop=(n == 0))
                    if n:
                        pe.wait_ge(q_ready, 2 * h + 2)
                        for way in range(2):
                            pe.wait_ge(c_ready, 2 * ((NB - 1) * h + n - 1) + way + 1)
                            mm = nc.tensor.matmul(d_out(way), h_q[h % 2][:, way, chunk_of(way, n), :],
                                                  state[:, way, n % 2, :], start=False, stop=True)
                    mm.then_inc(out_done, 1)
                    if n < NB - 1:
                        if n == 0 and h:
                            pe.wait_ge(c_ready, 2 * (NB - 1) * h)
                        for way in range(2):
                            c = chunk_of(way, n)
                            nc.tensor.matmul(d_state(way), h_kw[h % 2][:, way, c, :], m_v[:, c, h, :], start=True,
                                             stop=True).then_inc(dc_done, 1)
                    if h + 1 < MH:
                        prepare(h + 1, n)

        def mlstm_act(act):
            def weights(h):
                for way in range(2):
                    act.wait_ge(arg_ready, 2 * h + way + 1)
                    if h >= 2:
                        act.wait_ge(out_done, NB * (h - 1))
                    nc.scalar.activation(h_s[h % 2][:, way, :, :], h_arg[:, :, :], ACT.Exp,
                                         scale=-1.0).then_inc(exp_ready, 1)

            def squares(h):
                act.wait_ge(hm_left, NB * (h + 1))
                for c in range(NB):
                    if h * NB + c >= 4:
                        act.wait_ge(sq_heads, h * NB + c - 3)
                    nc.scalar.activation(h_junk[:, c % 4, :], hm[:, c, h, :], ACT.Square,
                                         accum_out=m_cols[:, 0, h * NB + c:h * NB + c + 1]).then_inc(sq_heads, 1)

            weights(0)
            for h in range(MH):
                if h:
                    squares(h - 1)
                if h + 1 < MH:
                    weights(h + 1)
            squares(MH - 1)

        def mlstm_dve(dve):
            dve.wait_ge(cols_turned, 1)
            dve.wait_ge(mix_done, N_TILES)
            flat = col[:, :, :, :].rearrange("p b q n -> p (b q n)")
            nc.vector.tensor_copy(flat[:, 0:S], ps[2][:, :]).then_inc(cols_left, 1)
            nc.vector.tensor_copy(flat[:, S:3 * NB * CHAIN_ROWS], ps[3][:, 0:3 * NB * CHAIN_ROWS - S]
                                  ).then_inc(cols_left, 1)
            dve.wait_ge(cols_left, 2)
            dve.wait_ge(chains_loaded, 48)
            for s in range(2):
                dve.wait_ge(sig_stored[s], 16 * 12)

            def weighed_keys(h):
                dve.wait_ge(kt_done, h + 1)
                if h >= 2:
                    dve.wait_ge(dc_done, 2 * (NB - 1) * (h - 1))
                for way in range(2):
                    nc.vector.scalar_tensor_tensor(out=h_kw[h % 2][:, way, :, :], in0=blocks(KT), scalar=K_SCALE,
                                                   in1=over_rows(column(way, h, WK_COL)), op0=ALU.mult,
                                                   op1=ALU.mult).then_inc(kw_ready, 1)

            def subtract(h, way):
                dve.wait_ge(rb_done, 2 * h + way + 1)
                if 2 * h + way:
                    dve.wait_ge(exp_ready, 2 * h + way)
                nc.vector.tensor_tensor(h_arg[:, :, :], blocks(BCAST), over_rows(column(way, h, G_COL)),
                                        ALU.subtract).then_inc(arg_sub, 1)

            def bound(h, way):
                dve.wait_ge(arg_sub, 2 * h + way + 1)
                nc.vector.tensor_tensor(h_arg[:, :, :], h_arg[:, :, :],
                                        order[:, way, :].unsqueeze(1).to_broadcast([P, NB, P]),
                                        ALU.max).then_inc(arg_ready, 1)

            def weighed_queries(h, way):
                dve.wait_ge(wb_done, 2 * h + way + 1)
                if h >= 2:
                    dve.wait_ge(out_done, NB * (h - 1))
                last = 0 if way else P - 1
                nc.vector.tensor_copy(h_dec[:, h % 2, way, :], blocks(BCAST)[:, :, last])
                nc.vector.tensor_tensor(h_q[h % 2][:, way, :, :].rearrange("p b n -> p (b n)"), mqk[:, h, :],
                                        BCAST[:, :], ALU.mult).then_inc(q_ready, 1)

            def weighed_scores(h, way):
                dve.wait_ge(exp_ready, 2 * h + way + 1)
                dve.wait_ge(st_done, h + 1)
                nc.vector.scalar_tensor_tensor(out=h_s[h % 2][:, way, :, :], in0=blocks(ST), scalar=K_SCALE,
                                               in1=h_s[h % 2][:, way, :, :], op0=ALU.mult, op1=ALU.mult
                                               ).then_inc(s_ready, 1)

            def prepare(h, step):
                if step == 1:
                    weighed_keys(h)
                elif step == 2:
                    subtract(h, 0)
                    bound(h, 0)
                elif step == 3:
                    weighed_queries(h, 0)
                elif step == 4:
                    weighed_scores(h, 0)
                    subtract(h, 1)
                elif step == 5:
                    bound(h, 1)
                    weighed_queries(h, 1)
                elif step == 6:
                    weighed_scores(h, 1)

            for step in range(7):
                prepare(0, step)
            dve.wait_ge(q_ready, 2)
            for h in range(MH):
                for n in range(NB):
                    done = h * NB + n
                    chunks = [chunk_of(way, n) for way in range(2)]
                    dve.wait_ge(out_done, done + 1)
                    for way in range(2):
                        op = nc.vector.tensor_scalar(h_den[:, 0, way:way + 1], d_out(way)[:, MV:MV + 1], -1.0,
                                                     col[:, chunks[way], EM_COL, 32 * way + h:32 * way + h + 1],
                                                     ALU.mult, ALU.max)
                    op.then_inc(den_bound, 1)
                    dve.wait_ge(den_bound, done + 1)
                    nc.vector.tensor_tensor(h_den[:, 0, :], h_den[:, 0, :], both_dens(), ALU.max).then_inc(den_max, 1)
                    dve.wait_ge(den_max, done + 1)
                    nc.vector.reciprocal(h_den[:, 1, :], h_den[:, 0, :]).then_inc(den_inv, 1)
                    dve.wait_ge(den_inv, done + 1)
                    for way in range(2):
                        if n < NB // 2:
                            op = nc.vector.tensor_scalar(hm[:, chunks[way], h, :], d_out(way)[:, 0:MV],
                                                         h_den[:, 1, way:way + 1], None, ALU.mult)
                        else:
                            op = nc.vector.scalar_tensor_tensor(out=hm[:, chunks[way], h, :],
                                                                in0=d_out(way)[:, 0:MV],
                                                                scalar=h_den[:, 1, way:way + 1],
                                                                in1=hm[:, chunks[way], h, :], op0=ALU.mult,
                                                                op1=ALU.add)
                    op.then_inc(hm_left, 1)
                    if n < NB - 1:
                        turn = 2 * ((NB - 1) * h + n)
                        for way in range(2):
                            dve.wait_ge(dc_done, turn + way + 1)
                            if n == 0:
                                nc.vector.tensor_copy(state[:, way, 1, :], d_state(way)).then_inc(c_ready, 1)
                            else:
                                dve.wait_ge(c_ready, turn + way - 1)
                                nc.vector.scalar_tensor_tensor(
                                    out=state[:, way, (n + 1) % 2, :], in0=state[:, way, n % 2, :],
                                    scalar=h_dec[:, h % 2, way, chunks[way]:chunks[way] + 1], in1=d_state(way),
                                    op0=ALU.mult, op1=ALU.add).then_inc(c_ready, 1)
                    if n == NB // 2 - 1:
                        dve.wait_ge(hm_left, done + 1)
                    if h + 1 < MH:
                        prepare(h + 1, n)

        def mlstm_sp(sp):
            sp.wait_ge(cols_turned, 1)
            sp.dma_start(chains[:, :, :, :].rearrange("p w h n -> p (w h n)"),
                         table("chains", CHAIN_ROWS)).then_inc(chains_loaded, 16)
            sp.dma_start(order[:, 0, :], table("later")).then_inc(chains_loaded, 16)
            sp.dma_start(order[:, 1, :], table("earlier")).then_inc(chains_loaded, 16)


        (heads_mean, heads_root, heads_inv, hm_scaled, hm_turned, hmhi_ready, mlo_ready, ohi_ready, olo_ready,
         br_attn, br_mlstm, br_sum, mghi_ready, resid_back) = (sem(x) for x in (
            "heads_mean", "heads_root", "heads_inv", "hm_scaled", "hm_turned", "hmhi_ready", "mlo_ready",
            "ohi_ready", "olo_ready", "br_attn", "br_mlstm", "br_sum", "mghi_ready", "resid_back"))
        sig_loaded = [sem(f"sig_loaded{n}") for n in range(2)]
        sig_made = [sem(f"sig_made{n}") for n in range(2)]
        sig_free = [sem(f"sig_free{n}") for n in range(2)]
        T_BR = N_TILES
        T_WO = T_BR + 2 * KD
        T_END = T_WO + KD
        GATED = KD // 2
        WIDTH_A, WIDTH_P = AH * AD, PLE

        def k_tiles(w, first):
            return w[:, bass.ds(first, P)].rearrange("(k p) n -> p k n", p=P)

        def load_part(sp, c, k, src):
            sp.wait_ge(wlo_ready, c.n(k - RING + 1))
            s = c.slot(k)
            nk = src.shape[1]
            sp.dma_start(w_raw[:, s, 0:nk * P].rearrange("p (k n) -> p k n", k=nk), src).then_inc(raw_loaded[s], 16)

        def branch_sp(sp, b):
            W_A, W_M, W_O = t["w_branch_attn"][0], t["w_branch_mlstm"][0], t["w_out"][0]
            mlstm_sp(sp)
            sp.wait_ge(wb_done, 2 * MH)
            sp.wait_ge(arg_ready, 2 * MH)
            for m in range(KD):
                if m == 2:
                    sp.wait_ge(out_done, MH * NB)
                    load_part(sp, Count(b + T_BR), 0, k_tiles(W_A, 0))
                    load(sp, Count(b + T_BR), 1, k_tiles(W_M, 0))
                if m >= 2:
                    sp.wait_ge(sig_free[m % 2], m // 2)
                sp.dma_start(sig_in[:, m % 2, :], sig_dram[m]).then_inc(sig_loaded[m % 2], 16)

            def merge_gates(m, k, i):
                for j in range(2):
                    sp.wait_ge(sig_free[j], Count(GATED + k, 2, i).n())
                    sp.dma_start(sig_in[:, j, :], sig_tile(m + KD * (1 + j))).then_inc(sig_loaded[j], 16)

            with sp.Fori(0, KD // 2 - 1) as i:
                c = Count(b + T_BR + 2, 4, i)
                for k in range(2):
                    merge_gates(i * 2 + k, k, i)
                    load_part(sp, c, 2 * k, k_tiles(W_A, i * (2 * P) + (k + 1) * P))
                    load(sp, c, 2 * k + 1, k_tiles(W_M, i * (2 * P) + (k + 1) * P))
            merge_gates(KD - 2, KD - 2, None)
            c = Count(b + T_WO - 2)
            load_part(sp, c, 0, k_tiles(W_A, (KD - 1) * P))
            load(sp, c, 1, k_tiles(W_M, (KD - 1) * P))
            merge_gates(KD - 1, KD - 1, None)
            for m in range(KD):
                load(sp, Count(b + T_WO), m, k_tiles(W_O, m * P))
                if m == 1:
                    sp.wait_ge(block_used, b + T_WO)
                    for k in range(KD):
                        sp.dma_start(resid[:, k, :], resid_dram[k]).then_inc(resid_back, 16)

        def branch_pe(pe, b):
            for m in range(KD):
                pe.wait_ge(hm_scaled, m // 2 + 1)
                if m >= 4:
                    pe.wait_ge(sig_free[m % 2], (m - 4) // 2 + 1)
                for c in range(NB):
                    mm = nc.tensor.transpose(ps[m % 4][:, c * P:(c + 1) * P],
                                             hm[:, c, m // 2, (m % 2) * P:(m % 2 + 1) * P], ident[:, :])
                mm.then_inc(hm_turned, 1)
            pe.wait_ge(olo_ready, AH // 2)
            pe.wait_ge(mlo_ready, KD)
            with pe.Fori(0, KD // 2) as i:
                c = Count(b + T_BR, 4, i)
                for j in range(2):
                    pe.wait_ge(wlo_ready, c.n(2 * j + 1))
                    pe.wait_ge(sig_free[0], Count(GATED + j - 1, 2, i).n())
                    product(ps[2 * j], [(c.slot(2 * j), k * P, o_hi[:, k, :], o_lo[:, k, :])
                                        for k in range(AH // 2)], new_block=True).then_inc(br_attn, 1)
                    pe.wait_ge(wlo_ready, c.n(2 * j + 2))
                    pe.wait_ge(sig_free[1], Count(GATED + j - 1, 2, i).n())
                    product(ps[2 * j + 1], [(c.slot(2 * j + 1), k * P, hm_hi[:, k, :], hm_lo[:, k, :])
                                            for k in range(KD)], new_block=True).then_inc(br_mlstm, 1)
            for j in range(2):
                pe.wait_ge(sig_free[j], GATED + KD)
            pe.wait_ge(mlo_ready, 2 * KD)
            with pe.Fori(0, KD // 4) as i:
                c, ct = Count(b + T_WO, 4, i), Count(N_TILES, 4, i)
                for m in range(4):
                    pe.wait_ge(wlo_ready, c.n(m + 1))
                    pe.wait_ge(mix_left, ct.n(m - 3))
                    product(ps[m], [(c.slot(m), k * P, mg_hi[:, k, :], mg_lo[:, k, :]) for k in range(KD)],
                            new_block=True).then_inc(mix_done, 1)

        def branch_act(act, b):
            act.wait_ge(heads_mean, 1)
            nc.scalar.activation(m_cols[:, 1, :], m_cols[:, 1, :], ACT.Sqrt).then_inc(heads_root, 1)
            act.wait_ge(out_done, MH * NB)
            for k in range(AH // 2):
                nc.scalar.activation(o_hi[:, k, :], att_q[:, k, :], ACT.Copy).then_inc(ohi_ready, 1)

            def gate(j, uses):
                act.wait_ge(sig_loaded[j], 16 * uses)
                nc.scalar.activation(sig_in[:, j, :], sig_in[:, j, :], ACT.Sigmoid).then_inc(sig_made[j], 1)

            gate(0, 1)
            gate(1, 1)
            for m in range(KD):
                act.wait_ge(sig_free[m % 2], m // 2 + 1)
                nc.scalar.activation(hm_hi[:, m, :], tmp[:, m % 2, :], ACT.Copy).then_inc(hmhi_ready, 1)
                if m + 2 < KD:
                    gate(m % 2, m // 2 + 2)
            split_hi(act, Count(b + T_BR), 0, WIDTH_A)

            def turn(c, g, last):
                for j in range(2):
                    split_hi(act, c, 2 * j + 1)
                    gate(0, g.n(j + 1))
                    gate(1, g.n(j + 1))
                    split_hi(act, c, 2 * j + 2, 1024 if last and j else WIDTH_A)

            with act.Fori(0, KD // 2 - 1) as i:
                turn(Count(b + T_BR, 4, i), Count(GATED, 2, i), False)
            turn(Count(b + T_WO - 4), Count(GATED + KD - 2), True)
            for m in range(KD):
                if m + 1 < KD:
                    split_hi(act, Count(b + T_WO), m + 1)
                act.wait_ge(mix_done, N_TILES + m + 1)
                nc.scalar.activation(mix_y[:, m, :], ps[m % 4][:, :], ACT.Copy).then_inc(mix_left, 1)

        def branch_dve(dve, b):
            dve.wait_ge(sq_heads, MH * NB)
            nc.vector.tensor_scalar(m_cols[:, 1, :], m_cols[:, 0, :], 1.0 / MV, EPS, ALU.mult,
                                    ALU.add).then_inc(heads_mean, 1)
            dve.wait_ge(heads_root, 1)
            nc.vector.reciprocal(m_cols[:, 2, :], m_cols[:, 1, :]).then_inc(heads_inv, 1)
            dve.wait_ge(heads_inv, 1)
            for h in range(MH):
                nc.vector.tensor_tensor(hm[:, :, h, :], hm[:, :, h, :],
                                        m_cols[:, 2, h * NB:(h + 1) * NB].unsqueeze(2).to_broadcast([P, NB, MV]),
                                        ALU.mult).then_inc(hm_scaled, 1)

            def gated(m):
                dve.wait_ge(hm_turned, m + 1)
                dve.wait_ge(sig_made[m % 2], m // 2 + 1)
                if m >= 2:
                    dve.wait_ge(mlo_ready, m - 1)
                nc.vector.scalar_tensor_tensor(out=tmp[:, m % 2, :], in0=ps[m % 4][:, :], scalar=vecs[:, 64 + m:65 + m],
                                               in1=sig_in[:, m % 2, :], op0=ALU.mult, op1=ALU.mult
                                               ).then_inc(sig_free[m % 2], 1)

            def gated_lo(m):
                dve.wait_ge(hmhi_ready, m + 1)
                nc.vector.tensor_tensor(hm_lo[:, m, :], tmp[:, m % 2, :], hm_hi[:, m, :].bitcast(F32),
                                        ALU.subtract).then_inc(mlo_ready, 1)

            gated(0)
            for m in range(1, KD):
                gated(m)
                gated_lo(m - 1)
            gated_lo(KD - 1)
            for k in range(AH // 2):
                dve.wait_ge(ohi_ready, k + 1)
                nc.vector.tensor_tensor(o_lo[:, k, :], att_q[:, k, :], o_hi[:, k, :].bitcast(F32),
                                        ALU.subtract).then_inc(olo_ready, 1)
            dve.wait_ge(olo_ready, AH // 2)
            dve.wait_ge(hm_turned, KD)
            split_lo(dve, Count(b + T_BR), 0, WIDTH_A)

            def turn(c, g, n0, m, last):
                for j in range(2):
                    split_lo(dve, c, 2 * j + 1)
                    split_lo(dve, c, 2 * j + 2, 1024 if last and j else WIDTH_A)
                    dve.wait_ge(br_attn, n0.n(j + 1))
                    dve.wait_ge(sig_made[0], g.n(j + 1))
                    dve.wait_ge(mlo_ready, n0.n(KD + j))
                    nc.vector.tensor_tensor(tmp[:, 0, :], ps[2 * j][:, :], sig_in[:, 0, :],
                                            ALU.mult).then_inc(sig_free[0], 1)
                    dve.wait_ge(br_mlstm, n0.n(j + 1))
                    dve.wait_ge(sig_made[1], g.n(j + 1))
                    nc.vector.tensor_tensor(tmp[:, 1, :], ps[2 * j + 1][:, :], sig_in[:, 1, :],
                                            ALU.mult).then_inc(sig_free[1], 1)
                    dve.wait_ge(sig_free[0], g.n(j + 1))
                    dve.wait_ge(sig_free[1], g.n(j + 1))
                    nc.vector.tensor_tensor(tmp[:, 0, :], tmp[:, 0, :], tmp[:, 1, :], ALU.add).then_inc(br_sum, 1)
                    dve.wait_ge(br_sum, n0.n(j + 1))
                    hi = mg_hi[:, bass.ds(m + j, 1), :].rearrange("p a n -> p (a n)")
                    lo = mg_lo[:, bass.ds(m + j, 1), :].rearrange("p a n -> p (a n)")
                    copy(hi, tmp[:, 0, :]).then_inc(mghi_ready, 1)
                    dve.wait_ge(mghi_ready, n0.n(j + 1))
                    nc.vector.tensor_tensor(lo, tmp[:, 0, :], hi.bitcast(F32), ALU.subtract).then_inc(mlo_ready, 1)

            with dve.Fori(0, KD // 2 - 1) as i:
                turn(Count(b + T_BR, 4, i), Count(GATED, 2, i), Count(0, 2, i), i * 2, False)
            turn(Count(b + T_WO - 4), Count(GATED + KD - 2), Count(KD - 2), KD - 2, True)
            for m in range(1, KD):
                split_lo(dve, Count(b + T_WO), m)

        p_loaded, p_turned, phi_ready, plo_ready = (sem(x) for x in ("p_loaded", "p_turned", "phi_ready",
                                                                     "plo_ready"))
        PAIRS = 2 * GROUPS * GROUP

        def ple_sp(sp, b):
            W_G, W_P = t["w_ple_gate"][0], t["w_ple_proj"][0]
            load(sp, Count(b), 0, k_tiles(W_G, 0))
            load_part(sp, Count(b), 1, k_tiles(W_P, 0))
            sp.wait_ge(sum_done, 7)
            sp.dma_start(p_in[:, :, :], t["p"][0, 0].rearrange("(n q) c -> q n c", q=P)).then_inc(p_loaded, 16)
            with sp.Fori(0, KD // 2 - 1) as i:
                c = Count(b + 2, 4, i)
                for k in range(2):
                    load(sp, c, 2 * k, k_tiles(W_G, i * (2 * P) + (k + 1) * P))
                    load_part(sp, c, 2 * k + 1, k_tiles(W_P, i * (2 * P) + (k + 1) * P))
            load(sp, Count(b + 2 * KD - 2), 0, k_tiles(W_G, (KD - 1) * P))
            load_part(sp, Count(b + 2 * KD - 2), 1, k_tiles(W_P, (KD - 1) * P))

        def ple_pe(pe, b):
            pe.wait_ge(p_loaded, 16)
            pe.wait_ge(root_ready, 7)
            for k in range(PLE // P):
                for n in range(NB):
                    mm = nc.tensor.transpose(ps[1 + k][:, n * P:(n + 1) * P], p_in[:, n, k * P:(k + 1) * P],
                                             ident[:, :])
                mm.then_inc(p_turned, 1)
            pe.wait_ge(ulo_ready, 4 * KD)
            pe.wait_ge(plo_ready, PLE // P)
            with pe.Fori(0, KD // 2) as i:
                c = Count(b, 4, i)
                for j in range(2):
                    pe.wait_ge(wlo_ready, c.n(2 * j + 1))
                    pe.wait_ge(silu_done, Count(PAIRS + j - 1, 2, i).n())
                    product(ps[2 * j], [(c.slot(2 * j), k * P, u_hi[:, k, :], u_lo[:, k, :]) for k in range(KD)],
                            new_block=True).then_inc(gateup_done, 1)
                    pe.wait_ge(wlo_ready, c.n(2 * j + 2))
                    pe.wait_ge(prod_done, Count(PAIRS + j - 1, 2, i).n())
                    product(ps[2 * j + 1], [(c.slot(2 * j + 1), k * P, p_hi[:, k, :], p_lo[:, k, :])
                                            for k in range(PLE // P)], new_block=True).then_inc(gateup_done, 1)

        def ple_act(act, b):
            for k in range(PLE // P):
                act.wait_ge(p_turned, k + 1)
                nc.scalar.activation(p_hi[:, k, :], ps[1 + k][:, :], ACT.Copy).then_inc(phi_ready, 1)
            def turn(c, g, last):
                for j in range(2):
                    split_hi(act, c, 2 * j + 1, WIDTH_P)
                    act.wait_ge(gateup_done, 2 * g.n(j) + 1)
                    act.wait_ge(prod_done, g.n(j - 1))
                    nc.scalar.activation(tmp[:, j, :], ps[2 * j][:, :], ACT.Sigmoid).then_inc(silu_done, 1)
                    if not (last and j):
                        split_hi(act, c, 2 * j + 2)

            with act.Fori(0, KD // 2 - 1) as i:
                turn(Count(b, 4, i), Count(PAIRS, 2, i), False)
            turn(Count(b + 2 * KD - 4), Count(PAIRS + KD - 2), True)

        def ple_dve(dve, b):
            for k in range(PLE // P):
                dve.wait_ge(phi_ready, k + 1)
                nc.vector.tensor_tensor(p_lo[:, k, :], ps[1 + k][:, :], p_hi[:, k, :].bitcast(F32),
                                        ALU.subtract).then_inc(plo_ready, 1)
            def turn(c, g, m, last):
                for j in range(2):
                    split_lo(dve, c, 2 * j + 1, WIDTH_P)
                    if not (last and j):
                        split_lo(dve, c, 2 * j + 2)
                    dve.wait_ge(silu_done, g.n(j + 1))
                    dve.wait_ge(gateup_done, 2 * g.n(j) + 2)
                    nc.vector.tensor_tensor(yacc[:, bass.ds(m + j, 1), :].rearrange("p a n -> p (a n)"),
                                            tmp[:, j, :], ps[2 * j + 1][:, :], ALU.mult).then_inc(prod_done, 1)

            with dve.Fori(0, KD // 2 - 1) as i:
                turn(Count(b, 4, i), Count(PAIRS, 2, i), i * 2, False)
            turn(Count(b + 2 * KD - 4), Count(PAIRS + KD - 2), KD - 2, True)

        vecs_copied = sem("vecs_copied")
        bias_zero = sem("bias_zero")
        B_MIX = BLOCKS_FFN
        B_FFN2 = B_MIX + T_END
        B_PLE = B_FFN2 + BLOCKS_FFN

        block = ctx.enter_context(nc.Block())

        @block.gpsimd
        def _(pool):
            nc.gpsimd.memset(ident[:, :], 0.0).then_inc(ident_zero, 1)
            pool.wait_ge(ident_zero, 1)
            nc.gpsimd.affine_select(out=ident[:, :], in_=ident[:, :], compare_op=ALU.not_equal, fill=1.0, base=0,
                                    pattern=[[-1, P]], channel_multiplier=1).then_inc(consts_ready, 1)
            nc.gpsimd.memset(band[:, :], 0.0).then_inc(ident_zero, 1)
            pool.wait_ge(ident_zero, 2)
            nc.gpsimd.memset(band[:, NB - 1:NB], 1.0).then_inc(consts_ready, 1)
            nc.gpsimd.memset(eps[:, :], EPS).then_inc(consts_ready, 1)
            nc.gpsimd.memset(gate_bias[:, :], 0.0).then_inc(bias_zero, 1)
            nc.gpsimd.memset(q_st[:, :, :, :], 0.0).then_inc(qst_zero, 1)
            pool.wait_ge(x_kept, KD)
            for m in range(KD):
                nc.gpsimd.memset(yacc[:, m, :], 0.0).then_inc(y_added, 1)
            pair_pool(pool, 1)
            post_pool(pool, 1, yacc)
            pool.wait_ge(rope_done, AH // 2 + 1)
            nc.gpsimd.memset(m_v[:, :, :, MV:MV + 1], 1.0).then_inc(ones_v, 1)
            pool.wait_ge(vt_done, 1)
            for side in (slice(0, TAPS // 2), slice(TAPS // 2 + S, S + TAPS - 1)):
                op = nc.gpsimd.memset(zpad[:, :, side], 0.0)
            op.then_inc(pad_zero, 1)
            pair_pool(pool, 3)
            pool.wait_ge(mix_left, N_TILES + KD)
            pool.wait_ge(resid_back, 16 * KD)
            post_pool(pool, 3, mix_y)
            for m in range(KD):
                nc.gpsimd.memset(yacc[:, m, :], 0.0).then_inc(y_added, 1)
            pair_pool(pool, 5)
            post_pool(pool, 5, yacc)
            pair_pool(pool, 7)
            post_pool(pool, 7, yacc)

        @block.sync
        def _(sp):
            for j in range(KD):
                sp.dma_start(x_in[:, j, :], t["x"][0, j * P:(j + 1) * P, :]).then_inc(x_loaded, 16)
            rows = 0
            for src in [t[name] for name in NORMS] + [t["mlstm_norm"], t["conv_b"], t["conv_w"]]:
                src = src.rearrange("a (k p) -> (a k) p", p=P) if len(src.shape) == 2 else \
                    src.rearrange("a c (k p) -> (a c k) p", p=P)
                sp.dma_start(vec_rows[rows:rows + src.shape[0], :], src).then_inc(vecs_loaded, 16)
                rows += src.shape[0]
            sp.dma_start(sinks[:, :], t["attn_sink"].to_broadcast([P, AH])).then_inc(small_loaded, 16)
            sp.wait_ge(bias_zero, 1)
            by_head = t["b_gates"].rearrange("a (w g h) -> w (a h) g", w=2, g=2)
            for way in range(2):
                sp.dma_start(gate_bias[32 * way:32 * way + MH, :], by_head[way],
                             allow_slow_non_contiguous=True).then_inc(small_loaded, 16)
            ffn_sp(sp, 0, 0, "ffn1_w1", "ffn1_w2")
            mix_sp(sp, B_MIX)
            branch_sp(sp, B_MIX)
            ffn_sp(sp, 1, B_FFN2, "ffn2_w1", "ffn2_w2")
            ple_sp(sp, B_PLE)
            for j in range(KD):
                sp.wait_ge(out_copied, j + 1)
                sp.dma_start(out[0, j * P:(j + 1) * P, :], x_out[:, j, :]).then_inc(stored, 16)
            sp.wait_ge(stored, 16 * KD)

        @block.scalar
        def _(act):
            for k in range(0, KD, 2):
                act.wait_ge(x_turned, k + 1)
                if k:
                    act.wait_ge(x_kept, k)
                nc.scalar.copy(resid[:, k, :], ps[k % 4][:, :]).then_inc(x_kept, 1)
            for k in range(2):
                split_hi(act, Count(0), k)
            square_act(act, 0, resid)
            root_act(act, 0)
            pre_act(act, 0)
            ffn_act(act, 0, 0)

            act.wait_ge(raw_q[0], 16)
            split_hi(act, Count(B_MIX), 0)
            square_act(act, 1, yacc)
            act.wait_ge(raw_q[1], 16)
            split_hi(act, Count(B_MIX), 1)
            root_act(act, 1)
            square_act(act, 2, resid)
            root_act(act, 2)
            pre_act(act, 2)
            mix_act(act, B_MIX)
            mlstm_act(act)
            branch_act(act, B_MIX)

            split_hi(act, Count(B_FFN2), 0)
            square_act(act, 3, mix_y)
            split_hi(act, Count(B_FFN2), 1)
            root_act(act, 3)
            square_act(act, 4, resid)
            root_act(act, 4)
            pre_act(act, 4)
            ffn_act(act, 1, B_FFN2)

            split_hi(act, Count(B_PLE), 0)
            square_act(act, 5, yacc)
            root_act(act, 5)
            square_act(act, 6, resid)
            root_act(act, 6)
            pre_act(act, 6)
            ple_act(act, B_PLE)
            square_act(act, 7, yacc)
            root_act(act, 7)

        @block.vector
        def _(dve):
            for k in range(1, KD, 2):
                dve.wait_ge(x_turned, k + 1)
                dve.wait_ge(x_kept, k)
                nc.vector.tensor_copy(resid[:, k, :], ps[k % 4][:, :]).then_inc(x_kept, 1)
            dve.wait_ge(vecs_turned, 1)
            nc.vector.tensor_copy(vecs[:, :], ps[0][:, 0:VEC_ROWS]).then_inc(vecs_ready, 1)
            dve.wait_ge(vecs_ready, 1)
            for n in (1, 5):
                nc.vector.tensor_scalar(gains[:, n, :], gains[:, n, :], 0.5, None, ALU.mult).then_inc(gains_halved, 1)
            for k in range(2):
                split_lo(dve, Count(0), k)
            pre_dve(dve, 0)
            ffn_dve(dve, 0, 0)

            split_lo(dve, Count(B_MIX), 0)
            split_lo(dve, Count(B_MIX), 1)
            dve.wait_ge(gains_halved, 2)
            post_dve(dve, 1, yacc)
            pre_dve(dve, 2)
            mix_dve(dve, B_MIX)
            mlstm_dve(dve)
            branch_dve(dve, B_MIX)

            split_lo(dve, Count(B_FFN2), 0)
            split_lo(dve, Count(B_FFN2), 1)
            post_dve(dve, 3, mix_y)
            pre_dve(dve, 4)
            ffn_dve(dve, 1, B_FFN2)

            split_lo(dve, Count(B_PLE), 0)
            post_dve(dve, 5, yacc)
            pre_dve(dve, 6)
            ple_dve(dve, B_PLE)
            post_dve(dve, 7, yacc)
            for j in range(KD):
                dve.wait_ge(out_turned, j + 1)
                nc.vector.tensor_copy(x_out[:, j, :], ps[j % 4][:, :]).then_inc(out_copied, 1)

        @block.tensor
        def _(pe):
            pe.wait_ge(consts_ready, 3)
            pe.wait_ge(x_loaded, 16 * KD)
            for k in range(KD):
                if k >= 4:
                    pe.wait_ge(x_kept, k - 3)
                for j in range(KD):
                    mm = nc.tensor.transpose(ps[k % 4][:, j * P:(j + 1) * P], x_in[:, j, k * P:(k + 1) * P],
                                             ident[:, :])
                mm.then_inc(x_turned, 1)
            pe.wait_ge(vecs_loaded, 16 * 11)
            pe.wait_ge(x_kept, 5)
            nc.tensor.transpose(ps[0][:, 0:VEC_ROWS], vec_rows[:, :], ident[0:VEC_ROWS, 0:VEC_ROWS]).then_inc(vecs_turned, 1)
            pe.wait_ge(x_kept, KD)
            norm_pe(pe, 0)
            ffn_pe(pe, 0, 0, 0)
            pe.wait_ge(y_added, KD * (GROUPS + 1) - 1)
            norm_pe(pe, 1, new_block=True)
            norm_pe(pe, 2)
            mix_pe(pe, B_MIX, 1)
            mlstm_pe(pe)
            branch_pe(pe, B_MIX)
            pe.wait_ge(mix_left, N_TILES + KD - 1)
            norm_pe(pe, 3, new_block=True)
            norm_pe(pe, 4)
            ffn_pe(pe, 1, B_FFN2, 2)
            pe.wait_ge(y_added, 2 * KD * (GROUPS + 1) - 1)
            norm_pe(pe, 5)
            norm_pe(pe, 6)
            ple_pe(pe, B_PLE)
            pe.wait_ge(silu_done, PAIRS + KD - 1)
            norm_pe(pe, 7)
            for k in range(KD):
                resid_wait(pe, 3, k)
            for j in range(KD):
                if j >= 4:
                    pe.wait_ge(out_copied, j - 3)
                for k in range(KD):
                    mm = nc.tensor.transpose(ps[j % 4][:, k * P:(k + 1) * P], resid[:, k, j * P:(j + 1) * P],
                                             ident[:, :])
                mm.then_inc(out_turned, 1)


def tables():
    import numpy as np

    f = np.float32
    p, c = np.arange(P)[:, None], np.arange(P)[None, :]
    made = {"ident": p == c}
    d = np.arange(P) % AD
    partner = np.where(d < ROPE // 2, np.arange(P) + ROPE // 2, np.arange(P) - ROPE // 2)
    partner = np.where(d < ROPE, partner, np.arange(P))
    made["perm"] = p == partner[None, :]
    key = np.arange(WINDOW)[None, :] - P
    made["window"] = np.where(np.abs(key - p) <= P, 0, -BLOCKED)
    made["later"] = np.where(p <= c, 0, BLOCKED)
    made["earlier"] = np.where(p >= c, 0, BLOCKED)
    chains = np.zeros((P, 2, MH, P))
    for way in range(2):
        for h in range(MH):
            chains[32 * way + h, way, h] = 1
    made["chains"] = chains.reshape(P, -1)
    inv = f(THETA) ** (-np.arange(0, ROPE, 2, dtype=f) / f(ROPE))
    angle = (np.arange(S, dtype=f)[:, None] * inv[None, :]).astype(f)
    cos, sin = np.ones((P, S)), np.zeros((P, S))
    for n in range(P):
        if n % AD < ROPE:
            cos[n] = np.cos(angle[:, n % AD % (ROPE // 2)])
            sin[n] = np.sin(angle[:, n % AD % (ROPE // 2)]) * (-1 if n % AD < ROPE // 2 else 1)
    made["cos"], made["sin"] = cos, sin
    token = np.arange(S)[None, :] % P
    made["inside"] = np.where(p < 32, token != 0, token != P - 1)
    return {"tables": np.concatenate([np.broadcast_to(made[n], (P, w)).astype(f) for n, (_, w) in TABLE.items()], 1)}


_INS = ['x', 'p', 'ffn1_norm_pre', 'ffn1_w1', 'ffn1_w2', 'ffn1_norm_post', 'mix_norm_pre', 'w_in', 'b_gates',
        'conv_w', 'conv_b', 'attn_sink', 'mlstm_norm', 'w_branch_attn', 'w_branch_mlstm', 'w_out', 'mix_norm_post',
        'ffn2_norm_pre', 'ffn2_w1', 'ffn2_w2', 'ffn2_norm_post', 'ple_norm_pre', 'w_ple_gate', 'w_ple_proj',
        'ple_norm_post']


def kernel(**inputs):
    import numpy as np
    import concourse.bacc as bacc
    from concourse.bass_utils import run_bass_kernel_spmd

    nc = bacc.Bacc("TRN2", target_bir_lowering=False, num_devices=1)
    arrays, args = {}, {}
    for name in _INS:
        arrays[name] = np.ascontiguousarray(inputs[name])
        args[name] = nc.dram_tensor(name, arrays[name].shape, F32, kind="ExternalInput").ap()
    for name, array in tables().items():
        arrays[name] = array
        args[name] = nc.dram_tensor(name, array.shape, F32, kind="ExternalInput").ap()
    out = nc.dram_tensor("out", (1, S, D), F32, kind="ExternalOutput").ap()
    build(nc, args, out)
    r = run_bass_kernel_spmd(nc, [arrays], core_ids=[0])
    return r.results[0]["out"]
```

```python
from contextlib import ExitStack

import concourse.bass as bass
from concourse import mybir
from concourse.alu_op_type import AluOpType as ALU

F32 = mybir.dt.float32
F32R = mybir.dt.float32r
ACT = mybir.ActivationFunctionType

P = 128
D = 1024
S = 1024
KD = D // P
HALF = 512
FFN = 2816
GROUP = 2
GROUPS = FFN // (GROUP * P)
EPS = 1e-6
NB = S // P

AH, AKV, AD = 8, 2, 64
ATT_SCALE = AD ** -0.5
WINDOW = 3 * P
ROPE = AD // 4
THETA = 500000.0
BLOCKED = 1e30

MH, MD, MV = 4, 128, 256
TAPS = 5
PLE = 256
CHAIN_ROWS = 64
K_SCALE = MD ** -0.5

C_AQ = 0
C_AK = C_AQ + AH * AD
C_AV = C_AK + AKV * AD
C_MQK = C_AV + AKV * AD
C_MV = C_MQK + 2 * MH * MD
C_MO = C_MV + MH * MV
C_MG = C_MO + MH * MV
C_BG = C_MG + 4 * MH

TABLE = {}
for _name, _width in (("ident", P), ("perm", P), ("window", WINDOW), ("later", P), ("earlier", P),
                      ("chains", 2 * MH * P), ("cos", S), ("sin", S), ("inside", S)):
    TABLE[_name] = (sum(w for _, w in TABLE.values()), _width)
TABLE_WIDTH = sum(w for _, w in TABLE.values())

N_QKV = 6
T_MQK = N_QKV
T_MV = T_MQK + KD
T_SIG = T_MV + KD
T_MG = T_SIG + 2 * KD
T_GM = T_MG + 1
N_TILES = T_GM + KD
KB = 1024
RING = 2
VEC_ROWS = 120
NORMS = ['ffn1_norm_pre', 'ffn1_norm_post', 'mix_norm_pre', 'mix_norm_post', 'ffn2_norm_pre', 'ffn2_norm_post',
         'ple_norm_pre', 'ple_norm_post']


class Count:

    def __init__(self, base, per=0, turn=None):
        self.base, self.per, self.turn = base, per, turn

    def n(self, k=0):
        return self.base + k if self.turn is None else self.turn * self.per + (self.base + k)

    def slot(self, k=0):
        return (self.base + k) % RING

    def uses(self, k=0):
        first = (self.base + k) // RING + 1
        return first if self.turn is None else self.turn * (self.per // RING) + first


def build(nc, t, out):
    with ExitStack() as ctx:
        base = (nc.sbuf_base + 63) // 64 * 64


        def at(name, kb, shape, dt=F32):
            return nc.alloc_sbuf_tensor_at(name, shape, dt, offset=base + int(kb * KB))

        def sem(name):
            return ctx.enter_context(nc.semaphore(name))

        resid = at("resid", 0, [P, KD, S])
        u_hi = at("u_hi", 32, [P, KD, S], F32R)
        u_lo = at("u_lo", 64, [P, KD, S], F32R)
        w_raw = at("w_raw", 96, [P, RING, 1024])
        w_hi = at("w_hi", 104, [P, RING, 1024], F32R)
        w_lo = at("w_lo", 112, [P, RING, 1024], F32R)
        tmp = at("tmp", 120, [P, 2, S])
        ident = at("ident", 132.25, [P, P])
        band = at("band", 132.75, [P, 2 * NB - 1])
        eps = at("eps", 132.875, [P, 1])
        x_sums = at("x_sums", 132.9375, [P, NB])
        vec_rows = at("vec_rows", 133.75, [VEC_ROWS, P])
        vecs = at("vecs", 134.25, [P, VEC_ROWS])
        gains = vecs[:, 0:8 * KD].rearrange("p (n k) -> p n k", n=8)
        rinv = at("rinv", 133.25, [NB, P])
        yacc = at("yacc", 142, [P, KD, S])
        hid_hi = at("hid_hi", 174, [P, 2, GROUP, S], F32R)
        hid_lo = at("hid_lo", 190, [P, 2, GROUP, S], F32R)
        sq = at("sq", 174, [P, KD, S])
        x_in = at("x_in", 142, [P, KD, D])
        x_out = at("x_out", 174, [P, KD, D])

        ps = [ctx.enter_context(nc.psum_tensor(f"acc{n}", [P, S], F32)) for n in range(4)]

        x_loaded = [sem(f"x_loaded{j}") for j in range(NB)]
        consts_ready = sem("consts_ready")
        ident_zero = sem("ident_zero")
        vecs_loaded = sem("vecs_loaded")
        vecs_turned = sem("vecs_turned")
        vecs_ready = sem("vecs_ready")
        gains_halved = sem("gains_halved")
        x_turned = sem("x_turned")
        x_kept = sem("x_kept")
        raw_loaded = [sem(f"raw_loaded{n}") for n in range(RING)]
        whi_ready = sem("whi_ready")
        wlo_ready = sem("wlo_ready")
        block_used = sem("block_used")
        gateup_done = sem("gateup_done")
        silu_done = sem("silu_done")
        prod_done = sem("prod_done")
        hhi_ready = sem("hhi_ready")
        hid_ready = sem("hid_ready")
        y_done = sem("y_done")
        y_added = sem("y_added")
        sq_ready = sem("sq_ready")
        sq_pair = sem("sq_pair")
        sq_last = sem("sq_last")
        sum_done = sem("sum_done")
        root_ready = sem("root_ready")
        rinv_ready = sem("rinv_ready")
        spread_done = sem("spread_done")
        u_made = sem("u_made")
        uhi_ready = sem("uhi_ready")
        ulo_ready = sem("ulo_ready")
        post_made = sem("post_made")
        resid_dve = sem("resid_dve")
        resid_pool = sem("resid_pool")
        out_turned = sem("out_turned")
        out_copied = [sem(f"out_copied{n}") for n in range(2)]
        stored = sem("stored")

        def w1_block(name, cols):
            return t[name][0, :, cols].rearrange("(k p) n -> p k n", p=P)

        def w2_block(name, rows, half):
            return t[name][0, rows, half * 512:half * 512 + 512].rearrange("(k p) n -> p k n", p=P)

        def load(sp, c, k, src):
            if c.base + k >= RING:
                sp.wait_ge(wlo_ready, c.n(k - RING + 1))
            s = c.slot(k)
            nk = src.shape[1]
            sp.dma_start(w_raw[:, s, :].rearrange("p (k n) -> p k n", k=nk), src).then_inc(raw_loaded[s], 16)

        def split_hi(act, c, k, width=1024):
            act.wait_ge(raw_loaded[c.slot(k)], c.uses(k) * 16)
            if c.base + k >= RING:
                act.wait_ge(block_used, c.n(k - RING + 1))
            nc.scalar.activation(w_hi[:, c.slot(k), 0:width], w_raw[:, c.slot(k), 0:width], ACT.Copy
                                 ).then_inc(whi_ready, 1)

        def split_lo(dve, c, k, width=1024):
            s = c.slot(k)
            dve.wait_ge(whi_ready, c.n(k + 1))
            nc.vector.tensor_tensor(w_lo[:, s, 0:width], w_raw[:, s, 0:width], w_hi[:, s, 0:width].bitcast(F32),
                                    ALU.subtract).then_inc(wlo_ready, 1)

        def product(acc, terms, first=True, last=True, new_block=False):
            for n, (s, off, a_hi, a_lo) in enumerate(terms):
                hi, lo = w_hi[:, s, off:off + P], w_lo[:, s, off:off + P]
                for h in range(2):
                    cols = slice(h * HALF, (h + 1) * HALF)
                    mm = nc.tensor.matmul(acc[:, cols], hi, a_hi[:, cols], start=(first and n == 0), stop=False)
                    if new_block and n == 0 and h == 0:
                        mm.then_inc(block_used, 1)
                    nc.tensor.matmul(acc[:, cols], hi, a_lo[:, cols], start=False, stop=False)
                    mm = nc.tensor.matmul(acc[:, cols], lo, a_hi[:, cols], start=False,
                                          stop=(last and n == len(terms) - 1))
            return mm

        def product_as_ready(pe, acc, terms, ready, new_block=False):
            for n, term in enumerate(terms):
                for wait in ready[n]:
                    pe.wait_ge(*wait)
                mm = product(acc, [term], first=(n == 0), last=(n == len(terms) - 1),
                             new_block=(new_block and n == 0))
            return mm

        def first_pair(pe, c, pre, done):
            for k in range(KD):
                pe.wait_ge(ulo_ready, KD * pre + k + 1)
                for j in range(2):
                    if k == 0:
                        pe.wait_ge(wlo_ready, c.n(j + 1))
                    mm = product(ps[j], [(c.slot(j), k * P, u_hi[:, k, :], u_lo[:, k, :])], first=(k == 0),
                                 last=(k == KD - 1), new_block=(j == 1 and k == KD - 1))
                    if k == KD - 1:
                        mm.then_inc(done, 1)

        ADDS = 4

        POOL_TILES = (1, 2, 4, 6)

        def resid_wait(eng, post, k):
            before = len([j for j in range(k + 1) if (j in POOL_TILES) == (k in POOL_TILES)])
            eng.wait_ge(resid_pool if k in POOL_TILES else resid_dve, KD // 2 * post + before)

        def norm_src_wait(eng, n, k):
            if n % 2 == 0:
                resid_wait(eng, n // 2 - 1, k)
            elif n == 3:
                eng.wait_ge(mix_left, N_TILES + k + 1)
            elif n == 7:
                eng.wait_ge(gateup_done, 4 * GROUPS * GROUP + 2 * KD - 1)
                eng.wait_ge(prod_done, 2 * GROUPS * GROUP + k + 1)
            else:
                eng.wait_ge(y_added, KD * (GROUPS + 1) * (n // 4 + 1) - KD + min(k + 1 + k // 6, KD))

        def sums(n):
            return ps[{0: 3, 7: 0}.get(n, 2)][0:NB, 0:P]

        RINV = ps[3]
        OUT = ps[0:3]

        def place(n, k):
            return [2, 3, 6, 7, 3, 7, 0, 1][k] if n % 2 else k

        def square_tile(n, k):
            return yacc[:, k, :] if n == 6 else sq[:, place(n, k), :]

        def square_act(act, n, src, tiles=range(KD)):
            for k in tiles:
                norm_src_wait(act, n, k)
                if n % 2 and k in (4, 5):
                    act.wait_ge(sq_pair, ADDS * (n // 2) + k - 3)
                nc.scalar.activation(square_tile(n, k), src[:, k, :], ACT.Square).then_inc(sq_ready, 1)

        def pair_pool(pool, n):
            for i, (a, b) in enumerate(((0, 1), (2, 3), (4, 5))):
                pool.wait_ge(sq_ready, KD * n + b + 1)
                a, b = place(n, a), place(n, b)
                nc.gpsimd.tensor_tensor(sq[:, a, :], sq[:, a, :], sq[:, b, :], ALU.add).then_inc(sq_pair, 1)
            pool.wait_ge(sq_pair, ADDS * (n // 2) + 3)
            a, b = place(n, 0), place(n, 2)
            nc.gpsimd.tensor_tensor(sq[:, a, :], sq[:, a, :], sq[:, b, :], ALU.add).then_inc(sq_pair, 1)

        def tokens_act(act):
            for j in range(NB):
                act.wait_ge(x_loaded[j], 16)
                nc.scalar.activation(sq[:, j, :], x_in[:, j, :], ACT.Square, accum_out=x_sums[:, j:j + 1]
                                     ).then_inc(sq_ready, 1)

        def norm0_pe(pe):
            pe.wait_ge(sq_ready, NB)
            nc.tensor.transpose(sums(0), x_sums[:, :], ident[:, :]).then_inc(sum_done, 1)

        def norm_pe(pe, n, new_block=False):
            tiles = [4, 6, 7, 0] if n % 2 else range(KD - 1)
            for k in tiles:
                if n % 2 and k < 6:
                    pe.wait_ge(sq_pair, ADDS * (n // 2) + (3 if k else 4))
                elif n % 2 == 0 and k == KD - 2:
                    pe.wait_ge(sq_last, n // 2)
                else:
                    pe.wait_ge(sq_ready, KD * n + k + 1)
                for j in range(NB):
                    mm = nc.tensor.matmul(sums(n), band[:, NB - 1 - j:2 * NB - 1 - j],
                                          square_tile(n, k)[:, j * P:(j + 1) * P], start=(k == tiles[0] and j == 0),
                                          stop=(k == tiles[-1] and j == NB - 1))
                    if new_block and k == tiles[0] and j == 0:
                        mm.then_inc(block_used, 1)
            mm.then_inc(sum_done, 1)
            spread_pe(pe, n)

        def spread_pe(pe, n):
            pe.wait_ge(rinv_ready, n + 1)
            for j in range(NB):
                mm = nc.tensor.matmul(RINV[:, j * P:(j + 1) * P], ident[0:NB, j:j + 1].to_broadcast([NB, P]),
                                      rinv[:, :], start=True, stop=True)
            mm.then_inc(spread_done, 1)

        def root_act(act, n):
            act.wait_ge(sum_done, n + 1)
            nc.scalar.activation(rinv[:, :], sums(n), ACT.Sqrt, bias=eps[0:NB, :], scale=1.0 / D
                                 ).then_inc(root_ready, 1)

        def invert_dve(dve, n):
            dve.wait_ge(root_ready, n + 1)
            nc.vector.reciprocal(rinv[:, :], rinv[:, :]).then_inc(rinv_ready, 1)

        def pre_dve(dve, n):
            pre = n // 2
            if n:
                invert_dve(dve, n)
            dve.wait_ge(spread_done, n + 1)
            for k in range(KD):
                if KD * pre + k >= 2:
                    dve.wait_ge(ulo_ready, KD * pre + k - 1)
                nc.vector.scalar_tensor_tensor(out=tmp[:, k % 2, :], in0=resid[:, k, :], scalar=gains[:, n, k:k + 1],
                                               in1=RINV[:, :], op0=ALU.mult, op1=ALU.mult).then_inc(u_made, 1)
                if k:
                    pre_lo(dve, pre, k - 1)
            pre_lo(dve, pre, KD - 1)

        def pre_lo(dve, pre, k):
            dve.wait_ge(uhi_ready, KD * pre + k + 1)
            nc.vector.tensor_tensor(u_lo[:, k, :], tmp[:, k % 2, :], u_hi[:, k, :].bitcast(F32),
                                    ALU.subtract).then_inc(ulo_ready, 1)

        def pre_act(act, n):
            pre = n // 2
            for k in range(KD):
                act.wait_ge(u_made, KD * pre + k + 1)
                nc.scalar.activation(u_hi[:, k, :], tmp[:, k % 2, :], ACT.Copy).then_inc(uhi_ready, 1)

        def post_dve(dve, n, y):
            post = n // 2
            invert_dve(dve, n)
            dve.wait_ge(spread_done, n + 1)
            for k in range(KD):
                nc.vector.scalar_tensor_tensor(out=y[:, k, :], in0=y[:, k, :], scalar=gains[:, n, k:k + 1],
                                               in1=RINV[:, :], op0=ALU.mult, op1=ALU.mult).then_inc(post_made, 1)
                if k not in POOL_TILES:
                    post_add(dve, nc.vector, post, k, y, resid_dve)
            if n < 7:
                dve.wait_ge(sq_ready, KD * (n + 2))
                a, b = square_tile(n + 1, KD - 2), square_tile(n + 1, KD - 1)
                nc.vector.tensor_tensor(a, a, b, ALU.add).then_inc(sq_last, 1)

        def post_pool(pool, n, y):
            for k in POOL_TILES:
                post_add(pool, nc.gpsimd, n // 2, k, y, resid_pool)

        def post_add(eng, engine, post, k, y, done):
            eng.wait_ge(post_made, KD * post + k + 1)
            engine.tensor_tensor(resid[:, k, :], resid[:, k, :], y[:, k, :], ALU.add).then_inc(done, 1)

        BLOCKS_FFN = GROUPS * 6

        def ffn_sp(sp, f, b, w1, w2):
            def s1(c, k, col):
                for j in range(GROUP):
                    load(sp, c, k + 2 * j, w1_block(w1, bass.ds(col + j * P, P)))
                    load(sp, c, k + 2 * j + 1, w1_block(w1, bass.ds(col + FFN + j * P, P)))

            def s2(c, k, row):
                for h in range(2):
                    load(sp, c, k + h, w2_block(w2, bass.ds(row, GROUP * P), h))

            W = GROUP * P
            s1(Count(b), 0, 0)
            with sp.Fori(0, GROUPS // 2) as i:
                c = Count(b + 4, 12, i)
                s1(c, 0, i * (2 * W) + W)
                s2(c, 4, i * (2 * W))
                s1(c, 6, i * (2 * W) + 2 * W)
                s2(c, 10, i * (2 * W) + W)
            s2(Count(b + BLOCKS_FFN - 2), 0, (GROUPS - 1) * W)

        def ffn_act(act, f, b):
            def s1(c, g, k, first=False):
                if not first:
                    split_hi(act, c, k + 1)
                split_hi(act, c, k + 2)
                for j in range(GROUP):
                    act.wait_ge(gateup_done, g.n() * 4 + 2 * j + 1)
                    if g.base * GROUP + j >= 2:
                        act.wait_ge(hid_ready, g.n() * GROUP + j - 1)
                    nc.scalar.activation(tmp[:, j, :], ps[2 * j][:, :], ACT.Silu).then_inc(silu_done, 1)
                    split_hi(act, c, k + 3 + j)

            def s2(c, k, more=True):
                split_hi(act, c, k + 1)
                if more:
                    split_hi(act, c, k + 2)

            s1(Count(b), Count(f * GROUPS), 0, first=True)
            with act.Fori(0, GROUPS // 2) as i:
                c = Count(b + 4, 12, i)
                s1(c, Count(f * GROUPS + 1, 2, i), 0)
                s2(c, 4)
                s1(c, Count(f * GROUPS + 2, 2, i), 6)
                s2(c, 10)
            s2(Count(b + BLOCKS_FFN - 2), 0, more=False)

        def ffn_dve(dve, f, b):
            def hidden(g, j):
                dve.wait_ge(silu_done, g.n() * 2 + j + 1)
                dve.wait_ge(gateup_done, g.n() * 4 + 2 * j + 2)
                par = (g.base - f * GROUPS) % 2
                nc.vector.tensor_tensor(tmp[:, j, :], tmp[:, j, :], ps[2 * j + 1][:, :],
                                        ALU.mult).then_inc(prod_done, 1)
                dve.wait_ge(prod_done, g.n() * 2 + j + 1)
                nc.vector.tensor_copy(hid_hi[:, par, j, :], tmp[:, j, :]).then_inc(hhi_ready, 1)
                dve.wait_ge(hhi_ready, g.n() * 2 + j + 1)
                nc.vector.tensor_tensor(hid_lo[:, par, j, :], tmp[:, j, :], hid_hi[:, par, j, :].bitcast(F32),
                                        ALU.subtract).then_inc(hid_ready, 1)

            def add_y(g, m):
                dve.wait_ge(y_done, g.n() * KD + m + 1)
                dve.wait_ge(y_added, g.n() * KD + KD * f + m + 1)
                nc.vector.tensor_tensor(yacc[:, m, :], yacc[:, m, :], ps[m % 4][:, :], ALU.add).then_inc(y_added, 1)

            def s1(c, g, k, y=None, first=False):
                if not first:
                    split_lo(dve, c, k + 1)
                if y is not None:
                    add_y(y, KD - 1)
                split_lo(dve, c, k + 2)
                split_lo(dve, c, k + 3)
                hidden(g, 0)
                split_lo(dve, c, k + 4)

            def s2(c, g, y, k, more=True):
                split_lo(dve, c, k + 1)
                if g is not None:
                    hidden(g, 1)
                for m in range(3):
                    add_y(y, m)
                if more:
                    split_lo(dve, c, k + 2)
                for m in range(3, KD - 1):
                    add_y(y, m)

            G = f * GROUPS
            s1(Count(b), Count(G), 0, first=True)
            hidden(Count(G), 1)
            with dve.Fori(0, GROUPS // 2) as i:
                c = Count(b + 4, 12, i)
                s1(c, Count(G + 1, 2, i), 0)
                s2(c, Count(G + 1, 2, i), Count(G, 2, i), 4)
                s1(c, Count(G + 2, 2, i), 6, y=Count(G, 2, i))
                s2(c, Count(G + 2, 2, i), Count(G + 1, 2, i), 10)
                add_y(Count(G + 1, 2, i), KD - 1)
            s2(Count(b + BLOCKS_FFN - 2), None, Count(G + GROUPS - 1), 0, more=False)
            add_y(Count(G + GROUPS - 1), KD - 1)

        def ffn_pe(pe, f, b, pre):
            def s1(c, g, k, first=False):
                if first:
                    first_pair(pe, c, pre, gateup_done)
                for n in range(2 if first else 0, 4):
                    pe.wait_ge(wlo_ready, c.n(k + n + 1))
                    if not first:
                        pe.wait_ge(y_added, (g.n() - 1) * KD + KD * f + 4 + n + 1)
                    product(ps[n], [(c.slot(k + n), kk * P, u_hi[:, kk, :], u_lo[:, kk, :])
                                    for kk in range(KD)], new_block=True).then_inc(gateup_done, 1)

            def s2(c, g, k, last_s1):
                par = (g.base - f * GROUPS) % 2
                pe.wait_ge(hid_ready, g.n() * GROUP + GROUP)
                for m in range(KD):
                    h = m // 4
                    if m % 4 == 0:
                        pe.wait_ge(wlo_ready, c.n(k + h + 1))
                    if m < 4:
                        if last_s1 is not None:
                            if m % 2 == 0:
                                pe.wait_ge(silu_done, last_s1.n() * GROUP + m // 2 + 1)
                            else:
                                pe.wait_ge(prod_done, last_s1.n() * GROUP + m // 2 + 1)
                        else:
                            pe.wait_ge(y_added, g.n() * KD + KD * f + 4 + m + 1)
                    else:
                        pe.wait_ge(y_added, g.n() * KD + KD * (f + 1) + m - 4 + 1)
                    mm = product(ps[m % 4], [(c.slot(k + h), j * 512 + (m % 4) * P, hid_hi[:, par, j, :],
                                              hid_lo[:, par, j, :]) for j in range(GROUP)],
                                 new_block=(m % 4 == 0))
                    mm.then_inc(y_done, 1)

            G = f * GROUPS
            s1(Count(b), Count(G), 0, first=True)
            with pe.Fori(0, GROUPS // 2) as i:
                c = Count(b + 4, 12, i)
                s1(c, Count(G + 1, 2, i), 0)
                s2(c, Count(G, 2, i), 4, Count(G + 1, 2, i))
                s1(c, Count(G + 2, 2, i), 6)
                s2(c, Count(G + 1, 2, i), 10, Count(G + 2, 2, i))
            s2(Count(b + BLOCKS_FFN - 2), Count(G + GROUPS - 1), 0, None)

        mqk = at("mqk", 0, [P, 2 * MH, S])
        zpad = at("zpad", 120, [P, 2, S + TAPS - 1])
        rope_t = at("rope_t", 128.25, [P, S])
        att_q = at("att_q", 142, [P, AH // 2, S])
        att_k = at("att_k", 158, [P, S])
        att_v = at("att_v", 162, [P, NB, P])
        cos_sb = at("cos_sb", 166, [P, S])
        sin_sb = at("sin_sb", 170, [P, S])
        m_v = at("m_v", 166, [P, NB, MH, MV + 1])
        q_st = at("q_st", 136, [P, 2, AH // 2, P])
        window = at("window", 140, [P, WINDOW])
        perm = at("perm", 141.5, [P, P])
        PROBS = 4
        prob = [at(f"prob{n}", [199, 200.5, 128.25, 129.75][n], [P, WINDOW]) for n in range(PROBS)]
        prob_t = at("prob_t", 202, [P, 2, WINDOW])
        o_sb = at("o_sb", 205, [P, AH * AD])
        sinks = at("sinks", 134.75, [P, AH])
        att = at("att", 134.8125, [P, 8, AH])
        A_MAX, A_NEG, A_SUM, A_SINK, A_ESINK, A_DEN, A_REC, neg_sinks = (att[:, n, :] for n in range(8))
        tick = at("tick", 135.8125, [P, 1])
        gate_bias = at("gate_bias", 135.0625, [CHAIN_ROWS, 2])
        m_cols = at("m_cols", 135.125, [P, 3, NB * MH])
        chunk_rows = at("chunk_rows", 135.5, [CHAIN_ROWS, 2, NB])

        r_li = at("r_li", 199, [CHAIN_ROWS, S])
        r_lf = at("r_lf", 162, [CHAIN_ROWS, S])
        r_b = at("r_b", 158, [CHAIN_ROWS, S])
        r_m = at("r_m", 203, [CHAIN_ROWS, S])
        r_in = at("r_in", 136, [CHAIN_ROWS, S])
        r_g, r_wi, r_r, r_em, r_wk = r_li, r_lf, r_b, r_m, r_in

        col = at("col", 32, [P, NB, 3, CHAIN_ROWS])
        state = at("state", 39.5, [P, 2, 2, MV + 1])
        h_s = [at("h_s0", 96, [P, 2, NB, P]), at("h_s1", 47.75, [P, 2, NB, P])]
        h_q = [at("h_q0", 104, [P, 2, NB, P]), at("h_q1", 55.75, [P, 2, NB, P])]
        h_kw = [at("h_kw0", 112, [P, 2, NB, P]), at("h_kw1", 120, [P, 2, NB, P])]
        h_dec = at("h_dec", 38.25, [P, 2, 2, NB])
        h_den = at("h_den", 38.4375, [P, 2, 2])
        h_arg = at("h_arg", 128.25, [P, NB, P])
        h_junk = at("h_junk", 136, [P, 4, MV])
        hm = at("hm", 64, [P, NB, MH, MV])
        chains = at("chains", 199, [CHAIN_ROWS, 2, MH, P])
        order = at("order", 203, [P, 2, P])

        hm_hi = at("hm_hi", 167, [P, KD, S], F32R)
        hm_lo = at("hm_lo", 32, [P, KD, S], F32R)
        o_hi = at("o_hi", 0, [P, AH // 2, S], F32R)
        o_lo = at("o_lo", 16, [P, AH // 2, S], F32R)
        mg_hi = at("mg_hi", 64, [P, KD, S], F32R)
        mg_lo = at("mg_lo", 135, [P, KD, S], F32R)
        wp_raw = at("wp_raw", 198, [P, PLE // P, D])
        wp_lo = at("wp_lo", 198, [P, PLE // P, D], F32R)
        wp_hi = at("wp_hi", 182, [P, PLE // P, D], F32R)
        p_in = at("p_in", 182, [P, NB, PLE])
        p_hi = at("p_hi", 174, [P, PLE // P, S], F32R)
        p_lo = at("p_lo", 190, [P, PLE // P, S], F32R)
        sig_in = [at(f"sig_in{n}", [199, 203, 128.25, 158][n], [P, S]) for n in range(4)]
        mix_y = at("mix_y", 32, [P, KD, S])

        sig_dram = nc.dram_tensor("sig_dram", (3 * KD, P, S), F32, kind="Internal").ap()
        resid_dram = nc.dram_tensor("resid_dram", (KD, P, S), F32, kind="Internal").ap()

        (spilled, tables_loaded, rot_done, rope_cos, rope_sin, rope_done, vt_done, vt_left, mix_done, mix_left,
         pad_zero, conv_step, conv_done, mqk_ready, ones_v, small_loaded) = (sem(x) for x in (
            "spilled", "tables_loaded", "rot_done", "rope_cos", "rope_sin", "rope_done", "vt_done", "vt_left",
            "mix_done", "mix_left", "pad_zero", "conv_step", "conv_done", "mqk_ready", "ones_v",
            "small_loaded"))
        (qst_ready, score_done, max_done, neg_ready, prob_ready, pt_done, pt_left, pv_done, sink_arg, sink_exp,
         den_ready, rec_ready, osb_ready, ot_done, ot_left, qst_zero, sinks_ready) = (sem(x) for x in (
            "qst_ready", "score_done", "max_done", "neg_ready", "prob_ready", "pt_done", "pt_left", "pv_done",
            "sink_arg", "sink_exp", "den_ready", "rec_ready", "osb_ready", "ot_done", "ot_left", "qst_zero",
            "sinks_ready"))
        raw_q = [sem(f"raw_q{n}") for n in range(RING)]
        sig_stored = [sem(f"sig_stored{n}") for n in range(2)]
        row_act, row_dve, gate_zeroed = (sem(x) for x in ("row_act", "row_dve", "gate_zeroed"))

        W_IN = t["w_in"][0]

        def copy(dst, src, scale=1.0):
            return nc.vector.tensor_scalar(dst, src, scale, None, ALU.mult)

        def in_block(first):
            return W_IN[:, bass.ds(first, P)].rearrange("(k p) n -> p k n", p=P)

        def table(name, rows=P):
            first, width = TABLE[name]
            return t["tables"][0:rows, first:first + width]

        def sig_tile(n):
            return sig_dram[bass.ds(n, 1)].rearrange("a p n -> (a p) n")

        def mix_sp(sp, b):
            c = Count(b)
            wq = W_IN[:, C_AQ:C_AQ + AH * AD].rearrange("(k p) (g i d) -> i p k g d", p=P, g=2, d=AD)

            for k in range(AH // 2):
                load_queries(sp, c, k, wq)
                if k == 1:
                    for m in range(KD):
                        resid_wait(sp, 0, m)
                        sp.dma_start(resid_dram[m], resid[:, m, :]).then_inc(spilled, 16)
                    sp.dma_start(cos_sb[:, :], table("cos")).then_inc(tables_loaded, 16)
                    sp.dma_start(sin_sb[:, :], table("sin")).then_inc(tables_loaded, 16)
                    sp.dma_start(perm[:, :], table("perm")).then_inc(tables_loaded, 16)
                    sp.dma_start(window[:, :], table("window")).then_inc(tables_loaded, 16)
            load(sp, c, 4, in_block(C_AK))
            load(sp, c, 5, in_block(C_AV))
            with sp.Fori(0, KD // 2) as i:
                c = Count(b + T_MQK, 2, i)
                for k in range(2):
                    load(sp, c, k, in_block(i * (2 * P) + (C_MQK + k * P)))
            with sp.Fori(0, KD // 2) as i:
                c = Count(b + T_MV, 2, i)
                for k in range(2):
                    load(sp, c, k, in_block(i * (2 * P) + (C_MV + k * P)))

            def store_sig(c, k, tile):
                sp.wait_ge(mix_left, c.n(k + 1))
                s = c.slot(k)
                sp.dma_start(sig_tile(tile), tmp[:, s, :]).then_inc(sig_stored[s], 16)

            c = Count(b + T_SIG)
            load(sp, c, 0, in_block(C_MO))
            load(sp, c, 1, in_block(C_BG))
            ct = Count(T_SIG)
            with sp.Fori(0, KD - 1) as i:
                c, ct = Count(b + T_SIG + 2, 2, i), Count(T_SIG, 2, i)
                load(sp, c, 0, in_block(i * P + (C_MO + P)))
                store_sig(ct, 0, i)
                load(sp, c, 1, in_block(i * P + (C_BG + P)))
                store_sig(ct, 1, i + KD)
            c, ct = Count(b + T_MG), Count(T_SIG + 2 * KD - 2)
            load_gates(sp, c)
            store_sig(ct, 0, KD - 1)
            load(sp, Count(b + T_GM), 0, in_block(C_BG + D))
            store_sig(ct, 1, 2 * KD - 1)
            sp.wait_ge(score_done, AH * NB)
            sp.dma_start(r_in[:, :], table("inside", CHAIN_ROWS)).then_inc(tables_loaded, 16)
            load(sp, Count(b + T_GM), 1, in_block(C_BG + D + P))
            for k in range(KD):
                if k + 2 < KD:
                    load(sp, Count(b + T_GM), k + 2, in_block(C_BG + D + (k + 2) * P))
                if k == KD - 1:
                    mlstm_sp(sp)
                store_sig(Count(T_GM), k, 2 * KD + k)

        def load_queries(sp, c, k, wq):
            if c.base + k >= RING:
                sp.wait_ge(wlo_ready, c.n(k - RING + 1))
            s = c.slot(k)
            both = w_raw[:, s, :].rearrange("p (k g d) -> p k g d", k=KD, g=2)
            sp.dma_start(both[:, :, 0, :], wq[k][:, :, 0, :]).then_inc(raw_q[s], 16)
            sp.dma_start(both[:, :, 1, :], wq[k][:, :, 1, :]).then_inc(raw_loaded[s], 16)

        def load_gates(sp, c):
            sp.wait_ge(wlo_ready, c.n(-RING + 1))
            s = c.slot(0)
            sp.dma_start(w_raw[:, s, 0:KD * 4 * MH].rearrange("p (k n) -> p k n", k=KD),
                         W_IN[:, C_MG:C_MG + 4 * MH].rearrange("(k p) n -> p k n", p=P)).then_inc(raw_loaded[s], 16)

        def mix_product(pe, ct, cb, k, pieces=range(KD)):
            acc = ps[ct.slot(k)]
            if pieces[0] == 0:
                pe.wait_ge(wlo_ready, cb.n(k + 1))
                if ct.base + k >= 2:
                    pe.wait_ge(mix_left, ct.n(k - 1))
            for kk in pieces:
                mm = product(acc, [(cb.slot(k), kk * P, u_hi[:, kk, :], u_lo[:, kk, :])], first=(kk == 0),
                             last=(kk == KD - 1), new_block=(kk == 0))
            if pieces[-1] == KD - 1:
                mm.then_inc(mix_done, 1)

        def rotate(pe, k):
            pe.wait_ge(mix_left, k + 1)
            if k:
                pe.wait_ge(rope_sin, k)
            else:
                pe.wait_ge(tables_loaded, 64)
            for h in range(2):
                cols = slice(h * HALF, (h + 1) * HALF)
                mm = nc.tensor.matmul(ps[2][:, cols], perm[:, :], tmp[:, k % 2, cols], start=True, stop=True)
            mm.then_inc(rot_done, 1)

        def turn_values(pe, ct, cv, k):
            pe.wait_ge(mix_left, ct.n(k + 1))
            if cv.base + k >= 1:
                pe.wait_ge(vt_left, cv.n(k))
            for n in range(NB):
                mm = nc.tensor.transpose(ps[3][:, n * P:(n + 1) * P], tmp[:, ct.slot(k), n * P:(n + 1) * P],
                                         ident[:, :])
            mm.then_inc(vt_done, 1)

        def heads():
            return [(j, j // 2, j % 2, j // 2 + AH // 2 * (j % 2)) for j in range(AH)]

        def att_window(n, edge):
            if edge == 0:
                return 0, 2, P
            if edge == 2:
                return (NB - 2) * P, 2, 0
            return n * P - P, 3, 0

        def score_bank(j):
            return ps[2][:, (j % 2) * HALF:(j % 2) * HALF + WINDOW]

        PT = ps[3][:, 0:WINDOW]
        OT = ps[3][:, 0:HALF]
        OA = ps[3][:, HALF:2 * HALF]

        def att_pe(pe, n, edge, cu, ct, cb):
            key0, blocks, _ = att_window(n, edge)
            width = blocks * P

            def score(j, i, g, head):
                if j == 0:
                    pe.wait_ge(qst_ready, n + 1)
                if cu.base + j >= 2:
                    pe.wait_ge(max_done, cu.n(j - 1))
                nc.tensor.matmul(score_bank(j)[:, 0:width], q_st[:, g, i, :], att_k[:, bass.ds(key0, width)],
                                 start=True, stop=True).then_inc(score_done, 1)

            def turn(j, i, g, head):
                pe.wait_ge(prob_ready, cu.n(j + 1))
                if j or cu.base:
                    pe.wait_ge(pt_left, cu.n(j))
                if j == 0 and cu.base:
                    pe.wait_ge(ot_left, n)
                for w in range(blocks):
                    mm = nc.tensor.transpose(PT[:, w * P:(w + 1) * P], prob[j % PROBS][:, w * P:(w + 1) * P],
                                             ident[:, :])
                mm.then_inc(pt_done, 1)

            def weigh(j, i, g, head):
                pe.wait_ge(pt_left, cu.n(j + 1))
                if j == 0 and cu.base:
                    pe.wait_ge(osb_ready, n)
                for w in range(blocks):
                    block_n = (key0 // P + w) if edge != 1 else n + (w - 1)
                    mm = nc.tensor.matmul(OA[:, head * AD:(head + 1) * AD], prob_t[:, j % 2, w * P:(w + 1) * P],
                                          att_v[:, bass.ds(block_n, 1), g * AD:(g + 1) * AD].rearrange(
                                              "p a d -> p (a d)"),
                                          start=(w == 0), stop=(w == blocks - 1))
                mm.then_inc(pv_done, 1)

            pieces = [(k, kk) for k in range(2) for kk in range(KD)]
            H = heads()
            for step in range(12):
                for _ in range({0: 2, 11: 4}.get(step, 1)):
                    k, kk = pieces.pop(0)
                    mix_product(pe, ct, cb, k, [kk])
                if step < AH:
                    score(*H[step])
                if 2 <= step <= AH + 1:
                    turn(*H[step - 2])
                if 3 <= step <= AH + 2:
                    weigh(*H[step - 3])
            pe.wait_ge(osb_ready, n + 1)
            for kt in range(AH // 2):
                mm = nc.tensor.transpose(OT[:, kt * P:(kt + 1) * P], o_sb[:, kt * P:(kt + 1) * P], ident[:, :])
            mm.then_inc(ot_done, 1)

        def mix_pe(pe, b, pre):
            cb, ct = Count(b), Count(0)
            first_pair(pe, cb, pre, mix_done)
            rotate(pe, 0)
            for k in range(2, N_QKV):
                mix_product(pe, ct, cb, k)
                rotate(pe, k - 1)
            turn_values(pe, Count(N_QKV - 1), Count(0), 0)
            with pe.Fori(0, KD // 2) as i:
                cb, ct = Count(b + T_MQK, 2, i), Count(T_MQK, 2, i)
                mix_product(pe, ct, cb, 0)
                mix_product(pe, ct, cb, 1)
            with pe.Fori(0, KD // 4) as i:
                cb, ct, cv = Count(b + T_MV, 4, i), Count(T_MV, 4, i), Count(1, 4, i)
                mix_product(pe, ct, cb, 0)
                for k in range(1, 4):
                    mix_product(pe, ct, cb, k)
                    turn_values(pe, ct, cv, k - 1)
                turn_values(pe, ct, cv, 3)
            att_pe(pe, 0, 0, Count(0), Count(T_SIG), Count(b + T_SIG))
            with pe.Fori(0, NB - 2) as i:
                att_pe(pe, i + 1, 1, Count(AH, AH, i), Count(T_SIG + 2, 2, i), Count(b + T_SIG + 2, 2, i))
            att_pe(pe, NB - 1, 2, Count(AH * (NB - 1)), Count(T_MG - 2), Count(b + T_MG - 2))
            mix_product(pe, Count(T_MG), Count(b + T_MG), 0)
            for k in range(KD):
                if k == KD - 1:
                    columns_pe(pe)
                mix_product(pe, Count(T_GM), Count(b + T_GM), k)

        def evac(act, ct, k, func, dst, before=()):
            act.wait_ge(mix_done, ct.n(k + 1))
            for signal, count in before:
                act.wait_ge(signal, count)
            nc.scalar.activation(dst, ps[ct.slot(k)][:, :], func).then_inc(mix_left, 1)

        def silu_conv(act, cc, k, m):
            act.wait_ge(conv_done, cc.n(k + 1))
            tile = mqk[:, bass.ds(m, 1), :].rearrange("p a n -> p (a n)")
            nc.scalar.activation(tile, tile, ACT.Silu).then_inc(mqk_ready, 1)

        def conv_act(act, b, i, first):
            cb, ct, cc = Count(b + T_MQK + first, 2, i), Count(T_MQK + first, 2, i), Count(first, 2, i)
            for k in range(2):
                if first + k >= 2:
                    act.wait_ge(conv_done, cc.n(k - 1))
                elif k == 0:
                    act.wait_ge(pad_zero, 1)
                evac(act, ct, k, ACT.Copy, zpad[:, k, TAPS // 2:TAPS // 2 + S])
                split_hi(act, cb, k + 2)
                silu_conv(act, cc, k, i * 2 + (first + k))

        def att_act(act, n, edge, cu, ct, cb, next_hi):
            blocks = att_window(n, edge)[1]
            width = blocks * P

            def expo(j):
                act.wait_ge(neg_ready, cu.n(j + 1))
                nc.scalar.activation(prob[j % PROBS][:, 0:width], prob[j % PROBS][:, 0:width], ACT.Exp,
                                     bias=A_NEG[:, j:j + 1], scale=ATT_SCALE,
                                     accum_out=A_SUM[:, j:j + 1]).then_inc(prob_ready, 1)

            def keep(j):
                act.wait_ge(pt_done, cu.n(j + 1))
                if cu.base + j >= 2:
                    act.wait_ge(pv_done, cu.n(j - 1))
                nc.scalar.copy(prob_t[:, j % 2, 0:width], PT[:, 0:width]).then_inc(pt_left, 1)

            def sig(k):
                s = ct.slot(k)
                before = []
                if ct.base + k >= T_SIG + 2:
                    uses = (ct.base + k - T_SIG) // 2
                    before = [(sig_stored[s], 16 * uses if ct.turn is None else ct.turn * 16 + 16 * uses)]
                evac(act, ct, k, ACT.Copy, tmp[:, s, :], before)

            for j in range(AH):
                expo(j)
                if j >= 2:
                    keep(j - 2)
                if j == 6:
                    sig(0)
                if j == 7:
                    next_hi(2)
            keep(AH - 2)
            keep(AH - 1)
            act.wait_ge(sink_arg, n + 1)
            nc.scalar.activation(A_ESINK[:, :], A_SINK[:, :], ACT.Exp).then_inc(sink_exp, 1)
            sig(1)
            next_hi(3)

        def gates_hi(act, c):
            s = c.slot()
            act.wait_ge(raw_loaded[s], c.uses() * 16)
            act.wait_ge(gate_zeroed, 2)
            for n in range(4):
                op = nc.scalar.activation(gate_cols(w_hi, s, n), raw_gate_cols(s, n), ACT.Copy)
            op.then_inc(whi_ready, 1)

        def gate_cols(w, s, n):
            first = 64 * (n % 2) + 32 * (n // 2)
            return w[:, s, :].rearrange("p (k n) -> p k n", k=KD)[:, :, first:first + MH]

        def raw_gate_cols(s, n):
            return w_raw[:, s, 0:KD * 4 * MH].rearrange("p (k n) -> p k n", k=KD)[:, :, n * MH:(n + 1) * MH]

        def mix_act(act, b):
            cb, ct = Count(b), Count(0)
            for k in range(N_QKV):
                if k < 2:
                    act.wait_ge(raw_q[cb.slot(k)], 32)
                evac(act, ct, k, ACT.Copy, tmp[:, k % 2, :],
                     [(rope_done, k - 1)] if k >= 2 else [(ulo_ready, 2 * KD)])
                split_hi(act, cb, k + 2)
            with act.Fori(0, MH // 2) as i:
                conv_act(act, b, i, 0)
            with act.Fori(0, MH // 2) as i:
                conv_act(act, b, i, MH)
            act.wait_ge(conv_done, KD)
            with act.Fori(0, KD // 4) as i:
                cb, ct = Count(b + T_MV, 4, i), Count(T_MV, 4, i)
                for k in range(4):
                    evac(act, ct, k, ACT.Copy, tmp[:, ct.slot(k), :], [(vt_done, Count(max(k, 1), 4, i).n())])
                    split_hi(act, cb, k + 2)
            act.wait_ge(vt_done, 1 + KD)
            cb = Count(b + T_SIG)
            att_act(act, 0, 0, Count(0), Count(T_SIG), cb, lambda k: split_hi(act, cb, k))
            with act.Fori(0, NB - 2) as i:
                cbi = Count(b + T_SIG + 2, 2, i)
                att_act(act, i + 1, 1, Count(AH, AH, i), Count(T_SIG + 2, 2, i), cbi,
                        lambda k: split_hi(act, cbi, k))
            last = {2: lambda: gates_hi(act, Count(b + T_MG)), 3: lambda: split_hi(act, Count(b + T_GM), 0)}
            att_act(act, NB - 1, 2, Count(AH * (NB - 1)), Count(T_MG - 2), Count(b + T_MG - 2),
                    lambda k: last[k]())
            act.wait_ge(mix_done, T_MG + 1)
            act.wait_ge(small_loaded, 48)
            act.wait_ge(pv_done, AH * NB)
            acc = ps[T_MG % 2]
            nc.scalar.activation(r_li[:, :], acc[0:CHAIN_ROWS, :], ACT.Identity,
                                 bias=gate_bias[:, 0:1]).then_inc(row_act, 1)
            nc.scalar.activation(r_lf[:, :], acc[CHAIN_ROWS:P, :], ACT.Copy).then_inc(mix_left, 1)
            split_hi(act, Count(b + T_GM), 1)
            act.wait_ge(row_dve, 1)
            nc.scalar.activation(r_b[:, :], r_lf[:, :], ACT.Abs).then_inc(row_act, 1)
            act.wait_ge(row_act, 2)
            nc.scalar.activation(r_b[:, :], r_b[:, :], ACT.Exp, scale=-1.0).then_inc(row_act, 1)
            act.wait_ge(row_act, 3)
            nc.scalar.activation(r_b[:, :], r_b[:, :], ACT.Ln, bias=1.0).then_inc(row_act, 1)

            def gm(ct, cb, k, stored):
                evac(act, ct, k, ACT.Copy, tmp[:, ct.slot(k), :], [(sig_stored[ct.slot(k)], stored)])
                if cb is not None:
                    split_hi(act, cb, k + 2)

            for k in range(2):
                gm(Count(T_GM), Count(b + T_GM), k, 16 * KD)
            act.wait_ge(row_dve, 12)
            nc.scalar.activation(r_wi[:, :], r_wi[:, :], ACT.Exp).then_inc(row_act, 1)
            nc.scalar.activation(r_em[:, :], r_em[:, :], ACT.Exp, scale=-1.0).then_inc(row_act, 1)
            nc.scalar.activation(r_wk[:, :], r_wk[:, :], ACT.Exp).then_inc(row_act, 1)
            with act.Fori(0, 2) as i:
                for k in range(2):
                    gm(Count(T_GM + 2, 2, i), Count(b + T_GM + 2, 2, i), k, i * 16 + 16 * (KD + 1))
            for k in range(6, KD):
                gm(Count(T_GM), None, k, 16 * (KD + k // 2))

        def block_queries(first):
            for g in range(2):
                rows = slice(64 * g, 64 * g + 64)
                op = copy(q_st[rows, g, :, :], att_q[rows, :, bass.ds(first, P)])
            op.then_inc(qst_ready, 1)

        def att_dve(dve, n, edge, cu, cb, next_lo, clear=None):
            key0, blocks, mask0 = att_window(n, edge)
            width = blocks * P
            if edge == 0:
                dve.wait_ge(qst_zero, 1)
                dve.wait_ge(rope_done, AH // 2 + 1)
                block_queries(n * P)
            for j in range(AH):
                if cu.base + j >= PROBS:
                    dve.wait_ge(pt_done, cu.n(j - PROBS + 1))
                dve.wait_ge(score_done, cu.n(j + 1))
                nc.vector.tensor_copy(tick[:, :], neg_sinks[:, 0:1])
                nc.vector.tensor_tensor_reduce(out=prob[j % PROBS][:, 0:width], in0=score_bank(j)[:, 0:width],
                                               in1=window[:, mask0:mask0 + width], scale=1.0, scalar=-3e38,
                                               op0=ALU.add, op1=ALU.max, accum_out=A_MAX[:, j:j + 1]
                                               ).then_inc(max_done, 1)
                dve.wait_ge(max_done, cu.n(j + 1))
                if j == 0 and cu.base:
                    dve.wait_ge(den_ready, n)
                nc.vector.tensor_scalar(A_NEG[:, j:j + 1], A_MAX[:, j:j + 1], -ATT_SCALE, neg_sinks[:, j:j + 1],
                                        ALU.mult, ALU.min).then_inc(neg_ready, 1)
            if clear is not None:
                clear()
            dve.wait_ge(neg_ready, cu.n(AH))
            nc.vector.tensor_tensor(A_SINK[:, :], A_NEG[:, :], neg_sinks[:, :], ALU.subtract).then_inc(sink_arg, 1)
            dve.wait_ge(sink_exp, n + 1)
            dve.wait_ge(prob_ready, cu.n(AH))
            nc.vector.tensor_tensor(A_DEN[:, :], A_SUM[:, :], A_ESINK[:, :], ALU.add).then_inc(den_ready, 1)
            dve.wait_ge(den_ready, n + 1)
            nc.vector.reciprocal(A_REC[:, :], A_DEN[:, :]).then_inc(rec_ready, 1)
            dve.wait_ge(rec_ready, n + 1)
            dve.wait_ge(pv_done, cu.n(AH))
            if cu.base:
                dve.wait_ge(ot_done, n)
            for g in range(2):
                heads_g = slice(g * AH // 2 * AD, (g + 1) * AH // 2 * AD)
                op = nc.vector.tensor_tensor(
                    o_sb[:, heads_g].rearrange("p (i d) -> p i d", d=AD),
                    OA[:, heads_g].rearrange("p (i d) -> p i d", d=AD),
                    A_REC[:, :].rearrange("p (i g) -> p g i", g=2)[:, g, :].unsqueeze(2).to_broadcast(
                        [P, AH // 2, AD]), ALU.mult)
            op.then_inc(osb_ready, 1)
            next_lo(2)
            dve.wait_ge(ot_done, n + 1)
            copy(att_q[:, :, bass.ds(n * P, P)], OT.rearrange("p (k n) -> p k n", n=P)).then_inc(ot_left, 1)
            if edge < 2:
                dve.wait_ge(score_done, cu.n(AH))
                block_queries(n * P + P)
            next_lo(3)

        def rope(dve, k):
            dst = att_q[:, k, :] if k < AH // 2 else att_k[:, :]
            dve.wait_ge(rot_done, k + 1)
            if k:
                dve.wait_ge(rope_done, k)
            nc.vector.tensor_tensor(dst, tmp[:, k % 2, :], cos_sb[:, :], ALU.mult).then_inc(rope_cos, 1)
            nc.vector.tensor_tensor(rope_t[:, :], ps[2][:, :], sin_sb[:, :], ALU.mult).then_inc(rope_sin, 1)
            dve.wait_ge(rope_cos, k + 1)
            dve.wait_ge(rope_sin, k + 1)
            nc.vector.tensor_tensor(dst, dst, rope_t[:, :], ALU.add).then_inc(rope_done, 1)

        def convolve(dve, cc, ct, k, m, slot):
            dve.wait_ge(mix_left, ct.n(k + 1))
            tile = mqk[:, bass.ds(m, 1), :].rearrange("p a n -> p (a n)")
            steps = Count(cc.base * (TAPS - 1), cc.per * (TAPS - 1), cc.turn)

            def vec(first):
                return vecs[:, bass.ds(m + first, 1)]

            nc.vector.tensor_scalar(tile, zpad[:, slot, 0:S], vec(80), vec(72), ALU.mult,
                                    ALU.add).then_inc(conv_step, 1)
            for tap in range(1, TAPS):
                dve.wait_ge(conv_step, steps.n((TAPS - 1) * k + tap))
                nc.vector.scalar_tensor_tensor(out=tile, in0=zpad[:, slot, tap:tap + S], scalar=vec(80 + KD * tap),
                                               in1=tile, op0=ALU.mult, op1=ALU.add
                                               ).then_inc(conv_step if tap < TAPS - 1 else conv_done, 1)

        def conv_dve(dve, b, i, first):
            cb, ct, cc = Count(b + T_MQK + first, 2, i), Count(T_MQK + first, 2, i), Count(first, 2, i)
            for k in range(2):
                split_lo(dve, cb, k + 2)
                convolve(dve, cc, ct, k, i * 2 + (first + k), k)

        def mix_dve(dve, b):
            cb = Count(b)
            dve.wait_ge(tables_loaded, 64)
            for k in range(N_QKV - 1):
                split_lo(dve, cb, k + 2)
                rope(dve, k)
            split_lo(dve, cb, N_QKV + 1)
            dve.wait_ge(vt_done, 1)
            nc.vector.tensor_copy(att_v[:, :, :], ps[3][:, :].rearrange("p (b n) -> p b n", n=P)
                                  ).then_inc(vt_left, 1)
            dve.wait_ge(spilled, 16 * KD)
            with dve.Fori(0, MH // 2) as i:
                conv_dve(dve, b, i, 0)
            with dve.Fori(0, MH // 2) as i:
                conv_dve(dve, b, i, MH)
            dve.wait_ge(ones_v, 1)
            with dve.Fori(0, KD // 4) as i:
                cb, cv = Count(b + T_MV, 4, i), Count(1, 4, i)
                for k in range(4):
                    split_lo(dve, cb, k + 2)
                    dve.wait_ge(vt_done, cv.n(k + 1))
                    copy(m_v[:, :, bass.ds(i * 2 + k // 2, 1), (k % 2) * P:(k % 2 + 1) * P],
                         ps[3][:, :].rearrange("p (b a n) -> p b a n", a=1, n=P)).then_inc(vt_left, 1)
            dve.wait_ge(small_loaded, 48)
            nc.vector.tensor_scalar(neg_sinks.rearrange("p (i g) -> p i g", g=2),
                                    sinks[:, :].rearrange("p (g i) -> p i g", g=2), -1.0, None, ALU.mult
                                    ).then_inc(sinks_ready, 1)
            dve.wait_ge(sinks_ready, 1)
            cb = Count(b + T_SIG)
            att_dve(dve, 0, 0, Count(0), cb, lambda k: split_lo(dve, cb, k))
            with dve.Fori(0, NB - 2) as i:
                cbi = Count(b + T_SIG + 2, 2, i)
                att_dve(dve, i + 1, 1, Count(AH, AH, i), cbi, lambda k: split_lo(dve, cbi, k))

            def gates_clear(c):
                dve.wait_ge(block_used, c.n(-RING + 1))
                dve.wait_ge(wlo_ready, c.n(-RING + 1))
                for w in (w_hi, w_lo):
                    nc.vector.memset(w[:, c.slot(), :].bitcast(F32), 0.0).then_inc(gate_zeroed, 1)

            def gates_lo(c):
                s = c.slot()
                dve.wait_ge(whi_ready, c.n(1))
                dve.wait_ge(gate_zeroed, 2)
                for n in range(4):
                    op = nc.vector.tensor_tensor(gate_cols(w_lo, s, n), raw_gate_cols(s, n),
                                                 gate_cols(w_hi, s, n).bitcast(F32), ALU.subtract)
                op.then_inc(wlo_ready, 1)

            last = {2: lambda: gates_lo(Count(b + T_MG)), 3: lambda: split_lo(dve, Count(b + T_GM), 0)}
            att_dve(dve, NB - 1, 2, Count(AH * (NB - 1)), Count(b + T_MG - 2), lambda k: last[k](),
                    clear=lambda: gates_clear(Count(b + T_MG)))
            split_lo(dve, Count(b + T_GM), 1)
            dve.wait_ge(mix_left, T_MG + 1)
            dve.wait_ge(tables_loaded, 80)

            fw, bw = slice(0, 32), slice(32, CHAIN_ROWS)
            nc.vector.tensor_scalar(r_lf[:, :], r_lf[:, :], gate_bias[:, 1:2], None, ALU.add).then_inc(row_dve, 1)
            dve.wait_ge(row_act, 4)
            nc.vector.scalar_tensor_tensor(out=r_lf[:, :], in0=r_lf[:, :], scalar=0.0, in1=r_b[:, :], op0=ALU.min,
                                           op1=ALU.subtract).then_inc(row_dve, 1)
            dve.wait_ge(row_dve, 2)
            nc.vector.tensor_tensor_scan(r_b[fw, :], r_in[fw, :], r_lf[fw, :], 0.0, ALU.mult,
                                         ALU.add).then_inc(row_dve, 1)
            nc.vector.tensor_tensor_scan(r_b[bw, ::-1], r_in[bw, ::-1], r_lf[bw, ::-1], 0.0, ALU.mult,
                                         ALU.add).then_inc(row_dve, 1)
            nc.vector.tensor_tensor_scan(r_m[fw, :], r_lf[fw, :], r_li[fw, :], 0.0, ALU.add,
                                         ALU.max).then_inc(row_dve, 1)
            nc.vector.tensor_tensor_scan(r_m[bw, ::-1], r_lf[bw, ::-1], r_li[bw, ::-1], 0.0, ALU.add,
                                         ALU.max).then_inc(row_dve, 1)
            dve.wait_ge(row_dve, 6)
            nc.vector.tensor_tensor(r_g[:, :], r_li[:, :], r_b[:, :], ALU.subtract).then_inc(row_dve, 1)
            dve.wait_ge(row_dve, 7)
            nc.vector.tensor_tensor(r_r[:, :], r_m[:, :], r_b[:, :], ALU.subtract).then_inc(row_dve, 1)
            dve.wait_ge(row_dve, 8)
            before, last_r = chunk_rows[:, 0, :], chunk_rows[:, 1, :]
            m_t = r_m[:, :].rearrange("p (b n) -> p b n", n=P)
            r_t = r_r[:, :].rearrange("p (b n) -> p b n", n=P)
            nc.vector.memset(chunk_rows[:, :, :], 0.0).then_inc(row_dve, 1)
            dve.wait_ge(row_dve, 9)
            nc.vector.tensor_copy(before[fw, 1:NB], m_t[fw, 0:NB - 1, P - 1])
            nc.vector.tensor_copy(before[bw, 0:NB - 1], m_t[bw, 1:NB, 0])
            nc.vector.tensor_copy(last_r[fw, :], r_t[fw, :, P - 1])
            nc.vector.tensor_copy(last_r[bw, :], r_t[bw, :, 0]).then_inc(row_dve, 1)
            dve.wait_ge(row_dve, 10)

            def spread(x):
                return x.unsqueeze(2).to_broadcast([CHAIN_ROWS, NB, P])

            nc.vector.tensor_tensor(r_wi[:, :].rearrange("p (b n) -> p b n", n=P), spread(before), r_t,
                                    ALU.subtract).then_inc(row_dve, 1)
            nc.vector.tensor_tensor(r_wk[:, :].rearrange("p (b n) -> p b n", n=P),
                                    r_g[:, :].rearrange("p (b n) -> p b n", n=P), spread(last_r),
                                    ALU.subtract).then_inc(row_dve, 1)
            cb = Count(b + T_GM)
            split_lo(dve, cb, 2)
            split_lo(dve, cb, 3)
            with dve.Fori(0, 2) as i:
                for k in range(2):
                    split_lo(dve, Count(b + T_GM + 2, 2, i), k + 2)
        (cols_turned, cols_left, chains_loaded, st_done, kt_done, rb_done, arg_sub, arg_ready, exp_ready, s_ready,
         wb_done, q_ready, kw_ready, out_done, dc_done, c_ready, den_bound, den_max, den_inv, hm_left,
         sq_heads) = (sem(x) for x in (
            "cols_turned", "cols_left", "chains_loaded", "st_done", "kt_done", "rb_done", "arg_sub", "arg_ready",
            "exp_ready", "s_ready", "wb_done", "q_ready", "kw_ready", "out_done", "dc_done", "c_ready",
            "den_bound", "den_max", "den_inv", "hm_left", "sq_heads"))
        ST = ps[0]
        BCAST = KT = ps[1]
        G_COL, WK_COL, EM_COL = range(3)

        def chunk_of(way, n):
            return n if way == 0 else NB - 1 - n

        def column(way, h, q):
            return col[:, :, q, 32 * way + h]

        def over_rows(x):
            return x.unsqueeze(2).to_broadcast([P, NB, P])

        def row_place(h, weights):
            return BCAST if h else ps[3] if weights else ps[2]

        def blocks(x):
            return x[:, :].rearrange("p (b n) -> p b n", n=P)

        def d_state(way):
            return ps[2][:, way * HALF:way * HALF + MV + 1]

        def out_place(h, n):
            return ps[1] if h == MH - 1 and n % 2 else ps[3]

        def d_out(h, way, n):
            return out_place(h, n)[:, way * HALF:way * HALF + MV + 1]

        def both_dens(h, n):
            return out_place(h, n)[:, :].rearrange("p (w n) -> p w n", w=2)[:, :, MV]

        (heads_mean, heads_root, heads_inv, hm_scaled, hm_turned, hmhi_ready, hmlo_pool, mlo_ready, ohi_ready,
         olo_ready, br_attn, br_mlstm, br_sum, mghi_ready, resid_back) = (sem(x) for x in (
            "heads_mean", "heads_root", "heads_inv", "hm_scaled", "hm_turned", "hmhi_ready", "hmlo_pool", "mlo_ready",
            "ohi_ready", "olo_ready", "br_attn", "br_mlstm", "br_sum", "mghi_ready", "resid_back"))
        sig_loaded = [sem(f"sig_loaded{n}") for n in range(4)]
        sig_made = [sem(f"sig_made{n}") for n in range(4)]
        sig_free = [sem(f"sig_free{n}") for n in range(2)]
        T_BR = N_TILES
        T_WO = T_BR + 2 * KD
        T_END = T_WO + KD
        GATED = KD // 2
        WIDTH_A = AH * AD

        def gate(act, j, uses):
            act.wait_ge(sig_loaded[j], 16 * uses)
            nc.scalar.activation(sig_in[j][:, :], sig_in[j][:, :], ACT.Sigmoid).then_inc(sig_made[j], 1)

        def columns_pe(pe):
            pe.wait_ge(row_act, 7)
            pe.wait_ge(row_dve, 12)
            for n in range(NB):
                for q, rows in ((G_COL, r_g), (WK_COL, r_wk), (EM_COL, r_em)):
                    at_ = (n * 3 + q) * CHAIN_ROWS
                    mm = nc.tensor.transpose(ps[2 + at_ // S][:, at_ % S:at_ % S + CHAIN_ROWS],
                                             rows[:, n * P:(n + 1) * P], ident[0:CHAIN_ROWS, 0:CHAIN_ROWS])
            mm.then_inc(cols_turned, 1)

        def mlstm_pe(pe):
            def scores(h):
                if h:
                    pe.wait_ge(s_ready, 2 * h)
                    pe.wait_ge(q_ready, 2 * h)
                    pe.wait_ge(kw_ready, 2 * h)
                else:
                    pe.wait_ge(mix_left, N_TILES - 1)
                for n in range(NB):
                    cols = slice(n * P, (n + 1) * P)
                    mm = nc.tensor.transpose(KT[:, cols], mqk[:, MH + h, cols], ident[:, :])
                mm.then_inc(kt_done, 1)
                if h == 0:
                    pe.wait_ge(mix_left, N_TILES)
                for n in range(NB):
                    cols = slice(n * P, (n + 1) * P)
                    mm = nc.tensor.matmul(ST[:, cols], mqk[:, MH + h, cols], mqk[:, h, cols], start=True, stop=True)
                mm.then_inc(st_done, 1)

            def row_on_all(h, way, rows, done, free):
                for wait in free:
                    pe.wait_ge(*wait)
                place = row_place(h, rows is r_wi)
                for f in range(2):
                    mm = nc.tensor.matmul(place[:, f * HALF:(f + 1) * HALF], chains[:, way, h, :],
                                          rows[:, f * HALF:(f + 1) * HALF], start=True, stop=True)
                mm.then_inc(done, 1)

            def prepare(h, step):
                if step == 0:
                    scores(h)
                elif step == 2:
                    row_on_all(h, 0, r_r, rb_done, [(kw_ready, 2 * h + 2)])
                elif step == 3:
                    row_on_all(h, 0, r_wi, wb_done, [(arg_sub, 2 * h + 1)])
                elif step == 4:
                    row_on_all(h, 1, r_r, rb_done, [(q_ready, 2 * h + 1)])
                elif step == 5:
                    row_on_all(h, 1, r_wi, wb_done, [(arg_sub, 2 * h + 2)])

            scores(0)
            row_on_all(0, 0, r_r, rb_done, [(chains_loaded, 48), (cols_left, 2)])
            row_on_all(0, 0, r_wi, wb_done, [])
            row_on_all(0, 1, r_r, rb_done, [(arg_sub, 1)])
            row_on_all(0, 1, r_wi, wb_done, [(q_ready, 1)])
            for h in range(MH):
                for n in range(NB):
                    done = h * NB + n
                    if n == 0:
                        pe.wait_ge(s_ready, 2 * h + 2)
                        pe.wait_ge(q_ready, 2 * h + 2)
                    earlier = done - 1 if h == MH - 1 and n else done
                    if earlier:
                        pe.wait_ge(hm_left, earlier)
                    for way in range(2):
                        c = chunk_of(way, n)
                        mm = nc.tensor.matmul(d_out(h, way, n), h_s[h % 2][:, way, c, :], m_v[:, c, h, :], start=True,
                                              stop=(n == 0))
                    if n:
                        for way in range(2):
                            pe.wait_ge(c_ready, 2 * ((NB - 1) * h + n - 1) + way + 1)
                            mm = nc.tensor.matmul(d_out(h, way, n), h_q[h % 2][:, way, chunk_of(way, n), :],
                                                  state[:, way, n % 2, :], start=False, stop=True)
                    mm.then_inc(out_done, 1)
                    if n < NB - 1:
                        if n == 0:
                            pe.wait_ge(kw_ready, 2 * h + 2)
                            if h:
                                pe.wait_ge(c_ready, 2 * (NB - 1) * h)
                        for way in range(2):
                            c = chunk_of(way, n)
                            nc.tensor.matmul(d_state(way), h_kw[h % 2][:, way, c, :], m_v[:, c, h, :], start=True,
                                             stop=True).then_inc(dc_done, 1)
                    if h + 1 < MH:
                        prepare(h + 1, n)

        def mlstm_act(act, b):
            def weights(h):
                for way in range(2):
                    act.wait_ge(arg_ready, 2 * h + way + 1)
                    if h >= 2:
                        act.wait_ge(out_done, NB * (h - 1))
                    nc.scalar.activation(h_s[h % 2][:, way, :, :], h_arg[:, :, :], ACT.Exp,
                                         scale=-1.0).then_inc(exp_ready, 1)

            def squares(h):
                for c in range(NB):
                    step = NB // 2 + c // 2
                    act.wait_ge(hm_left, NB * h + step + 1)
                    if h * NB + c >= 4:
                        act.wait_ge(sq_heads, h * NB + c - 3)
                    chunk = step if c % 2 else NB - 1 - step
                    nc.scalar.activation(h_junk[:, c % 4, :], hm[:, chunk, h, :], ACT.Square,
                                         accum_out=m_cols[:, 0, h * NB + chunk:h * NB + chunk + 1]
                                         ).then_inc(sq_heads, 1)

            def root(h):
                act.wait_ge(heads_mean, h + 1)
                cols = m_cols[:, 1, h * NB:(h + 1) * NB]
                nc.scalar.activation(cols, cols, ACT.Sqrt).then_inc(heads_root, 1)

            weights(0)
            for h in range(MH - 1):
                if h:
                    root(h - 1)
                weights(h + 1)
                squares(h)
            for sem_, count in ((q_ready, 2 * MH), (st_done, MH), (kt_done, MH)):
                act.wait_ge(sem_, count)
            for k in range(AH // 2):
                nc.scalar.activation(o_hi[:, k, :], att_q[:, k, :], ACT.Copy).then_inc(ohi_ready, 1)
            root(MH - 2)
            split_hi(act, Count(b + T_BR), 0, WIDTH_A)
            for j in range(4):
                gate(act, j, 1)
            squares(MH - 1)
            root(MH - 1)
            split_hi(act, Count(b + T_BR), 1)

        def head_mean(dve, h):
            dve.wait_ge(sq_heads, NB * (h + 1))
            nc.vector.tensor_scalar(m_cols[:, 1, h * NB:(h + 1) * NB], m_cols[:, 0, h * NB:(h + 1) * NB], 1.0 / MV,
                                    EPS, ALU.mult, ALU.add).then_inc(heads_mean, 1)

        def head_inverse(dve, h):
            dve.wait_ge(heads_root, h + 1)
            nc.vector.reciprocal(m_cols[:, 2, h * NB:(h + 1) * NB], m_cols[:, 1, h * NB:(h + 1) * NB]
                                 ).then_inc(heads_inv, 1)

        def scale_head(eng, engine, h):
            eng.wait_ge(heads_inv, h + 1)
            engine.tensor_tensor(hm[:, :, h, :], hm[:, :, h, :],
                                 m_cols[:, 2, h * NB:(h + 1) * NB].unsqueeze(2).to_broadcast([P, NB, MV]),
                                 ALU.mult).then_inc(hm_scaled, 1)

        def mlstm_dve(dve, b):
            dve.wait_ge(cols_turned, 1)
            dve.wait_ge(mix_done, N_TILES)
            flat = col[:, :, :, :].rearrange("p b q n -> p (b q n)")
            nc.vector.tensor_copy(flat[:, 0:S], ps[2][:, :]).then_inc(cols_left, 1)
            nc.vector.tensor_copy(flat[:, S:3 * NB * CHAIN_ROWS], ps[3][:, 0:3 * NB * CHAIN_ROWS - S]
                                  ).then_inc(cols_left, 1)
            dve.wait_ge(cols_left, 2)
            dve.wait_ge(chains_loaded, 48)

            def weighed_keys(h):
                dve.wait_ge(kt_done, h + 1)
                if h == 1:
                    for s in range(2):
                        dve.wait_ge(sig_stored[s], 16 * 12)
                if h >= 2:
                    dve.wait_ge(dc_done, 2 * (NB - 1) * (h - 1))
                for way in range(2):
                    nc.vector.scalar_tensor_tensor(out=h_kw[h % 2][:, way, :, :], in0=blocks(KT), scalar=K_SCALE,
                                                   in1=over_rows(column(way, h, WK_COL)), op0=ALU.mult,
                                                   op1=ALU.mult).then_inc(kw_ready, 1)

            def subtract(h, way):
                dve.wait_ge(rb_done, 2 * h + way + 1)
                if 2 * h + way:
                    dve.wait_ge(exp_ready, 2 * h + way)
                nc.vector.tensor_tensor(h_arg[:, :, :], blocks(row_place(h, False)), over_rows(column(way, h, G_COL)),
                                        ALU.subtract).then_inc(arg_sub, 1)

            def bound(h, way):
                dve.wait_ge(arg_sub, 2 * h + way + 1)
                nc.vector.tensor_tensor(h_arg[:, :, :], h_arg[:, :, :],
                                        order[:, way, :].unsqueeze(1).to_broadcast([P, NB, P]),
                                        ALU.max).then_inc(arg_ready, 1)

            def weighed_queries(h, way):
                dve.wait_ge(wb_done, 2 * h + way + 1)
                if h >= 2:
                    dve.wait_ge(out_done, NB * (h - 1))
                last = 0 if way else P - 1
                nc.vector.tensor_copy(h_dec[:, h % 2, way, :], blocks(row_place(h, True))[:, :, last])
                nc.vector.tensor_tensor(h_q[h % 2][:, way, :, :].rearrange("p b n -> p (b n)"), mqk[:, h, :],
                                        row_place(h, True)[:, :], ALU.mult).then_inc(q_ready, 1)

            def weighed_scores(h, way):
                dve.wait_ge(exp_ready, 2 * h + way + 1)
                dve.wait_ge(st_done, h + 1)
                nc.vector.scalar_tensor_tensor(out=h_s[h % 2][:, way, :, :], in0=blocks(ST), scalar=K_SCALE,
                                               in1=h_s[h % 2][:, way, :, :], op0=ALU.mult, op1=ALU.mult
                                               ).then_inc(s_ready, 1)

            def prepare(h, step):
                if step == 1:
                    weighed_keys(h)
                    if h >= 2:
                        head_mean(dve, h - 2)
                elif step == 2:
                    subtract(h, 0)
                    bound(h, 0)
                elif step == 3:
                    weighed_queries(h, 0)
                    if h >= 2:
                        head_inverse(dve, h - 2)
                elif step == 4:
                    weighed_scores(h, 0)
                    subtract(h, 1)
                elif step == 5:
                    bound(h, 1)
                    weighed_queries(h, 1)
                elif step == 6:
                    weighed_scores(h, 1)

            def last_head(step):
                if step == 1:
                    head_mean(dve, MH - 2)
                elif step == 3:
                    head_inverse(dve, MH - 2)
                elif step == 5:
                    split_lo(dve, Count(b + T_BR), 0, WIDTH_A)

            def leave(h, n, chunks):
                for way in range(2):
                    if n < NB // 2:
                        op = nc.vector.tensor_scalar(hm[:, chunks[way], h, :], d_out(h, way, n)[:, 0:MV],
                                                     h_den[:, 1, way:way + 1], None, ALU.mult)
                    else:
                        op = nc.vector.scalar_tensor_tensor(out=hm[:, chunks[way], h, :],
                                                            in0=d_out(h, way, n)[:, 0:MV],
                                                            scalar=h_den[:, 1, way:way + 1],
                                                            in1=hm[:, chunks[way], h, :], op0=ALU.mult,
                                                            op1=ALU.add)
                op.then_inc(hm_left, 1)

            def next_state(h, n, chunks):
                if n == NB - 1:
                    return
                turn = 2 * ((NB - 1) * h + n)
                for way in range(2):
                    dve.wait_ge(dc_done, turn + way + 1)
                    if n == 0:
                        nc.vector.tensor_copy(state[:, way, 1, :], d_state(way)).then_inc(c_ready, 1)
                    else:
                        dve.wait_ge(c_ready, turn + way - 1)
                        nc.vector.scalar_tensor_tensor(
                            out=state[:, way, (n + 1) % 2, :], in0=state[:, way, n % 2, :],
                            scalar=h_dec[:, h % 2, way, chunks[way]:chunks[way] + 1], in1=d_state(way),
                            op0=ALU.mult, op1=ALU.add).then_inc(c_ready, 1)

            subtract(0, 0)
            bound(0, 0)
            weighed_queries(0, 0)
            subtract(0, 1)
            bound(0, 1)
            weighed_scores(0, 0)
            weighed_queries(0, 1)
            weighed_scores(0, 1)
            weighed_keys(0)
            dve.wait_ge(q_ready, 2)
            for h in range(MH):
                for n in range(NB):
                    done = h * NB + n
                    chunks = [chunk_of(way, n) for way in range(2)]
                    dve.wait_ge(out_done, done + 1)
                    for way in range(2):
                        op = nc.vector.tensor_scalar(h_den[:, 0, way:way + 1], d_out(h, way, n)[:, MV:MV + 1], -1.0,
                                                     col[:, chunks[way], EM_COL, 32 * way + h:32 * way + h + 1],
                                                     ALU.mult, ALU.max)
                    op.then_inc(den_bound, 1)
                    dve.wait_ge(den_bound, done + 1)
                    nc.vector.tensor_tensor(h_den[:, 0, :], h_den[:, 0, :], both_dens(h, n), ALU.max
                                            ).then_inc(den_max, 1)
                    dve.wait_ge(den_max, done + 1)
                    nc.vector.reciprocal(h_den[:, 1, :], h_den[:, 0, :]).then_inc(den_inv, 1)
                    dve.wait_ge(den_inv, done + 1)
                    for step in (next_state, leave) if h == MH - 1 else (leave, next_state):
                        step(h, n, chunks)
                    if n == NB // 2 - 1:
                        dve.wait_ge(hm_left, done + 1)
                    if h + 1 < MH:
                        prepare(h + 1, n)
                    else:
                        last_head(n)

        def mlstm_sp(sp):
            sp.wait_ge(cols_turned, 1)
            sp.dma_start(chains[:, :, :, :].rearrange("p w h n -> p (w h n)"),
                         table("chains", CHAIN_ROWS)).then_inc(chains_loaded, 16)
            sp.dma_start(order[:, 0, :], table("later")).then_inc(chains_loaded, 16)
            sp.dma_start(order[:, 1, :], table("earlier")).then_inc(chains_loaded, 16)


        def k_tiles(w, first):
            return w[:, bass.ds(first, P)].rearrange("(k p) n -> p k n", p=P)

        def load_part(sp, c, k, src):
            sp.wait_ge(wlo_ready, c.n(k - RING + 1))
            s = c.slot(k)
            nk = src.shape[1]
            sp.dma_start(w_raw[:, s, 0:nk * P].rearrange("p (k n) -> p k n", k=nk), src).then_inc(raw_loaded[s], 16)

        def branch_sp(sp, b):
            W_A, W_M, W_O = t["w_branch_attn"][0], t["w_branch_mlstm"][0], t["w_out"][0]
            sp.wait_ge(wb_done, 2 * MH)
            sp.wait_ge(arg_ready, 2 * MH)
            sp.wait_ge(exp_ready, 2 * MH)
            for m in range(KD):
                if m == 4:
                    sp.wait_ge(out_done, (MH - 1) * NB)
                    load_part(sp, Count(b + T_BR), 0, k_tiles(W_A, 0))
                    load(sp, Count(b + T_BR), 1, k_tiles(W_M, 0))
                if m >= 4:
                    sp.wait_ge(sig_free[m % 2], (m - 4) // 2 + 1)
                sp.dma_start(sig_in[m % 4][:, :], sig_dram[m]).then_inc(sig_loaded[m % 4], 16)

            def merge_gates(m, k, i):
                for j in range(2):
                    sp.wait_ge(sig_free[j], Count(GATED + k, 2, i).n())
                    sp.dma_start(sig_in[j][:, :], sig_tile(m + KD * (1 + j))).then_inc(sig_loaded[j], 16)

            with sp.Fori(0, KD // 2 - 1) as i:
                c = Count(b + T_BR + 2, 4, i)
                for k in range(2):
                    merge_gates(i * 2 + k, k, i)
                    load_part(sp, c, 2 * k, k_tiles(W_A, i * (2 * P) + (k + 1) * P))
                    load(sp, c, 2 * k + 1, k_tiles(W_M, i * (2 * P) + (k + 1) * P))
            merge_gates(KD - 2, KD - 2, None)
            c = Count(b + T_WO - 2)
            load_part(sp, c, 0, k_tiles(W_A, (KD - 1) * P))
            load(sp, c, 1, k_tiles(W_M, (KD - 1) * P))
            merge_gates(KD - 1, KD - 1, None)
            for m in range(KD):
                load(sp, Count(b + T_WO), m, k_tiles(W_O, m * P))
                if m == 1:
                    sp.wait_ge(block_used, b + T_WO)
                    for k in range(KD):
                        sp.dma_start(resid[:, k, :], resid_dram[k]).then_inc(resid_back, 16)

        def hm_parts(k):
            return (mlo_ready if k % 2 else hmlo_pool, k // 2 + 1)

        def branch_pe(pe, b):
            def attn(c, k, j):
                product(ps[2 * j], [(c.slot(k), kk * P, o_hi[:, kk, :], o_lo[:, kk, :]) for kk in range(AH // 2)],
                        new_block=True).then_inc(br_attn, 1)

            pe.wait_ge(wlo_ready, b + T_BR + 1)
            pe.wait_ge(olo_ready, AH // 2)
            pe.wait_ge(s_ready, 2 * MH)
            for m in range(KD):
                if m == 2:
                    attn(Count(b + T_BR), 0, 0)
                pe.wait_ge(hm_scaled, m // 2 + 1)
                if m == 0:
                    pe.wait_ge(c_ready, 2 * (NB - 1) * MH)
                    pe.wait_ge(hm_left, NB * MH)
                if m >= 2:
                    pe.wait_ge(sig_free[m % 2], m // 2)
                for c in range(NB):
                    mm = nc.tensor.transpose(ps[2 + m % 2][:, c * P:(c + 1) * P],
                                             hm[:, c, m // 2, (m % 2) * P:(m % 2 + 1) * P], ident[:, :])
                mm.then_inc(hm_turned, 1)

            def turn(c, g, last):
                for j in range(2):
                    pe.wait_ge(wlo_ready, c.n(2 * j + 2))
                    pe.wait_ge(sig_free[1], g.n(j - 1))
                    product_as_ready(pe, ps[2 * j + 1], [(c.slot(2 * j + 1), k * P, hm_hi[:, k, :], hm_lo[:, k, :])
                                                         for k in range(KD)], [[hm_parts(k)] for k in range(KD)],
                                     new_block=True).then_inc(br_mlstm, 1)
                    if not (last and j):
                        pe.wait_ge(wlo_ready, c.n(2 * j + 3))
                        pe.wait_ge(sig_free[0], g.n(j))
                        attn(c, 2 * j + 2, 1 - j)

            with pe.Fori(0, KD // 2 - 1) as i:
                turn(Count(b + T_BR, 4, i), Count(GATED, 2, i), False)
            turn(Count(b + T_WO - 4), Count(GATED + KD - 2), True)
            with pe.Fori(0, KD // 4) as i:
                c, ct = Count(b + T_WO, 4, i), Count(N_TILES, 4, i)
                for m in range(4):
                    pe.wait_ge(wlo_ready, c.n(m + 1))
                    pe.wait_ge(sig_free[m % 2], GATED + KD - 1 + m // 2)
                    pe.wait_ge(mix_left, ct.n(m - 3))
                    product_as_ready(pe, ps[m], [(c.slot(m), k * P, mg_hi[:, k, :], mg_lo[:, k, :])
                                                 for k in range(KD)],
                                     [[(mlo_ready, GATED + k + 1)] if m == 0 else [] for k in range(KD)],
                                     new_block=True).then_inc(mix_done, 1)

        def branch_act(act, b):
            act.wait_ge(dc_done, 2 * (NB - 1) * MH)
            act.wait_ge(out_done, MH * NB)
            for m in range(KD):
                act.wait_ge(sig_free[m % 2], m // 2 + 1)
                nc.scalar.activation(hm_hi[:, m, :], tmp[:, m % 2, :], ACT.Copy).then_inc(hmhi_ready, 1)
                if m + 4 < KD:
                    gate(act, m % 4, 2)

            def turn(c, g, last):
                for j in range(2):
                    gate(act, 0, g.n(j - 1))
                    gate(act, 1, g.n(j - 1))
                    split_hi(act, c, 2 * j + 2, 1024 if last and j else WIDTH_A)
                    split_hi(act, c, 2 * j + 3)

            with act.Fori(0, KD // 2 - 1) as i:
                turn(Count(b + T_BR, 4, i), Count(GATED, 2, i), False)
            turn(Count(b + T_WO - 4), Count(GATED + KD - 2), True)
            for m in range(KD):
                act.wait_ge(mix_done, N_TILES + m + 1)
                nc.scalar.activation(mix_y[:, m, :], ps[m % 4][:, :], ACT.Copy).then_inc(mix_left, 1)
                if m == KD - 1:
                    split_hi(act, Count(b + T_END), 0)
                square_act(act, 3, mix_y, [m])
                if m + 2 < KD:
                    split_hi(act, Count(b + T_WO), m + 2)

        def branch_dve(dve, b):
            dve.wait_ge(dc_done, 2 * (NB - 1) * MH)

            def gated(m):
                dve.wait_ge(hm_turned, m + 1)
                dve.wait_ge(sig_made[m % 4], m // 4 + 1)
                if m >= 2:
                    dve.wait_ge(*hm_parts(m - 2))
                nc.vector.scalar_tensor_tensor(out=tmp[:, m % 2, :], in0=ps[2 + m % 2][:, :],
                                               scalar=vecs[:, 64 + m:65 + m], in1=sig_in[m % 4][:, :], op0=ALU.mult,
                                               op1=ALU.mult).then_inc(sig_free[m % 2], 1)

            for m in range(KD):
                gated(m)
                if m == 1:
                    head_mean(dve, MH - 1)
                    head_inverse(dve, MH - 1)
                    dve.wait_ge(hm_scaled, MH - 1)
                    scale_head(dve, nc.vector, MH - 1)
                    split_lo(dve, Count(b + T_BR), 1)
                if m % 2 == 0 and m:
                    hm_subtract(dve, nc.vector, m - 1, mlo_ready)
            hm_subtract(dve, nc.vector, KD - 1, mlo_ready)

            def turn(c, g, n0, m, last):
                for j in range(2):
                    split_lo(dve, c, 2 * j + 2, 1024 if last and j else WIDTH_A)
                    dve.wait_ge(br_attn, n0.n(j + 1))
                    dve.wait_ge(sig_made[0], g.n(j - 1))
                    dve.wait_ge(mlo_ready, g.n(j))
                    dve.wait_ge(hmlo_pool, GATED)
                    nc.vector.tensor_tensor(tmp[:, 0, :], ps[2 * j][:, :], sig_in[0][:, :],
                                            ALU.mult).then_inc(sig_free[0], 1)
                    if not (last and j):
                        split_lo(dve, c, 2 * j + 3)
                    dve.wait_ge(br_mlstm, n0.n(j + 1))
                    dve.wait_ge(sig_made[1], g.n(j - 1))
                    nc.vector.tensor_tensor(tmp[:, 1, :], ps[2 * j + 1][:, :], sig_in[1][:, :],
                                            ALU.mult).then_inc(sig_free[1], 1)
                    dve.wait_ge(sig_free[0], g.n(j + 1))
                    dve.wait_ge(sig_free[1], g.n(j + 1))
                    nc.vector.tensor_tensor(tmp[:, 0, :], tmp[:, 0, :], tmp[:, 1, :], ALU.add).then_inc(br_sum, 1)
                    dve.wait_ge(br_sum, n0.n(j + 1))
                    hi = mg_hi[:, bass.ds(m + j, 1), :].rearrange("p a n -> p (a n)")
                    lo = mg_lo[:, bass.ds(m + j, 1), :].rearrange("p a n -> p (a n)")
                    copy(hi, tmp[:, 0, :]).then_inc(mghi_ready, 1)
                    dve.wait_ge(mghi_ready, n0.n(j + 1))
                    nc.vector.tensor_tensor(lo, tmp[:, 0, :], hi.bitcast(F32), ALU.subtract).then_inc(mlo_ready, 1)

            with dve.Fori(0, KD // 2 - 1) as i:
                turn(Count(b + T_BR, 4, i), Count(GATED, 2, i), Count(0, 2, i), i * 2, False)
            turn(Count(b + T_WO - 4), Count(GATED + KD - 2), Count(KD - 2), KD - 2, True)
            for m in range(1, KD):
                split_lo(dve, Count(b + T_WO), m)

        def hm_subtract(eng, engine, m, done):
            eng.wait_ge(hmhi_ready, m + 1)
            engine.tensor_tensor(hm_lo[:, m, :], tmp[:, m % 2, :], hm_hi[:, m, :].bitcast(F32),
                                 ALU.subtract).then_inc(done, 1)

        def branch_pool(pool):
            for h in range(MH - 2):
                scale_head(pool, nc.gpsimd, h)
            for k in range(AH // 2):
                pool.wait_ge(ohi_ready, k + 1)
                nc.gpsimd.tensor_tensor(o_lo[:, k, :], att_q[:, k, :], o_hi[:, k, :].bitcast(F32),
                                        ALU.subtract).then_inc(olo_ready, 1)
            scale_head(pool, nc.gpsimd, MH - 2)
            pool.wait_ge(out_done, MH * NB)
            for m in range(0, KD, 2):
                hm_subtract(pool, nc.gpsimd, m, hmlo_pool)

        p_loaded, p_turned, phi_ready, plo_ready, wp_loaded, wphi_ready, wplo_ready = (sem(x) for x in (
            "p_loaded", "p_turned", "phi_ready", "plo_ready", "wp_loaded", "wphi_ready", "wplo_ready"))
        PAIRS = 2 * GROUPS * GROUP

        def ple_sp(sp, b):
            W_G, W_P = t["w_ple_gate"][0], t["w_ple_proj"][0]
            load(sp, Count(b), 0, k_tiles(W_G, 0))
            sp.wait_ge(sum_done, 6)
            sp.dma_start(p_in[:, :, :], t["p"][0, 0].rearrange("(n q) c -> q n c", q=P)).then_inc(p_loaded, 16)
            sp.dma_start(wp_raw[:, :, :], W_P.rearrange("(k p) n -> p k n", p=P)).then_inc(wp_loaded, 16)
            load(sp, Count(b), 1, k_tiles(W_G, P))
            with sp.Fori(0, KD // 2 - 1) as i:
                for k in range(2):
                    load(sp, Count(b + 2, 2, i), k, k_tiles(W_G, i * (2 * P) + (k + 2) * P))

        def p_pe(pe):
            pe.wait_ge(p_loaded, 16)
            for k in range(PLE // P):
                for n in range(NB):
                    mm = nc.tensor.transpose(ps[k][:, n * P:(n + 1) * P], p_in[:, n, k * P:(k + 1) * P], ident[:, :])
                mm.then_inc(p_turned, 1)

        def p_act(act):
            for k in range(PLE // P):
                act.wait_ge(p_turned, k + 1)
                nc.scalar.activation(p_hi[:, k, :], ps[k][:, :], ACT.Copy).then_inc(phi_ready, 1)
            act.wait_ge(wp_loaded, 16)
            for k in range(PLE // P):
                nc.scalar.activation(wp_hi[:, k, :], wp_raw[:, k, :], ACT.Copy).then_inc(wphi_ready, 1)

        def p_dve(dve):
            for k in range(PLE // P):
                dve.wait_ge(phi_ready, k + 1)
                nc.vector.tensor_tensor(p_lo[:, k, :], ps[k][:, :], p_hi[:, k, :].bitcast(F32),
                                        ALU.subtract).then_inc(plo_ready, 1)
            for k in range(PLE // P):
                dve.wait_ge(wphi_ready, k + 1)
                nc.vector.tensor_tensor(wp_lo[:, k, :], wp_raw[:, k, :], wp_hi[:, k, :].bitcast(F32),
                                        ALU.subtract).then_inc(wplo_ready, 1)

        def projection(m, acc):
            for k in range(PLE // P):
                hi, lo = (w[:, k, m * P:(m + 1) * P] for w in (wp_hi, wp_lo))
                for h in range(2):
                    cols = slice(h * HALF, (h + 1) * HALF)
                    nc.tensor.matmul(acc[:, cols], hi, p_hi[:, k, cols], start=(k == 0), stop=False)
                    nc.tensor.matmul(acc[:, cols], hi, p_lo[:, k, cols], start=False, stop=False)
                    mm = nc.tensor.matmul(acc[:, cols], lo, p_hi[:, k, cols], start=False, stop=(k == PLE // P - 1))
            return mm

        def ple_pe(pe, b):
            pe.wait_ge(plo_ready, PLE // P)
            pe.wait_ge(wplo_ready, PLE // P)
            for m in range(KD):
                j = m % 2
                pe.wait_ge(prod_done, PAIRS + m - 1)
                projection(m, ps[2 * j + 1]).then_inc(gateup_done, 1)
                pe.wait_ge(wlo_ready, b + m + 1)
                pe.wait_ge(silu_done, PAIRS + m - 1)
                product_as_ready(pe, ps[2 * j], [((b + m) % RING, k * P, u_hi[:, k, :], u_lo[:, k, :])
                                                 for k in range(KD)],
                                 [[(ulo_ready, 3 * KD + k + 1)] if m == 0 else [] for k in range(KD)],
                                 new_block=True).then_inc(gateup_done, 1)

        def ple_act(act, b):
            def turn(c, g, last):
                for j in range(2):
                    if not (last and j):
                        split_hi(act, c, j + 1)
                    act.wait_ge(gateup_done, 2 * g.n(j) + 2)
                    act.wait_ge(prod_done, g.n(j - 1))
                    nc.scalar.activation(tmp[:, j, :], ps[2 * j][:, :], ACT.Sigmoid).then_inc(silu_done, 1)
                    if last:
                        square_act(act, 7, yacc, (range(6, 7) if j else range(6)))

            with act.Fori(0, KD // 2 - 1) as i:
                turn(Count(b, 2, i), Count(PAIRS, 2, i), False)
            turn(Count(b + KD - 2), Count(PAIRS + KD - 2), True)
            square_act(act, 7, yacc, [KD - 1])

        def ple_dve(dve, b):
            def turn(c, g, m, last):
                for j in range(2):
                    if not (last and j):
                        split_lo(dve, c, j + 1)
                    dve.wait_ge(silu_done, g.n(j + 1))
                    nc.vector.tensor_tensor(yacc[:, bass.ds(m + j, 1), :].rearrange("p a n -> p (a n)"),
                                            tmp[:, j, :], ps[2 * j + 1][:, :], ALU.mult).then_inc(prod_done, 1)

            with dve.Fori(0, KD // 2 - 1) as i:
                turn(Count(b, 2, i), Count(PAIRS, 2, i), i * 2, False)
            turn(Count(b + KD - 2), Count(PAIRS + KD - 2), KD - 2, True)

        bias_zero = sem("bias_zero")
        B_MIX = BLOCKS_FFN
        B_FFN2 = B_MIX + T_END
        B_PLE = B_FFN2 + BLOCKS_FFN

        block = ctx.enter_context(nc.Block())

        @block.gpsimd
        def _(pool):
            nc.gpsimd.memset(ident[:, :], 0.0).then_inc(ident_zero, 1)
            pool.wait_ge(ident_zero, 1)
            nc.gpsimd.affine_select(out=ident[:, :], in_=ident[:, :], compare_op=ALU.not_equal, fill=1.0, base=0,
                                    pattern=[[-1, P]], channel_multiplier=1).then_inc(consts_ready, 1)
            nc.gpsimd.memset(band[:, :], 0.0).then_inc(ident_zero, 1)
            pool.wait_ge(ident_zero, 2)
            nc.gpsimd.memset(band[:, NB - 1:NB], 1.0).then_inc(consts_ready, 1)
            nc.gpsimd.memset(eps[:, :], EPS).then_inc(consts_ready, 1)
            nc.gpsimd.memset(gate_bias[:, :], 0.0).then_inc(bias_zero, 1)
            nc.gpsimd.memset(q_st[:, :, :, :], 0.0).then_inc(qst_zero, 1)
            pool.wait_ge(x_kept, KD)
            for m in range(KD):
                nc.gpsimd.memset(yacc[:, m, :], 0.0).then_inc(y_added, 1)
            pair_pool(pool, 1)
            post_pool(pool, 1, yacc)
            pool.wait_ge(rope_done, AH // 2 + 1)
            nc.gpsimd.memset(m_v[:, :, :, MV:MV + 1], 1.0).then_inc(ones_v, 1)
            pool.wait_ge(vt_done, 1)
            for side in (slice(0, TAPS // 2), slice(TAPS // 2 + S, S + TAPS - 1)):
                op = nc.gpsimd.memset(zpad[:, :, side], 0.0)
            op.then_inc(pad_zero, 1)
            branch_pool(pool)
            pair_pool(pool, 3)
            pool.wait_ge(mix_left, N_TILES + KD)
            pool.wait_ge(resid_back, 16 * KD)
            post_pool(pool, 3, mix_y)
            for m in range(KD):
                nc.gpsimd.memset(yacc[:, m, :], 0.0).then_inc(y_added, 1)
            pair_pool(pool, 5)
            post_pool(pool, 5, yacc)
            pair_pool(pool, 7)
            post_pool(pool, 7, yacc)

        @block.sync
        def _(sp):
            for j in range(KD):
                sp.dma_start(x_in[:, j, :], t["x"][0, j * P:(j + 1) * P, :]).then_inc(x_loaded[j], 16)
            rows = 0
            for src in [t[name] for name in NORMS] + [t["mlstm_norm"], t["conv_b"], t["conv_w"]]:
                src = src.rearrange("a (k p) -> (a k) p", p=P) if len(src.shape) == 2 else \
                    src.rearrange("a c (k p) -> (a c k) p", p=P)
                sp.dma_start(vec_rows[rows:rows + src.shape[0], :], src).then_inc(vecs_loaded, 16)
                rows += src.shape[0]
            sp.dma_start(sinks[:, :], t["attn_sink"].to_broadcast([P, AH])).then_inc(small_loaded, 16)
            sp.wait_ge(bias_zero, 1)
            by_head = t["b_gates"].rearrange("a (w g h) -> w (a h) g", w=2, g=2)
            for way in range(2):
                sp.dma_start(gate_bias[32 * way:32 * way + MH, :], by_head[way],
                             allow_slow_non_contiguous=True).then_inc(small_loaded, 16)
            ffn_sp(sp, 0, 0, "ffn1_w1", "ffn1_w2")
            mix_sp(sp, B_MIX)
            branch_sp(sp, B_MIX)
            ffn_sp(sp, 1, B_FFN2, "ffn2_w1", "ffn2_w2")
            ple_sp(sp, B_PLE)
            for j in range(KD):
                sp.wait_ge(out_copied[j % 2], j // 2 + 1)
                sp.dma_start(out[0, j * P:(j + 1) * P, :], x_out[:, j, :]).then_inc(stored, 16)
            sp.wait_ge(stored, 16 * KD)

        @block.scalar
        def _(act):
            tokens_act(act)
            root_act(act, 0)
            for k in range(0, KD, 2):
                if k >= 4:
                    split_hi(act, Count(0), k // 2 - 2)
                act.wait_ge(x_turned, k + 1)
                if k:
                    act.wait_ge(x_kept, k)
                nc.scalar.copy(resid[:, k, :], ps[k % 3][:, :]).then_inc(x_kept, 1)
            pre_act(act, 0)
            ffn_act(act, 0, 0)

            act.wait_ge(raw_q[0], 16)
            split_hi(act, Count(B_MIX), 0)
            square_act(act, 1, yacc)
            act.wait_ge(raw_q[1], 16)
            split_hi(act, Count(B_MIX), 1)
            root_act(act, 1)
            square_act(act, 2, resid)
            root_act(act, 2)
            pre_act(act, 2)
            mix_act(act, B_MIX)
            mlstm_act(act, B_MIX)
            branch_act(act, B_MIX)

            split_hi(act, Count(B_FFN2), 1)
            root_act(act, 3)
            square_act(act, 4, resid)
            root_act(act, 4)
            pre_act(act, 4)
            ffn_act(act, 1, B_FFN2)

            split_hi(act, Count(B_PLE), 0)
            square_act(act, 5, yacc)
            root_act(act, 5)
            p_act(act)
            square_act(act, 6, resid)
            root_act(act, 6)
            pre_act(act, 6)
            ple_act(act, B_PLE)
            root_act(act, 7)
            for j in range(0, NB, 2):
                act.wait_ge(out_turned, j + 1)
                nc.scalar.copy(x_out[:, j, :], OUT[j % 3][:, :]).then_inc(out_copied[0], 1)

        @block.vector
        def _(dve):
            for k in range(1, KD, 2):
                if k == 3:
                    invert_dve(dve, 0)
                if k == 7:
                    split_lo(dve, Count(0), 0)
                dve.wait_ge(x_turned, k + 1)
                dve.wait_ge(x_kept, k)
                nc.vector.tensor_copy(resid[:, k, :], ps[k % 3][:, :]).then_inc(x_kept, 1)
            dve.wait_ge(vecs_turned, 1)
            nc.vector.tensor_copy(vecs[:, :], ps[2][:, 0:VEC_ROWS]).then_inc(vecs_ready, 1)
            dve.wait_ge(vecs_ready, 1)
            for n in (1, 5):
                nc.vector.tensor_scalar(gains[:, n, :], gains[:, n, :], 0.5, None, ALU.mult).then_inc(gains_halved, 1)
            split_lo(dve, Count(0), 1)
            pre_dve(dve, 0)
            ffn_dve(dve, 0, 0)

            split_lo(dve, Count(B_MIX), 0)
            split_lo(dve, Count(B_MIX), 1)
            dve.wait_ge(gains_halved, 2)
            post_dve(dve, 1, yacc)
            pre_dve(dve, 2)
            mix_dve(dve, B_MIX)
            mlstm_dve(dve, B_MIX)
            branch_dve(dve, B_MIX)

            split_lo(dve, Count(B_FFN2), 0)
            split_lo(dve, Count(B_FFN2), 1)
            post_dve(dve, 3, mix_y)
            pre_dve(dve, 4)
            ffn_dve(dve, 1, B_FFN2)

            split_lo(dve, Count(B_PLE), 0)
            post_dve(dve, 5, yacc)
            p_dve(dve)
            pre_dve(dve, 6)
            ple_dve(dve, B_PLE)
            post_dve(dve, 7, yacc)
            for j in range(1, NB, 2):
                dve.wait_ge(out_turned, j + 1)
                nc.vector.tensor_copy(x_out[:, j, :], OUT[j % 3][:, :]).then_inc(out_copied[1], 1)

        @block.tensor
        def _(pe):
            pe.wait_ge(consts_ready, 3)
            for j in range(NB):
                pe.wait_ge(x_loaded[j], 16)
            for k in range(KD):
                if k >= 3:
                    pe.wait_ge(x_kept, k - 2)
                if k == 1:
                    norm0_pe(pe)
                if k == 4:
                    spread_pe(pe, 0)
                for j in range(KD):
                    mm = nc.tensor.transpose(ps[k % 3][:, j * P:(j + 1) * P], x_in[:, j, k * P:(k + 1) * P],
                                             ident[:, :])
                mm.then_inc(x_turned, 1)
            pe.wait_ge(vecs_loaded, 16 * 11)
            pe.wait_ge(x_kept, 6)
            nc.tensor.transpose(ps[2][:, 0:VEC_ROWS], vec_rows[:, :], ident[0:VEC_ROWS, 0:VEC_ROWS]
                                ).then_inc(vecs_turned, 1)
            pe.wait_ge(x_kept, KD)
            ffn_pe(pe, 0, 0, 0)
            pe.wait_ge(y_added, KD * (GROUPS + 1) - 1)
            norm_pe(pe, 1, new_block=True)
            norm_pe(pe, 2)
            mix_pe(pe, B_MIX, 1)
            mlstm_pe(pe)
            branch_pe(pe, B_MIX)
            pe.wait_ge(mix_left, N_TILES + KD - 1)
            norm_pe(pe, 3, new_block=True)
            norm_pe(pe, 4)
            ffn_pe(pe, 1, B_FFN2, 2)
            pe.wait_ge(y_added, 2 * KD * (GROUPS + 1) - 1)
            norm_pe(pe, 5)
            p_pe(pe)
            norm_pe(pe, 6)
            ple_pe(pe, B_PLE)
            pe.wait_ge(silu_done, PAIRS + KD - 1)
            norm_pe(pe, 7)

            def turn_out(j, k):
                return nc.tensor.transpose(OUT[j % 3][:, k * P:(k + 1) * P], resid[:, k, j * P:(j + 1) * P],
                                           ident[:, :])

            for k in range(KD):
                resid_wait(pe, 3, k)
                for j in range(3):
                    mm = turn_out(j, k)
                    if k == KD - 1:
                        mm.then_inc(out_turned, 1)
            for j in range(3, NB):
                pe.wait_ge(out_copied[(j - 3) % 2], (j - 3) // 2 + 1)
                for k in range(KD):
                    mm = turn_out(j, k)
                mm.then_inc(out_turned, 1)


def tables():
    import numpy as np

    f = np.float32
    p, c = np.arange(P)[:, None], np.arange(P)[None, :]
    made = {"ident": p == c}
    d = np.arange(P) % AD
    partner = np.where(d < ROPE // 2, np.arange(P) + ROPE // 2, np.arange(P) - ROPE // 2)
    partner = np.where(d < ROPE, partner, np.arange(P))
    made["perm"] = p == partner[None, :]
    key = np.arange(WINDOW)[None, :] - P
    made["window"] = np.where(np.abs(key - p) <= P, 0, -BLOCKED)
    made["later"] = np.where(p <= c, 0, BLOCKED)
    made["earlier"] = np.where(p >= c, 0, BLOCKED)
    chains = np.zeros((P, 2, MH, P))
    for way in range(2):
        for h in range(MH):
            chains[32 * way + h, way, h] = 1
    made["chains"] = chains.reshape(P, -1)
    inv = f(THETA) ** (-np.arange(0, ROPE, 2, dtype=f) / f(ROPE))
    angle = (np.arange(S, dtype=f)[:, None] * inv[None, :]).astype(f)
    cos, sin = np.ones((P, S)), np.zeros((P, S))
    for n in range(P):
        if n % AD < ROPE:
            cos[n] = np.cos(angle[:, n % AD % (ROPE // 2)])
            sin[n] = np.sin(angle[:, n % AD % (ROPE // 2)]) * (-1 if n % AD < ROPE // 2 else 1)
    made["cos"], made["sin"] = cos, sin
    token = np.arange(S)[None, :] % P
    made["inside"] = np.where(p < 32, token != 0, token != P - 1)
    return {"tables": np.concatenate([np.broadcast_to(made[n], (P, w)).astype(f) for n, (_, w) in TABLE.items()], 1)}


_INS = ['x', 'p', 'ffn1_norm_pre', 'ffn1_w1', 'ffn1_w2', 'ffn1_norm_post', 'mix_norm_pre', 'w_in', 'b_gates',
        'conv_w', 'conv_b', 'attn_sink', 'mlstm_norm', 'w_branch_attn', 'w_branch_mlstm', 'w_out', 'mix_norm_post',
        'ffn2_norm_pre', 'ffn2_w1', 'ffn2_w2', 'ffn2_norm_post', 'ple_norm_pre', 'w_ple_gate', 'w_ple_proj',
        'ple_norm_post']


def kernel(**inputs):
    import numpy as np
    import concourse.bacc as bacc
    from concourse.bass_utils import run_bass_kernel_spmd

    nc = bacc.Bacc("TRN2", target_bir_lowering=False, num_devices=1)
    arrays, args = {}, {}
    for name in _INS:
        arrays[name] = np.ascontiguousarray(inputs[name])
        args[name] = nc.dram_tensor(name, arrays[name].shape, F32, kind="ExternalInput").ap()
    for name, array in tables().items():
        arrays[name] = array
        args[name] = nc.dram_tensor(name, array.shape, F32, kind="ExternalInput").ap()
    out = nc.dram_tensor("out", (1, S, D), F32, kind="ExternalOutput").ap()
    build(nc, args, out)
    r = run_bass_kernel_spmd(nc, [arrays], core_ids=[0])
    return r.results[0]["out"]
```
